# Optimizing a Trainium2 kernel written in Bass

```python
import jax, jax.numpy as jnp
from jax import lax
import numpy as np

D_MODEL = 1024
BATCH = 1
SEQ = 256
DEPTH = 2
DEC_BATCH = 8
DEC_SEQ = 8
PAST_LEN = 1024
PAGE_SIZE = 128

N_META = 16
EPS = 1e-6
POOL_WINDOWS = (2, 4, 8, 16)
N_POOL_GROUPS = len(POOL_WINDOWS)
POOL_GROUP = D_MODEL // N_POOL_GROUPS
POOL_BUF = max(POOL_WINDOWS) - 1
N_HEADS = 16
Q_LORA = 384
KV_LORA = 256
QK_NOPE = 64
QK_ROPE = 32
V_HEAD = 64
ROPE_BASE = 10000.0
Q_BLOCK = 128
ATTN_SCALE = (QK_NOPE + QK_ROPE) ** -0.5
D_FF = 2816
N_EXPERTS = 8
TOP_K = 2
N_POOL_LAYERS = (DEPTH + 1) // 2
N_ATTN_LAYERS = DEPTH // 2

kernel_name = 'hybrid_pool_mla_moe_step'

def rmsnorm(x, g):
    xf = x.astype(jnp.float32)
    y = xf * lax.rsqrt(jnp.mean(xf * xf, axis=-1, keepdims=True) + EPS)
    return (y * g.astype(jnp.float32)).astype(x.dtype)

def rope(x, pos):
    half = QK_ROPE // 2
    freqs = 1.0 / (ROPE_BASE ** (jnp.arange(half, dtype=jnp.float32) * (2.0 / QK_ROPE)))
    ang = pos.astype(jnp.float32)[:, None] * freqs[None, :]
    shape = (ang.shape[0],) + (1,) * (x.ndim - 3) + (half,)
    cos = jnp.cos(ang).reshape(shape)
    sin = jnp.sin(ang).reshape(shape)
    xf = x.astype(jnp.float32)
    x1, x2 = xf[..., :half], xf[..., half:]
    return jnp.concatenate([x1 * cos - x2 * sin, x2 * cos + x1 * sin], axis=-1).astype(x.dtype)

def multiscale_pool(h_ext, n_out, w_pool, scale):
    B, L, D = h_ext.shape
    cs = jnp.cumsum(h_ext.astype(jnp.float32), axis=1)
    cs = jnp.concatenate([jnp.zeros((B, 1, D), jnp.float32), cs], axis=1)
    hi = jnp.arange(L - n_out + 1, L + 1)
    h_out = h_ext[:, L - n_out:].astype(jnp.float32)
    groups = []
    for g, w in enumerate(POOL_WINDOWS):
        c0, c1 = g * POOL_GROUP, (g + 1) * POOL_GROUP
        csg = cs[:, :, c0:c1]
        lo = jnp.maximum(hi - w, 0)
        cnt = (hi - lo).astype(jnp.float32)[None, :, None]
        mean = (csg[:, hi] - csg[:, lo]) / cnt
        groups.append(mean - h_out[:, :, c0:c1])
    d = jnp.stack(groups, axis=2).astype(h_ext.dtype)
    y = jnp.einsum('btgc,gcd->btgd', d, w_pool).reshape(B, n_out, D)
    return y * scale

def mla_project(h, pos, w_in, g_q, g_kv, w_uq):
    B, T, _ = h.shape
    proj = h @ w_in
    cq, ckv, kpe = jnp.split(proj, [Q_LORA, Q_LORA + KV_LORA], axis=-1)
    q = (rmsnorm(cq, g_q) @ w_uq).reshape(B, T, N_HEADS, QK_NOPE + QK_ROPE)
    q_nope = q[..., :QK_NOPE]
    q_pe = rope(q[..., QK_NOPE:], pos)
    return q_nope, q_pe, rmsnorm(ckv, g_kv), rope(kpe, pos)

def mla_attend(q_nope, q_pe, q_pos, k_pos, ckv, kpe, w_uk, w_uv):
    q_lat = jnp.einsum('bqhn,chn->bqhc', q_nope, w_uk)
    s = jnp.einsum('bqhc,btc->bhqt', q_lat, ckv) + jnp.einsum('bqhr,btr->bhqt', q_pe, kpe)
    s = s.astype(jnp.float32) * ATTN_SCALE
    mask = k_pos[None, :] <= q_pos[:, None]
    s = jnp.where(mask[None, None], s, -1e30)
    p = jax.nn.softmax(s, axis=-1).astype(ckv.dtype)
    o_lat = jnp.einsum('bhqt,btc->bqhc', p, ckv)
    return jnp.einsum('bqhc,chv->bqhv', o_lat, w_uv)

def mla_attention(q_nope, q_pe, q_pos, ckv, kpe, w_uk, w_uv, w_o):
    B, Tq = q_nope.shape[:2]
    blk = min(Q_BLOCK, Tq)
    nblk = -(-Tq // blk)
    pad = nblk * blk - Tq
    padq = lambda a: jnp.pad(a, ((0, 0), (0, pad)) + ((0, 0),) * (a.ndim - 2))
    qn = padq(q_nope).reshape(B, nblk, blk, N_HEADS, QK_NOPE).swapaxes(0, 1)
    qp = padq(q_pe).reshape(B, nblk, blk, N_HEADS, QK_ROPE).swapaxes(0, 1)
    qpos = jnp.pad(q_pos, (0, pad), mode='edge').reshape(nblk, blk)
    k_pos = jnp.arange(ckv.shape[1], dtype=jnp.int32)

    def one_block(args):
        qn_b, qp_b, qpos_b = args
        return mla_attend(qn_b, qp_b, qpos_b, k_pos, ckv, kpe, w_uk, w_uv)

    o = lax.map(one_block, (qn, qp, qpos))
    o = o.swapaxes(0, 1).reshape(B, nblk * blk, N_HEADS * V_HEAD)[:, :Tq]
    return o @ w_o

def swiglu(h, w_gate, w_up, w_down):
    return (jax.nn.silu(h @ w_gate) * (h @ w_up)) @ w_down

def moe_swiglu(h, w_router, b_router, w_gate, w_up, w_down):
    shp = h.shape
    t = h.reshape(-1, shp[-1])
    logits = (t @ w_router).astype(jnp.float32)
    _, top_idx = lax.top_k(logits + b_router.astype(jnp.float32), TOP_K)
    top_w = jax.nn.softmax(jnp.take_along_axis(logits, top_idx, axis=-1), axis=-1)
    gates = jnp.sum(jax.nn.one_hot(top_idx, N_EXPERTS, dtype=jnp.float32) * top_w[..., None], axis=1).astype(h.dtype)
    out = jnp.zeros_like(t)
    for e in range(N_EXPERTS):
        out = out + gates[:, e:e + 1] * swiglu(t, w_gate[e], w_up[e], w_down[e])
    return out.reshape(shp)

def setup_inputs(seed: int = 0) -> dict:
    key = jax.random.key(seed)
    ks = jax.random.split(key, 27)
    f32 = jnp.float32
    n_pages = PAST_LEN // PAGE_SIZE
    n_used = DEC_BATCH * n_pages
    n_phys = n_used + n_used // 4 + 1

    def w(k, shape, fan_in):
        return jax.random.normal(k, shape, f32) * (fan_in ** -0.5)

    def gain(k, shape):
        return 1.0 + 0.02 * jax.random.normal(k, shape, f32)

    return {
        'x_prompt': jax.random.normal(ks[0], (BATCH, SEQ, D_MODEL), f32),
        'x_sample': jax.random.normal(ks[1], (DEC_BATCH, DEC_SEQ, D_MODEL), f32),
        'cache_ckv': jax.random.normal(ks[2], (N_ATTN_LAYERS, n_phys, PAGE_SIZE, KV_LORA), f32),
        'cache_kpe': jax.random.normal(ks[3], (N_ATTN_LAYERS, n_phys, PAGE_SIZE, QK_ROPE), f32),
        'state_pool': jax.random.normal(ks[4], (N_POOL_LAYERS, DEC_BATCH, POOL_BUF, D_MODEL), f32),
        'page_table': jax.random.permutation(ks[5], n_phys)[:n_used].reshape(DEC_BATCH, n_pages).astype(jnp.int32),
        'meta_tokens': jax.random.normal(ks[6], (N_META, D_MODEL), f32),
        'g_mix': gain(ks[7], (DEPTH, D_MODEL)),
        'g_ffn': gain(ks[8], (DEPTH, D_MODEL)),
        'g_final': gain(ks[9], (D_MODEL,)),
        'pool_w': w(ks[10], (N_POOL_LAYERS, N_POOL_GROUPS, POOL_GROUP, POOL_GROUP), POOL_GROUP),
        'pool_scale': gain(ks[11], (N_POOL_LAYERS, D_MODEL)),
        'mla_w_in': w(ks[12], (N_ATTN_LAYERS, D_MODEL, Q_LORA + KV_LORA + QK_ROPE), D_MODEL),
        'mla_g_q': gain(ks[13], (N_ATTN_LAYERS, Q_LORA)),
        'mla_g_kv': gain(ks[14], (N_ATTN_LAYERS, KV_LORA)),
        'mla_w_uq': w(ks[15], (N_ATTN_LAYERS, Q_LORA, N_HEADS * (QK_NOPE + QK_ROPE)), Q_LORA),
        'mla_w_uk': w(ks[16], (N_ATTN_LAYERS, KV_LORA, N_HEADS, QK_NOPE), KV_LORA),
        'mla_w_uv': w(ks[17], (N_ATTN_LAYERS, KV_LORA, N_HEADS, V_HEAD), KV_LORA),
        'mla_w_o': w(ks[18], (N_ATTN_LAYERS, N_HEADS * V_HEAD, D_MODEL), N_HEADS * V_HEAD),
        'ffn_w_gate': w(ks[19], (N_POOL_LAYERS, D_MODEL, D_FF), D_MODEL),
        'ffn_w_up': w(ks[20], (N_POOL_LAYERS, D_MODEL, D_FF), D_MODEL),
        'ffn_w_down': w(ks[21], (N_POOL_LAYERS, D_FF, D_MODEL), D_FF),
        'moe_w_router': w(ks[22], (N_ATTN_LAYERS, D_MODEL, N_EXPERTS), D_MODEL),
        'moe_b_router': 0.01 * jax.random.normal(ks[23], (N_ATTN_LAYERS, N_EXPERTS), f32),
        'moe_w_gate': w(ks[24], (N_ATTN_LAYERS, N_EXPERTS, D_MODEL, D_FF), D_MODEL),
        'moe_w_up': w(ks[25], (N_ATTN_LAYERS, N_EXPERTS, D_MODEL, D_FF), D_MODEL),
        'moe_w_down': w(ks[26], (N_ATTN_LAYERS, N_EXPERTS, D_FF, D_MODEL), D_FF),
    }

def reference(x_prompt, x_sample, cache_ckv, cache_kpe, state_pool, page_table, meta_tokens,
              g_mix, g_ffn, g_final, pool_w, pool_scale,
              mla_w_in, mla_g_q, mla_g_kv, mla_w_uq, mla_w_uk, mla_w_uv, mla_w_o,
              ffn_w_gate, ffn_w_up, ffn_w_down,
              moe_w_router, moe_b_router, moe_w_gate, moe_w_up, moe_w_down):
    B = x_prompt.shape[0]
    DB, S, D = x_sample.shape
    meta = jnp.broadcast_to(meta_tokens.astype(x_prompt.dtype)[None], (B, N_META, D))
    xp = jnp.concatenate([meta, x_prompt], axis=1)
    T = xp.shape[1]
    xs = x_sample
    pos_p = jnp.arange(T, dtype=jnp.int32)
    pos_s = PAST_LEN + jnp.arange(S, dtype=jnp.int32)

    ckv_p_rows, kpe_p_rows, pool_p_rows = [], [], []
    ckv_s_rows, kpe_s_rows, pool_s_rows = [], [], []
    for i in range(DEPTH):
        j = i // 2
        hp = rmsnorm(xp, g_mix[i])
        hs = rmsnorm(xs, g_mix[i])
        if i % 2 == 0:
            hs_ext = jnp.concatenate([state_pool[j].astype(hs.dtype), hs], axis=1)
            mp = multiscale_pool(hp, T, pool_w[j], pool_scale[j])
            ms = multiscale_pool(hs_ext, S, pool_w[j], pool_scale[j])
            pool_p_rows.append(hp[:, T - POOL_BUF:])
            pool_s_rows.append(hs_ext[:, hs_ext.shape[1] - POOL_BUF:])
        else:
            qn_p, qp_p, ckv_p, kpe_p = mla_project(hp, pos_p, mla_w_in[j], mla_g_q[j], mla_g_kv[j], mla_w_uq[j])
            mp = mla_attention(qn_p, qp_p, pos_p, ckv_p, kpe_p, mla_w_uk[j], mla_w_uv[j], mla_w_o[j])
            qn_s, qp_s, ckv_s, kpe_s = mla_project(hs, pos_s, mla_w_in[j], mla_g_q[j], mla_g_kv[j], mla_w_uq[j])
            past_ckv = cache_ckv[j][page_table].reshape(DB, -1, KV_LORA).astype(ckv_s.dtype)
            past_kpe = cache_kpe[j][page_table].reshape(DB, -1, QK_ROPE).astype(kpe_s.dtype)
            ckv_all = jnp.concatenate([past_ckv, ckv_s], axis=1)
            kpe_all = jnp.concatenate([past_kpe, kpe_s], axis=1)
            ms = mla_attention(qn_s, qp_s, pos_s, ckv_all, kpe_all, mla_w_uk[j], mla_w_uv[j], mla_w_o[j])
            ckv_p_rows.append(ckv_p)
            kpe_p_rows.append(kpe_p)
            ckv_s_rows.append(ckv_s)
            kpe_s_rows.append(kpe_s)
        xp = xp + mp
        xs = xs + ms
        hp = rmsnorm(xp, g_ffn[i])
        hs = rmsnorm(xs, g_ffn[i])
        if i % 2 == 0:
            xp = xp + swiglu(hp, ffn_w_gate[j], ffn_w_up[j], ffn_w_down[j])
            xs = xs + swiglu(hs, ffn_w_gate[j], ffn_w_up[j], ffn_w_down[j])
        else:
            xp = xp + moe_swiglu(hp, moe_w_router[j], moe_b_router[j], moe_w_gate[j], moe_w_up[j], moe_w_down[j])
            xs = xs + moe_swiglu(hs, moe_w_router[j], moe_b_router[j], moe_w_gate[j], moe_w_up[j], moe_w_down[j])

    y_prompt = rmsnorm(xp, g_final)[:, N_META:]
    y_sample = rmsnorm(xs, g_final)
    ckv_prompt = jnp.stack(ckv_p_rows)
    kpe_prompt = jnp.stack(kpe_p_rows)
    pool_prompt = jnp.stack(pool_p_rows)
    ckv_sample = jnp.stack(ckv_s_rows)
    kpe_sample = jnp.stack(kpe_s_rows)
    pool_sample = jnp.stack(pool_s_rows)
    return (y_prompt, y_sample, ckv_prompt, kpe_prompt, pool_prompt, ckv_sample, kpe_sample, pool_sample)


_drawn_inputs = setup_inputs


def setup_inputs(seed=0):
    import zlib

    import numpy as np

    out = dict(_drawn_inputs(seed))
    spreads = {}
    factors = {'g_final': 8.11, 'mla_g_q': 7.545, 'mla_g_kv': 2.923, 'moe_b_router': 5.598}
    for name, (base, spread) in spreads.items():
        noise = np.random.default_rng([zlib.crc32(name.encode()), seed]).standard_normal(out[name].shape)
        drawn = base * np.exp(spread * noise) if base else spread * noise
        out[name] = __import__('jax').numpy.asarray(drawn.astype(out[name].dtype))
    for name, factor in factors.items():
        out[name] = (out[name] * factor).astype(out[name].dtype)
    return out
```

```python
from contextlib import ExitStack

import numpy as np

import concourse.bass as bass
from concourse import mybir

F32 = mybir.dt.float32
F32R = mybir.dt.float32r
BF16 = mybir.dt.bfloat16
I32 = mybir.dt.int32
ALU = mybir.AluOpType
ACT = mybir.ActivationFunctionType
AX = mybir.AxisListType

P = 128
D = 1024
KD = D // P
SEQ, META, NB, NS = 256, 16, 8, 8
SMP = NB * NS
TP = SEQ + META
T = SMP + TP
NT = 3
TT = T // NT
WINDOWS = (2, 4, 8, 16)
BUF = 15
EPS = 1e-6
H = 16
QL, KL, NOPE, ROPE, VH = 384, 256, 64, 32, 64
HALF = ROPE // 2
QH = NOPE + ROPE
KV = KL + ROPE
PROJ = QL + KL + ROPE
PAST, PAGE = 1024, 128
NPG = PAST // PAGE
SCALE = float(QH) ** -0.5
FF = 2816
NE = 8
CAP = 128
MAXI = 2 * T // CAP + NE
NEG = -1e30
LOW = -3e38

RING = 3
CW = [256] * 10 + [128] * 2
C0 = [sum(CW[:c]) for c in range(len(CW))]
NC = len(CW)
assert sum(CW) == FF and NC % RING == 0

QT = [(0, 16), (16, 128), (144, 128)]

_W = [("ident", 128), ("upper", TT), ("iota", 128), ("part", 1), ("mask", TP), ("maskd", NS),
      ("cos", NT * HALF), ("sin", NT * HALF), ("eidx", NE), ("items", MAXI)]
_WP = [("pm0", 4 * TT), ("pm1", 4 * TT), ("ptail", 4 * 16), ("pstate", 4 * SMP)]
COL, NCOL, NPOOL = {}, 0, 0
for _k, _w in _W:
    COL[_k] = (NCOL, NCOL + _w)
    NCOL += _w
for _k, _w in _WP:
    COL[_k] = (NPOOL, NPOOL + _w)
    NPOOL += _w


def shape_constants():
    c, pooling = np.zeros((P, NCOL), np.float32), np.zeros((P, NPOOL), np.float32)

    def put(name, a):
        (pooling if name[0] == "p" and name != "part" else c)[:a.shape[0], COL[name][0]:COL[name][1]] = a.reshape(a.shape[0], -1)

    put("ident", np.eye(P))
    put("upper", np.triu(np.ones((TT, TT)), 1))
    put("iota", np.tile(np.arange(P), (P, 1)))
    put("part", np.arange(P)[:, None])
    r = np.arange(P)[:, None]
    put("mask", np.where(np.arange(TP)[None] <= 144 + r, 0.0, NEG))
    put("maskd", np.where(np.arange(NS)[None] <= r % NS, 0.0, NEG))
    pos = np.concatenate([np.tile(PAST + np.arange(NS), NB), np.arange(TP)]).astype(np.float32)
    freqs = (np.float32(1) / np.float32(10000.0) ** (np.arange(HALF, dtype=np.float32) * np.float32(2.0 / ROPE))).astype(np.float32)
    ang = (pos[:, None] * freqs[None]).astype(np.float32).reshape(NT, TT, HALF).swapaxes(0, 1)
    put("cos", np.cos(ang))
    put("sin", np.sin(ang))
    put("eidx", np.tile(np.arange(NE), (P, 1)))
    put("items", np.tile(np.arange(MAXI), (P, 1)))
    def band(a, b, w):
        n = np.minimum(b[None] + 1, w)
        return ((a[:, None] <= b[None]) & (a[:, None] > b[None] - w)) / n - (a[:, None] == b[None])
    m0, m1 = np.zeros((2, TT, 4, TT))
    tail, state = np.zeros((TT, 4, 16)), np.zeros((NB * BUF, 4, SMP))
    first = TT - SMP
    for g, w in enumerate(WINDOWS):
        m0[SMP:, g, SMP:] = band(np.arange(first), np.arange(first), w)
        s = np.arange(NS)
        one = ((s[:, None] <= s[None]) & (s[:, None] > s[None] - w)) / w - (s[:, None] == s[None])
        old = (np.arange(BUF)[:, None] - BUF > s[None] - w) / w
        for b in range(NB):
            m0[b * NS:(b + 1) * NS, g, b * NS:(b + 1) * NS] = one
            state[b * BUF:(b + 1) * BUF, g, b * NS:(b + 1) * NS] = old
        q = first + np.arange(TT)
        m1[:, g] = band(q, q, w)
        tail[:, g] = band(q, q[-1] + 1 + np.arange(16), w)
    tail[:SMP] = 0.0
    put("pm0", m0)
    put("pm1", m1)
    put("ptail", tail)
    put("pstate", state)
    return c, pooling


def program(nc, a, o):
    ctx = ExitStack()

    top = [16640]

    def place(name, shape, dtype, off=None):
        n = 4 * int(np.prod(shape[1:]))
        if off is None:
            off = top[0]
            top[0] += (n + 31) // 32 * 32
        return nc.alloc_sbuf_tensor_at(name, shape, dtype, offset=off)

    X = place("X", [TT, NT, D], F32)
    H_OFF = top[0]
    HN = place("HN", [TT, NT, D], F32)
    HT_OFF = top[0]
    HT = place("HT", [P, KD, T], F32)
    CN = place("CN", [P, NCOL], F32)
    SCR_OFF = top[0]
    SCR = place("SCR", [P, D], F32)
    G_OFF = top[0]
    G = [place(f"G{i}", [TT, D], F32) for i in range(3)]
    GQ = place("GQ", [TT, QL], F32)
    GKV = place("GKV", [TT, KL], F32)
    SS = place("SS", [TT, 32], F32)
    RS = place("RS", [TT, 32], F32)
    ZB = place("ZB", [1, 512], BF16)
    RPS = [place(f"RPS{i}", [P, 4], F32) for i in range(2)]
    DS = place("DS", [P, 8], F32)
    DM = place("DM", [P, NS], F32)
    NHALF = place("NHALF", [TT, 2], F32)
    A = top[0]
    END = nc.sbuf_usable_end

    def area():
        cur = [A]

        def get(name, shape, dtype=F32, off=None):
            if off is not None:
                return place(name, shape, dtype, off)
            n = (4 * int(np.prod(shape[1:])) + 31) // 32 * 32
            t = place(name, shape, dtype, cur[0])
            cur[0] += n
            assert cur[0] <= END, (name, cur[0] - END)
            return t
        get.cur = cur
        return get

    get = area()
    GU = [get(f"GU{i}", [P, KD * 2 * 256]) for i in range(RING)]
    DN = [get(f"DN{i}", [P, 2 * D]) for i in range(RING)]
    UH = [get(f"UH{i}", [P, 2048], F32R) for i in range(3)]
    UL = [get(f"UL{i}", [P, 2048], F32R) for i in range(3)]
    FFN_END = get.cur[0]
    HTH = place("HTH", [P, KD, T], F32R, HT_OFF)
    HTL = get("HTL", [P, KD, T], F32R)
    SG = get("SG", [P, T])
    AF = get("AF", [P, T])
    AH = get("AH", [P, 2, T], F32R)
    AL = get("AL", [P, 2, T], F32R)
    get = area()
    get.cur[0] = FFN_END
    ST = get("ST", [NB * BUF, D])
    PW = get("PW", [P, KD, 256])
    DT = place("DT", [P, KD, T], F32, HT_OFF)
    PTMP = get("PTMP", [TT, 512])
    CP = get("CP", [P, NPOOL])

    get = area()
    S1 = get.cur[0]
    WIN = get("WIN", [P, KD, PROJ])
    S2 = get.cur[0]
    Q = get("Q", [TT, NT, H * QH])
    S3 = get.cur[0]
    WUQ = get("WUQ", [P, 3, H * QH])
    S5 = get.cur[0]
    QTR = get("QTR", [QH, H, T])
    S6 = get.cur[0]
    KT = get("KT", [QH, H, TP])
    S7 = get.cur[0]
    UKT = get("UKT", [NOPE, H, KL])
    QLT = get("QLT", [P, 2, NB, H * NS])
    QPT = get("QPT", [QH, NB, H * NS])
    WUV = get("WUV", [P, 2, H * VH])
    S11 = get.cur[0]
    WUK = get("WUK", [P, 2, H * NOPE])
    KVN = get("KVN", [TT, NT, KV])
    CKT = get("CKT", [P, 2, T])
    KPT = get("KPT", [QH, T])
    PR = place("PR", [TT, NT, PROJ], F32, H_OFF)
    CQT = place("CQT", [P, 3, T], F32, H_OFF + 8064)
    OT = place("OT", [P, KD, T], F32, HT_OFF)
    CC = [place(f"CC{i}", [P, NPG, KV], F32, S1 + i * 9216) for i in range(2)]
    V = place("V", [P, 3, H * VH], F32, S2)
    PP = [place(f"PP{i}", [P, TP], F32, S2 + 12288 + i * 1088) for i in range(2)]
    PPT = place("PPT", [P, 3, P], F32, S2 + 12288 + 2176)
    CT = place("CT", [P, 3, PAST], F32, S3)
    KNEW = place("KNEW", [NS, NB, KL], F32, S7)
    WO = place("WO", [P, KD, D], F32, S5)
    PD = place("PD", [P, PAST + NS], F32, H_OFF)
    PDT = place("PDT", [P, NPG + 1, P], F32, H_OFF + 4128)
    OL = place("OL", [P, KL], F32, H_OFF + 8736)
    OLT = place("OLT", [P, 2, H, SMP], F32, S11)
    QR = place("QR", [TT, 4, H, HALF], F32, SCR_OFF)
    KR = place("KR", [TT, 4, HALF], F32, SCR_OFF + 2048)

    get = area()
    get.cur[0] = FFN_END
    HNH = get("HNH", [TT, NT, D], F32R)
    HNL = get("HNL", [TT, NT, D], F32R)
    EG = get("EG", [P, 256])
    XH = place("XH", [P, KD, CAP], F32R, H_OFF)
    XL = place("XL", [P, KD, CAP], F32R, H_OFF + 4096)
    EA = place("EA", [P, 256], F32, H_OFF + 8192)
    ATH = [place("ATH0", [P, 2, CAP], F32R, H_OFF + 9216), place("ATH1", [P, 2, CAP], F32R, HT_OFF + 9600)]
    ATL = [place("ATL0", [P, 2, CAP], F32R, H_OFF + 10240), get("ATL1", [P, 2, CAP], F32R)]
    YH = place("YH", [P, D], F32R, G_OFF)
    YL = place("YL", [P, D], F32R, G_OFF + 4096)
    SEL = place("SEL", [TT, NT, CAP], F32R, HT_OFF)
    G1 = place("G1", [P, T], F32, HT_OFF + 1536)
    G2 = place("G2", [P, T], F32, HT_OFF + 2880)
    W1 = place("W1", [P, T], F32, HT_OFF + 4224)
    W2 = place("W2", [P, T], F32, HT_OFF + 5568)
    SWH = place("SWH", [P, T], F32R, HT_OFF + 6912)
    SWL = place("SWL", [P, T], F32R, HT_OFF + 8256)
    T1 = place("T1", [P, T], F32, SCR_OFF)
    T2 = place("T2", [P, T], F32, SCR_OFF + 1344)
    TS = place("TS", [TT, CAP], F32, SCR_OFF + 2688)
    WR = get("WR", [P, KD, NE])
    BR = get("BR", [TT, NE])
    RT = place("RT", [TT, 10, NT, NE], F32, G_OFF)
    RC = get("RC", [TT, 12, NT])
    TO = place("TO", [P, 6, NE], F32, G_OFF + 1024)
    IE = place("IE", [1, MAXI, NE], F32, G_OFF + 1216)
    EF = place("EF", [1, MAXI], F32, G_OFF + 1664)
    DG = place("DG", [TT, TT], F32, G_OFF + 1728)
    ONE = place("ONE", [TT, P], F32, G_OFF + 2176)
    EI = get("EI", [1, MAXI], I32)
    NI = get("NI", [1, 1], I32)
    PJ = get("PJ", [P, 1])

    PS = ctx.enter_context(nc.psum_tensor("PS", [P, 8, 512], F32))

    def sem(name):
        return ctx.enter_context(nc.semaphore(name))

    def cn(name, rows=P):
        return (CP if name in dict(_WP) else CN)[0:rows, COL[name][0]:COL[name][1]]

    ident = cn("ident")

    x_in, consts_in, gains_in = sem("x_in"), sem("consts_in"), sem("gains_in")
    gain1_in, gain4_in, smallgains_in = sem("gain1_in"), sem("gain4_in"), sem("smallgains_in")
    gain3_in = sem("gain3_in")
    pool_in = sem("pool_in")
    gu_in = [sem(f"gu_in{i}") for i in range(RING)]
    dn_in = [sem(f"dn_in{i}") for i in range(RING)]
    unit_high = [sem(f"unit_high{i}") for i in range(3)]
    unit_low = [sem(f"unit_low{i}") for i in range(3)]
    unit_used = {i: sem(f"unit_used{i}") for i in (0, 2)}
    win_in, wuq_in, wuk_in, wuv_in, wo_in = (sem(n) for n in ("win_in", "wuq_in", "wuk_in", "wuv_in", "wo_in"))
    cache_in = [sem("cache_in0"), sem("cache_in1")]
    pages_in, knew_in, router_in = sem("pages_in"), sem("knew_in"), sem("router_in")
    squares = [sem(f"squares{i}") for i in range(5)]
    normed = [sem(f"normed{i}") for i in range(5)]
    turned = [sem(f"turned{i}") for i in range(4)]
    turned_act = [sem(f"turned_act{i}") for i in range(4)]
    turned_dve = [sem(f"turned_dve{i}") for i in range(4)]
    pool_mm, pool_act, pool_dve, pool_y, pool_out = (sem(n) for n in ("pool_mm", "pool_act", "pool_dve", "pool_y", "pool_out"))
    x_pooled, x_dense, x_mixed, x_added = (sem(n) for n in ("x_pooled", "x_dense", "x_mixed", "x_added"))
    gate_mm, up_mm, silu_done, act_made, act_high, act_low, down_mm = (
        sem(n) for n in ("gate_mm", "up_mm", "silu_done", "act_made", "act_high", "act_low", "down_mm"))
    stored = sem("stored")
    dve_step = sem("dve_step")
    act_step = sem("act_step")
    inverse_root, inverse_root_qk = [sem(f"inverse_root{i}") for i in range(5)], sem("inverse_root_qk")
    pool_step = sem("pool_step")

    block = ctx.enter_context(nc.Block())

    def linker(eng, s, base=0):
        n = [0]

        def link(ins):
            n[0] += 1
            ins.then_inc(s, 1)
            eng.wait_ge(s, base + n[0])
        link.n = n
        return link

    proj_mm, proj_out = sem("proj_mm"), sem("proj_out")
    sq_q = sem("sq_q")
    latent_ready, cq_ready = sem("latent_ready"), sem("cq_ready")
    lat_t, lat_e = sem("lat_t"), sem("lat_e")
    q_mm, q_ev, q_rot, qt_t, qt_act, qt_dve = (sem(n) for n in ("q_mm", "q_ev", "q_rot", "qt_t", "qt_act", "qt_dve"))
    k_mm, k_ev, kpe_copied, v_mm, v_ev, uk_t, uk_ev, ql_mm, ql_ev, qp_copied = (
        sem(n) for n in ("k_mm", "k_ev", "kpe_copied", "v_mm", "v_ev", "uk_t", "uk_ev", "ql_mm", "ql_ev", "qp_copied"))
    s_mm, s_nm, s_exp, s_norm, s_pt, s_ptc, s_o, s_oc = (
        sem(n) for n in ("s_mm", "s_nm", "s_exp", "s_norm", "s_pt", "s_ptc", "s_o", "s_oc"))
    d_ct, d_cte_act, d_cte_dve, d_s, d_nm, d_exp, d_rs, d_pt, d_ptc_act, d_ptc_dve, d_o, d_ol, d_olt, d_olc = (
        sem(n) for n in ("d_ct", "d_cte_act", "d_cte_dve", "d_s", "d_nm", "d_exp", "d_rs", "d_pt", "d_ptc_act",
                         "d_ptc_dve", "d_o", "d_ol", "d_olt", "d_olc"))
    do_mm, do_ev, wo_mm = sem("do_mm"), sem("do_ev"), sem("wo_mm")
    r_mm, r_cnt_mm, r_dve, r_act, r_bce, items_known = (
        sem(n) for n in ("r_mm", "r_cnt_mm", "r_dve", "r_act", "r_bce", "items_known"))
    hn_high, hn_low = sem("hn_high"), sem("hn_low")
    i_sel, i_g, i_xh, i_xl, i_gu, i_sg, i_a, i_t, i_ath, i_atl, i_y, i_yh, i_yl, i_sw, i_o = (
        sem(n) for n in ("i_sel", "i_g", "i_xh", "i_xl", "i_gu", "i_sg", "i_a", "i_t", "i_ath", "i_atl", "i_y",
                         "i_yh", "i_yl", "i_sw", "i_o"))
    item_step, _ = sem("item_step"), None
    diag_made = sem("diag_made")

    def dense_weights(c):
        f, w = C0[c], CW[c]
        return (a["ffn_w_gate"][0, :, f:f + w].rearrange("(k p) f -> p k f", p=P),
                a["ffn_w_up"][0, :, f:f + w].rearrange("(k p) f -> p k f", p=P),
                a["ffn_w_down"][0, f:f + w, :].rearrange("(j p) d -> p j d", p=P))

    def expert_weights(e, c):
        f, w = C0[c], CW[c]
        one = bass.ds(e, 1)
        return (a["moe_w_gate"][0, one, :, f:f + w].rearrange("e (k p) f -> p (e k) f", p=P),
                a["moe_w_up"][0, one, :, f:f + w].rearrange("e (k p) f -> p (e k) f", p=P),
                a["moe_w_down"][0, one, f:f + w, :].rearrange("e (j p) d -> p (e j) d", p=P))

    def raw_gu(slot, w):
        return GU[slot][:, 0:KD * 2 * w].rearrange("p (k g f) -> p k g f", k=KD, g=2)

    def raw_dn(slot, w):
        return DN[slot][:, 0:w // P * D].rearrange("p (j d) -> p j d", d=D)

    def unit_source(kind, c, slot, u):
        w = CW[c]
        if u == 2:
            return DN[slot][:, 0:w // P * D], w // P * D
        if kind == "dense" and w == 256:
            return raw_gu(slot, w)[:, :, :, u * P:(u + 1) * P].rearrange("p k g f -> p (k g) f"), 2048
        n = KD * w
        return GU[slot][:, u * n:(u + 1) * n], n

    def unit(t, kind, c, u):
        src, n = unit_source(kind, c, 0, u)
        return t[u][:, 0:n].rearrange("p (k f) -> p k f", f=P) if len(src.shape) == 3 else t[u][:, 0:n]

    def load_chunk(sp, weights, w, slot, free_gu, free_dn):
        gate, up, down = weights
        if free_gu is not None:
            sp.wait_ge(unit_low[1], free_gu)
        sp.dma_start(raw_gu(slot, w)[:, :, 0, :], gate).then_inc(gu_in[slot], 16)
        sp.dma_start(raw_gu(slot, w)[:, :, 1, :], up).then_inc(gu_in[slot], 16)
        if free_dn is not None:
            sp.wait_ge(unit_low[2], free_dn)
        sp.dma_start(raw_dn(slot, w), down).then_inc(dn_in[slot], 16)

    @block.sync
    def _(sp):
        sp.dma_start(X[0:SMP, 0, :], a["x_sample"].rearrange("b s d -> (b s) d")).then_inc(x_in, 16)
        sp.dma_start(X[SMP:SMP + META, 0, :], a["meta_tokens"]).then_inc(x_in, 16)
        sp.dma_start(X[SMP + META:TT, 0, :], a["x_prompt"][0, 0:TT - SMP - META, :]).then_inc(x_in, 16)
        for t in (1, 2):
            r = t * TT - SMP - META
            sp.dma_start(X[:, t, :], a["x_prompt"][0, r:r + TT, :]).then_inc(x_in, 16)
        sp.dma_start(G[0][:, :], a["g_mix"][0:1, :].partition_broadcast(TT)).then_inc(gains_in, 16)
        sp.dma_start(CN[:, :], a["consts"]).then_inc(consts_in, 16)
        sp.dma_start(CP[:, :], a["consts_pool"]).then_inc(pool_in, 16)
        sp.dma_start(ST[:, :], a["state_pool"][0].rearrange("b n d -> (b n) d")).then_inc(pool_in, 16)
        sp.dma_start(PW[:, :, :], a["pool_w"][0].rearrange("g (c p) n -> p (g c) n", p=P)).then_inc(pool_in, 16)
        sp.dma_start(G[1][:, :], a["pool_scale"][0:1, :].partition_broadcast(TT)).then_inc(gains_in, 16)
        sp.dma_start(G[2][:, :], a["g_ffn"][0:1, :].partition_broadcast(TT)).then_inc(gains_in, 16)
        sp.dma_start(GQ[:, :], a["mla_g_q"][0:1, :].partition_broadcast(TT)).then_inc(smallgains_in, 16)
        sp.dma_start(GKV[:, :], a["mla_g_kv"][0:1, :].partition_broadcast(TT)).then_inc(smallgains_in, 16)
        for c in range(RING):
            load_chunk(sp, dense_weights(c), CW[c], c, None, None)
        sp.wait_ge(x_pooled, NT)
        sp.dma_start(G[0][:, :], a["g_mix"][1:2, :].partition_broadcast(TT)).then_inc(gain1_in, 16)
        for c in range(RING, NC):
            load_chunk(sp, dense_weights(c), CW[c], c % RING, c - RING + 1, c - RING + 1)
        sp.wait_ge(unit_low[2], NC)
        sp.wait_ge(unit_low[1], NC)
        sp.dma_start(WIN[:, :, :], a["mla_w_in"][0].rearrange("(k p) n -> p k n", p=P)).then_inc(win_in, 16)
        sp.dma_start(WUQ[:, :, :], a["mla_w_uq"][0].rearrange("(k p) n -> p k n", p=P)).then_inc(wuq_in, 16)
        sp.wait_ge(x_dense, NT)
        sp.dma_start(G[2][:, :], a["g_ffn"][1:2, :].partition_broadcast(TT)).then_inc(gain3_in, 16)
        sp.dma_start(WUK[:, :, :], a["mla_w_uk"][0].rearrange("(c p) h n -> p c (h n)", p=P)).then_inc(wuk_in, 16)
        sp.dma_start(WUV[:, :, :], a["mla_w_uv"][0].rearrange("(c p) h v -> p c (h v)", p=P)).then_inc(wuv_in, 16)

        nphys = a["cache_ckv"].shape[1]

        def load_cache(b):
            with sp.Fori(0, NPG) as i:
                page = sp.value_load(a["page_table"][b:b + 1, bass.ds(i, 1)], min_val=0, max_val=nphys - 1)
                one, to = bass.ds(page, 1), bass.ds(i, 1)
                sp.dma_start(CC[b % 2][:, to, 0:KL], a["cache_ckv"][0, one, :, :].rearrange("e p c -> p e c"))\
                  .then_inc(cache_in[b % 2], 16)
                sp.dma_start(CC[b % 2][:, to, KL:KV], a["cache_kpe"][0, one, :, :].rearrange("e p c -> p e c"))\
                  .then_inc(cache_in[b % 2], 16)

        sp.wait_ge(proj_mm, 2 * NT)
        for b in range(2):
            load_cache(b)
        sp.wait_ge(uk_ev, H * 2)
        sp.wait_ge(ql_ev, 2 * 2)
        for b in range(NB):
            sp.dma_start(KNEW[:, b, :], KVN[b * NS:(b + 1) * NS, 0, 0:KL]).then_inc(knew_in, 16)
        sp.wait_ge(s_oc, H)
        sp.wait_ge(qp_copied, 1)
        sp.dma_start(WO[:, :, :], a["mla_w_o"][0].rearrange("(k p) n -> p k n", p=P)).then_inc(wo_in, 16)
        for b in range(2, NB):
            sp.wait_ge(d_o, b - 1)
            load_cache(b)
        sp.wait_ge(wo_mm, 2 * NT)
        sp.dma_start(WR[:, :, :], a["moe_w_router"][0].rearrange("(k p) n -> p k n", p=P)).then_inc(router_in, 16)
        sp.dma_start(BR[:, :], a["moe_b_router"][0:1, :].partition_broadcast(TT)).then_inc(router_in, 16)
        sp.wait_ge(normed[3], NT)
        sp.dma_start(G[2][:, :], a["g_final"].rearrange("(a d) -> a d", a=1).partition_broadcast(TT)).then_inc(gain4_in, 16)
        sp.wait_ge(items_known, 2)
        n_items = sp.value_load(NI[0:1, 0:1], min_val=1, max_val=MAXI)
        with sp.Fori(0, n_items) as j:
            e = sp.value_load(EI[0:1, bass.ds(j, 1)], min_val=0, max_val=NE - 1)
            for c in range(NC):
                free = NC - RING + 1 + j * NC + c
                load_chunk(sp, expert_weights(e, c), CW[c], c % RING, free, free)

    @block.gpsimd
    def _(pool):
        count = [0]

        def store(dst, src):
            count[0] += 16
            pool.dma_start(dst, src).then_inc(stored, 16)

        nc.gpsimd.memset(NHALF[:, :], -0.5).then_inc(pool_step, 1)
        pool.wait_ge(pool_step, 1)
        steps = [1]

        def inverse_roots(i, step, width, done):
            cols = slice(i, i + step * (width - 1) + 1, step)
            steps[0] += 1
            nc.gpsimd.tensor_scalar(RS[:, cols], SS[:, cols], EPS, None, ALU.add).then_inc(pool_step, 1)
            pool.wait_ge(pool_step, steps[0])
            nc.gpsimd.tensor_tensor(RS[:, cols], RS[:, cols], NHALF[:, 0:width], ALU.pow).then_inc(done, 1)

        def roots_of(n):
            for t in range(NT):
                pool.wait_ge(squares[n], t + 1)
                inverse_roots(3 * n + t, 1, 1, inverse_root[n])

        roots_of(0)
        pool.wait_ge(normed[0], NT)
        pool.dma_start(o["pool_prompt"][0, 0], HN[TT - BUF:TT, 2, :]).then_inc(pool_out, 16)
        for b in range(NB):
            pool.dma_start(o["pool_sample"][0, b, BUF - NS:BUF, :], HN[b * NS:(b + 1) * NS, 0, :]).then_inc(pool_out, 16)
            pool.dma_start(o["pool_sample"][0, b, 0:BUF - NS, :], a["state_pool"][0, b, NS:BUF, :]).then_inc(pool_out, 16)
        roots_of(1)
        roots_of(2)
        for t in range(NT):
            pool.wait_ge(sq_q, 2 * t + 2)
            inverse_roots(15 + t, 3, 2, inverse_root_qk)
        pool.wait_ge(latent_ready, NT)
        store(o["ckv_sample"][0].rearrange("b s c -> (b s) c"), KVN[0:SMP, 0, 0:KL])
        store(o["kpe_sample"][0].rearrange("b s c -> (b s) c"), KVN[0:SMP, 0, KL:KV])
        for t in range(NT):
            p0 = SMP if t == 0 else 0
            r0 = t * TT + p0 - SMP
            store(o["ckv_prompt"][0, 0, r0:r0 + TT - p0, :], KVN[p0:TT, t, 0:KL])
            store(o["kpe_prompt"][0, 0, r0:r0 + TT - p0, :], KVN[p0:TT, t, KL:KV])
        pool.wait_ge(lat_e, 6)
        for h in range(H):
            nc.gpsimd.tensor_copy(KT[NOPE:QH, h, :], KPT[NOPE:QH, SMP:T]).then_inc(kpe_copied, 1)
        roots_of(3)
        roots_of(4)
        pool.wait_ge(normed[4], NT)
        store(o["y_sample"].rearrange("b s d -> (b s) d"), HN[0:SMP, 0, :])
        store(o["y_prompt"][0, 0:TT - SMP - META, :], HN[SMP + META:TT, 0, :])
        for t in (1, 2):
            r = t * TT - SMP - META
            store(o["y_prompt"][0, r:r + TT, :], HN[:, t, :])
        pool.wait_ge(stored, count[0])
        pool.wait_ge(pool_out, 16 * (1 + 2 * NB))

    @block.scalar
    def _(act):
        link = linker(act, act_step)

        def squares_of(n, ready):
            for t in range(NT):
                ready(t)
                if t:
                    act.wait_ge(squares[n], t)
                nc.scalar.activation(SCR[0:TT, :], X[:, t, :], ACT.Square, scale=1 / 32,
                                     accum_out=SS[:, 3 * n + t:3 * n + t + 1]).then_inc(squares[n], 1)

        def turn_out(n, dst):
            for d in range(1, KD, 2):
                act.wait_ge(turned[n], d + 1)
                nc.scalar.copy(dst[:, d, :], PS[:, d, 0:T]).then_inc(turned_act[n], 1)

        def split_high(kind, c, u, waits):
            slot = c % RING
            src, n = unit_source(kind, c, slot, u)
            raw, used = waits
            act.wait_ge(dn_in[slot] if u == 2 else gu_in[slot], raw)
            if used is not None:
                act.wait_ge(*used)
            nc.scalar.copy(unit(UH, kind, c, u), src).then_inc(unit_high[u], 1)

        squares_of(0, lambda t: act.wait_ge(x_in, 16 * 5))
        for d in range(1, KD, 2):
            act.wait_ge(pool_mm, d + 1)
            nc.scalar.copy(DT[:, d, :], PS[:, d, 0:T]).then_inc(pool_act, 1)
        squares_of(1, lambda t: act.wait_ge(x_pooled, t + 1))
        for u in range(3):
            split_high("dense", 0, u, (16 if u == 2 else 32, None))
        for d in range(KD):
            act.wait_ge(turned[1], d + 1)
            nc.scalar.copy(HTH[:, d, :], PS[:, d, 0:T]).then_inc(turned_act[1], 1)

        def dense_used(c, q, u):
            if u == 2:
                return down_mm, 2 + ff_tile(q, CW[c] // P - 1, c) + 1
            if CW[c] == 256:
                return up_mm, ff_tile(q, u, c) + 1
            return (unit_used[0], c - 9) if u == 0 else (up_mm, ff_tile(q, 0, c) + 1)

        def dense_step(c, q, rounds, last):
            for j in range(2):
                if j < CW[c] // P:
                    tile = ff_tile(q, j, c)
                    act.wait_ge(gate_mm, tile + 1)
                    nc.scalar.activation(SG[:, :], PS[:, 0, 0:T], ACT.Silu).then_inc(silu_done, 1)
                    act.wait_ge(act_made, tile + 1)
                    act.wait_ge(down_mm, tile + 1)
                    nc.scalar.copy(AH[:, j if CW[c] == 256 else c % 2, :], AF[:, :]).then_inc(act_high, 1)
                if not last:
                    nxt = c + 1
                    split_high("dense", nxt, j, (rounds(nxt) * 32, dense_used(c, q, j)))
            if not last:
                split_high("dense", c + 1, 2, (rounds(c + 1) * 16, dense_used(c, q, 2)))

        def ff_tile(q, j, c):
            return 2 * q + j if CW[c] == 256 else 20 + (c - 10)

        with act.Fori(0, 3) as r:
            for i in range(RING):
                dense_step(i, r * RING + i, lambda n, r=r: r + 1 + (n // RING), False)
        for c in range(9, NC):
            dense_step(c, c, lambda n: n // RING + 1, c == NC - 1)
        squares_of(2, lambda t: act.wait_ge(x_dense, t + 1))
        turn_out(2, HT)

        for t in range(NT):
            act.wait_ge(proj_mm, 2 * t + 1)
            link(nc.scalar.copy(PR[:, t, 0:512], PS[0:TT, 2 * t, :]))
            act.wait_ge(proj_mm, 2 * t + 2)
            nc.scalar.copy(PR[:, t, 512:PROJ], PS[0:TT, 2 * t + 1, 0:PROJ - 512]).then_inc(proj_out, 1)
            act.wait_ge(proj_out, t + 1)
            if t:
                act.wait_ge(sq_q, 2 * t)
            nc.scalar.activation(SCR[0:TT, 0:QL], PR[:, t, 0:QL], ACT.Square, scale=float(QL) ** -0.5,
                                 accum_out=SS[:, 15 + t:16 + t]).then_inc(sq_q, 1)
            act.wait_ge(sq_q, 2 * t + 1)
            nc.scalar.activation(SCR[0:TT, 0:KL], PR[:, t, QL:QL + KL], ACT.Square, scale=1 / 16,
                                 accum_out=SS[:, 18 + t:19 + t]).then_inc(sq_q, 1)
        for t in range(NT):
            for i in range(2):
                act.wait_ge(q_mm, 3 * t + i + 1)
                nc.scalar.copy(Q[:, t, i * 512:(i + 1) * 512], PS[0:TT, q_bank(t, i), :]).then_inc(q_ev, 1)
        for h in range(1, H, 2):
            act.wait_ge(qt_t, h + 1)
            nc.scalar.copy(QTR[:, h, :], PS[0:QH, h % 8, 0:T]).then_inc(qt_act, 1)
        for h in range(H):
            act.wait_ge(k_mm, h + 1)
            nc.scalar.copy(KT[0:NOPE, h, :], PS[0:NOPE, h % 4, 0:TP]).then_inc(k_ev, 1)
        for h in range(H):
            for c in range(2):
                n = 2 * h + c
                if n % 4 == 3:
                    act.wait_ge(uk_t, n + 1)
                    src = PS[0:NOPE, 4 + n // 4 % 2, :].rearrange("p (i x) -> p i x", i=2)
                    nc.scalar.copy(UKT[:, h - 1:h + 1, :], src).then_inc(uk_ev, 4)
        for h in range(H):
            for i, (p0, rows) in enumerate(QT):
                n = 3 * h + i
                keys = p0 + rows
                act.wait_ge(s_nm, n + 1)
                nc.scalar.activation(PP[n % 2][0:rows, 0:keys], PP[n % 2][0:rows, 0:keys], ACT.Exp, scale=SCALE,
                                     bias=RPS[n % 2][0:rows, 1:2], accum_out=RPS[n % 2][0:rows, 2:3]).then_inc(s_exp, 1)
                act.wait_ge(s_pt, n + 1)
                if n >= 1:
                    act.wait_ge(s_o, n)
                if i:
                    nc.scalar.copy(PPT[:, 1:i + 1, 0:rows],
                                   PS[:, 2, P:(i + 1) * P].rearrange("p (b r) -> p b r", r=P)[:, :, 0:rows])
                nc.scalar.copy(PPT[0:QT[0][1], 0, 0:rows], PS[0:QT[0][1], 2, 0:rows]).then_inc(s_ptc, 1)
        for b in range(NB):
            for g in (1, 3, 5):
                act.wait_ge(d_ct, 6 * b + g + 1)
                if b:
                    act.wait_ge(d_s, b)
                part = g // 2
                lo, hi = (NOPE, QH) if part == 2 else (0, P)
                nc.scalar.copy(CT[lo:hi, part, 512:1024], PS[lo:hi, 3 + (6 * b + g) % 2, :]).then_inc(d_cte_act, 1)
            act.wait_ge(d_nm, b + 1)
            if b:
                act.wait_ge(d_pt, 3 * b)
            nc.scalar.activation(PD[:, 0:PAST], PS[:, 0:2, :].rearrange("p b n -> p (b n)"), ACT.Exp, scale=SCALE,
                                 bias=DS[:, 3:4], accum_out=DS[:, 4:5]).then_inc(d_exp, 1)
            nc.scalar.activation(PD[:, PAST:PAST + NS], DM[:, :], ACT.Exp, scale=SCALE,
                                 bias=DS[:, 3:4], accum_out=DS[:, 5:6]).then_inc(d_exp, 1)
            act.wait_ge(d_pt, 3 * b + 1)
            if b:
                act.wait_ge(d_o, b)
            nc.scalar.copy(PDT[:, 0:4, :].rearrange("p a q -> p (a q)"), PS[:, 3, :]).then_inc(d_ptc_act, 1)
            act.wait_ge(d_olt, b + 1)
            nc.scalar.copy(OLT[:, :, :, b * NS:(b + 1) * NS],
                           PS[:, 6, 0:2 * P].rearrange("p (c h s) -> p c h s", c=2, h=H)).then_inc(d_olc, 1)
        for g in range(2):
            act.wait_ge(do_mm, g + 1)
            nc.scalar.copy(OT[:, 4 * g:4 * g + 4, 0:SMP], PS[:, g, 0:4 * SMP].rearrange("p (k t) -> p k t", k=4)).then_inc(do_ev, 1)
        squares_of(3, lambda t: act.wait_ge(x_mixed, t + 1))
        turn_out(3, HT)
        for t in range(NT):
            act.wait_ge(normed[3], t + 1)
            nc.scalar.copy(HNH[:, t, :], HN[:, t, :]).then_inc(hn_high, 1)
        act.wait_ge(r_dve, 1)
        nc.scalar.activation(RC[:, 6:8, :], RC[:, 4:6, :], ACT.Exp).then_inc(r_act, 1)
        for i in range(4):
            act.wait_ge(r_cnt_mm, 1 + NT * (i + 1))
            nc.scalar.copy((G1, G2, W1, W2)[i][:, :], PS[:, 4 + i, 0:T]).then_inc(r_bce, 1)

        act.wait_ge(items_known, 2)
        n_items = act.value_load(NI[0:1, 0:1], min_val=1, max_val=MAXI)
        with act.Fori(0, n_items) as j:
            fill = NC // RING

            def split(c, u):
                n = fill + j * fill + c // RING + 1
                used = None if c == 0 else ((unit_used[0], 2 + NC * j + c), (i_gu, NC * j + c),
                                            (unit_used[2], NC * j + c))[u]
                split_high("moe", c, u, (n * (16 if u == 2 else 32), used))

            split(0, 0)
            split(0, 1)
            for g in range(2):
                act.wait_ge(i_g, 4 * j + 2 * g + 1)
                nc.scalar.copy(XH[:, 4 * g:4 * g + 4, :].rearrange("p k c -> p (k c)"), PS[:, 6, :]).then_inc(i_xh, 1)
            for c in range(NC + 1):
                if c + 1 < NC:
                    split(c + 1, 0)
                if c < NC:
                    w = CW[c]
                    act.wait_ge(i_gu, NC * j + c + 1)
                    if c:
                        act.wait_ge(i_a, NC * j + c)
                    nc.scalar.activation(EG[:, 0:w], PS[:, c % RING, 0:w], ACT.Silu).then_inc(i_sg, 1)
                if c + 1 < NC:
                    split(c + 1, 1)
                if c >= 1:
                    w = CW[c - 1]
                    act.wait_ge(i_t, NC * j + c)
                    nc.scalar.copy(ATH[(c - 1) % 2][:, 0:w // P, :].rearrange("p k c -> p (k c)"), PS[:, 3, 0:w]).then_inc(i_ath, 1)
                    split(c - 1, 2)
            act.wait_ge(unit_used[2], NC * j + NC)
            nc.scalar.copy(YH[:, :], PS[:, 4:6, :].rearrange("p b n -> p (b n)")).then_inc(i_yh, 1)

        act.wait_ge(x_added, n_items * (2 * NT))
        squares_of(4, lambda t: None)

    @block.vector
    def _(dve):
        link = linker(dve, dve_step)
        V_ = nc.vector

        link(V_.memset(ZB[:, :], 0.0))

        def norm(n, gain):
            for t in range(NT):
                i = 3 * n + t
                dve.wait_ge(inverse_root[n], t + 1)
                V_.scalar_tensor_tensor(out=HN[:, t, :], in0=X[:, t, :], scalar=RS[:, i:i + 1], in1=gain,
                                        op0=ALU.mult, op1=ALU.mult).then_inc(normed[n], 1)

        def turn_out(n, dst):
            for d in range(0, KD, 2):
                dve.wait_ge(turned[n], d + 1)
                V_.tensor_copy(dst[:, d, :], PS[:, d, 0:T]).then_inc(turned_dve[n], 1)

        def split_low(kind, c, u, high):
            src, n = unit_source(kind, c, c % RING, u)
            dve.wait_ge(unit_high[u], high)
            V_.tensor_tensor(unit(UL, kind, c, u), src, unit(UH, kind, c, u).bitcast(F32),
                             ALU.subtract).then_inc(unit_low[u], 1)

        dve.wait_ge(gains_in, 16 * 3)
        norm(0, G[0][:, :])
        for d in range(0, KD, 2):
            dve.wait_ge(pool_mm, d + 1)
            V_.tensor_copy(DT[:, d, :], PS[:, d, 0:T]).then_inc(pool_dve, 1)
        for t in range(NT):
            for half in range(2):
                dve.wait_ge(pool_y, 2 * t + half + 1)
                cols = slice(half * 512, half * 512 + 512)
                link(V_.tensor_tensor(PTMP[:, :], PS[0:TT, 2 * t + half, :], G[1][:, cols], ALU.mult))
                ins = V_.tensor_tensor(X[:, t, cols], X[:, t, cols], PTMP[:, :], ALU.add)
                if half == 0:
                    link(ins)
            ins.then_inc(x_pooled, 1)
            dve.wait_ge(x_pooled, t + 1)
        dve.wait_ge(pool_out, 16 * (1 + 2 * NB))
        norm(1, G[2][:, :])
        for u in range(3):
            split_low("dense", 0, u, 1)
        for d in range(KD):
            dve.wait_ge(turned_act[1], d + 1)
            V_.tensor_tensor(HTL[:, d, :], PS[:, d, 0:T], HTH[:, d, :].bitcast(F32), ALU.subtract)\
              .then_inc(turned_dve[1], 1)

        def ff_tile(q, j, c):
            return 2 * q + j if CW[c] == 256 else 20 + (c - 10)

        def dense_step(c, q, last):
            for j in range(2):
                if j < CW[c] // P:
                    tile = ff_tile(q, j, c)
                    half = j if CW[c] == 256 else c % 2
                    dve.wait_ge(silu_done, tile + 1)
                    dve.wait_ge(up_mm, tile + 1)
                    dve.wait_ge(unit_low[2] if j == 0 else act_low, q + 1 if j == 0 else tile)
                    V_.tensor_tensor(AF[:, :], SG[:, :], PS[:, 1, 0:T], ALU.mult).then_inc(act_made, 1)
                    dve.wait_ge(act_high, tile + 1)
                    V_.tensor_tensor(AL[:, half, :], AF[:, :], AH[:, half, :].bitcast(F32), ALU.subtract)\
                      .then_inc(act_low, 1)
                if not last:
                    split_low("dense", c + 1, j, q + 2)
            if not last:
                split_low("dense", c + 1, 2, q + 2)

        with dve.Fori(0, 3) as r:
            for i in range(RING):
                dense_step(i, r * RING + i, False)
        for c in range(9, NC):
            dense_step(c, c, c == NC - 1)
        dve.wait_ge(down_mm, 2 + 22)
        for t in range(NT):
            for half in range(2):
                cols = slice(half * 512, half * 512 + 512)
                ins = V_.tensor_tensor(X[:, t, cols], X[:, t, cols], PS[0:TT, 2 + 2 * t + half, :], ALU.add)
                if half == 0:
                    link(ins)
            ins.then_inc(x_dense, 1)
            dve.wait_ge(x_dense, t + 1)
        dve.wait_ge(gain1_in, 16)
        norm(2, G[0][:, :])
        turn_out(2, HT)

        dve.wait_ge(smallgains_in, 32)
        cos = cn("cos", TT).rearrange("p (t f) -> p t f", t=NT)
        sin = cn("sin", TT).rearrange("p (t f) -> p t f", t=NT)
        for t in range(NT):
            dve.wait_ge(inverse_root_qk, t + 1)
            dve.wait_ge(proj_out, t + 1)
            V_.scalar_tensor_tensor(out=PR[:, t, 0:QL], in0=PR[:, t, 0:QL], scalar=RS[:, 15 + t:16 + t],
                                    in1=GQ[:, :], op0=ALU.mult, op1=ALU.mult).then_inc(cq_ready, 1)
            V_.scalar_tensor_tensor(out=KVN[:, t, 0:KL], in0=PR[:, t, QL:QL + KL], scalar=RS[:, 18 + t:19 + t],
                                    in1=GKV[:, :], op0=ALU.mult, op1=ALU.mult)
            x1, x2 = PR[:, t, QL + KL:QL + KL + HALF], PR[:, t, QL + KL + HALF:PROJ]
            V_.tensor_tensor(KR[:, 0, :], x1, cos[:, t, :], ALU.mult)
            V_.tensor_tensor(KR[:, 1, :], x2, sin[:, t, :], ALU.mult)
            V_.tensor_tensor(KR[:, 2, :], x2, cos[:, t, :], ALU.mult)
            link(V_.tensor_tensor(KR[:, 3, :], x1, sin[:, t, :], ALU.mult))
            link(V_.tensor_tensor(KVN[:, t, KL:KL + HALF], KR[:, 0, :], KR[:, 1, :], ALU.subtract))
            V_.tensor_tensor(KVN[:, t, KL + HALF:KV], KR[:, 2, :], KR[:, 3, :], ALU.add).then_inc(latent_ready, 1)
            dve.wait_ge(latent_ready, t + 1)
        for n in range(6):
            dve.wait_ge(lat_t, n + 1)
            if n < 3:
                V_.tensor_copy(CQT[:, n, :], PS[:, n, 0:T]).then_inc(lat_e, 1)
            elif n < 5:
                V_.tensor_copy(CKT[:, n - 3, :], PS[:, n, 0:T]).then_inc(lat_e, 1)
            else:
                V_.tensor_copy(KPT[NOPE:QH, :], PS[NOPE:QH, n, 0:T]).then_inc(lat_e, 1)
        for t in range(NT):
            dve.wait_ge(q_mm, 3 * t + 3)
            link(V_.tensor_copy(Q[:, t, 1024:1536], PS[0:TT, q_bank(t, 2), :]))
            dve.wait_ge(q_ev, 2 * (t + 1))
            pe_part = Q[:, t, :].rearrange("p (h x) -> p h x", h=H)
            x1, x2 = pe_part[:, :, NOPE:NOPE + HALF], pe_part[:, :, NOPE + HALF:QH]
            c3 = cos[:, t:t + 1, :].to_broadcast([TT, H, HALF])
            s3 = sin[:, t:t + 1, :].to_broadcast([TT, H, HALF])
            V_.tensor_tensor(QR[:, 0], x1, c3, ALU.mult)
            V_.tensor_tensor(QR[:, 1], x2, s3, ALU.mult)
            V_.tensor_tensor(QR[:, 2], x2, c3, ALU.mult)
            link(V_.tensor_tensor(QR[:, 3], x1, s3, ALU.mult))
            V_.tensor_tensor(x1, QR[:, 0], QR[:, 1], ALU.subtract)
            ins = V_.tensor_tensor(x2, QR[:, 2], QR[:, 3], ALU.add)
            ins.then_inc(q_rot, 1)
            dve.wait_ge(q_rot, t + 1)
        for h in range(0, H, 2):
            dve.wait_ge(qt_t, h + 1)
            V_.tensor_copy(QTR[:, h, :], PS[0:QH, h % 8, 0:T]).then_inc(qt_dve, 1)
        dve.wait_ge(qt_dve, H // 2)
        dve.wait_ge(qt_act, H // 2)
        V_.tensor_copy(QPT[NOPE:QH, :, :].rearrange("p b (h s) -> p h b s", h=H),
                       QTR[NOPE:QH, :, 0:SMP].rearrange("p h (b s) -> p h b s", b=NB)).then_inc(qp_copied, 1)
        for i, (p0, rows) in enumerate(QT):
            for half in range(2):
                n = 2 * i + half
                dve.wait_ge(v_mm, n + 1)
                V_.tensor_copy(V[0:rows, i, half * 512:(half + 1) * 512], PS[0:rows, 6 + half, :]).then_inc(v_ev, 1)
        for n in range(4):
            c, g = n // 2, n % 2
            dve.wait_ge(ql_mm, n + 1)
            V_.tensor_copy(QLT[:, c, :, :].rearrange("p b (h s) -> p h b s", h=H)[:, 8 * g:8 * g + 8],
                           PS[:, n, :].rearrange("p (h b s) -> p h b s", h=8, b=NB)).then_inc(ql_ev, 1)
        for h in range(H):
            for i, (p0, rows) in enumerate(QT):
                n = 3 * h + i
                keys = p0 + rows
                st = RPS[n % 2]
                dve.wait_ge(s_mm, n + 1)
                if n >= 2:
                    dve.wait_ge(s_pt, n - 1)
                V_.tensor_tensor_reduce(PP[n % 2][0:rows, 0:keys], PS[0:rows, n % 2, 0:keys],
                                        cn("mask")[0:rows, 144 - p0:144 - p0 + keys], 1.0, LOW, ALU.add, ALU.max,
                                        st[0:rows, 0:1]).then_inc(dve_step, 1)
                link.n[0] += 1
                dve.wait_ge(dve_step, link.n[0])
                V_.tensor_scalar(st[0:rows, 1:2], st[0:rows, 0:1], -SCALE, None, ALU.mult).then_inc(s_nm, 1)
                dve.wait_ge(s_exp, n + 1)
                link(V_.reciprocal(st[0:rows, 3:4], st[0:rows, 2:3]))
                V_.tensor_scalar(PP[n % 2][0:rows, 0:keys], PP[n % 2][0:rows, 0:keys], st[0:rows, 3:4], None,
                                 ALU.mult).then_inc(s_norm, 1)
            lo = h % 2 * VH
            dve.wait_ge(s_o, 3 * h + 3)
            V_.tensor_copy(OT[lo:lo + VH, h // 2, SMP:T], PS[lo:lo + VH, 6 + h // 2 % 2, 0:TP]).then_inc(s_oc, 1)
        for b in range(NB):
            for g in (0, 2, 4):
                dve.wait_ge(d_ct, 6 * b + g + 1)
                if b:
                    dve.wait_ge(d_s, b)
                part = g // 2
                lo, hi = (NOPE, QH) if part == 2 else (0, P)
                V_.tensor_copy(CT[lo:hi, part, 0:512], PS[lo:hi, 3 + (6 * b + g) % 2, :]).then_inc(d_cte_dve, 1)
            dve.wait_ge(d_s, b + 1)
            if b:
                dve.wait_ge(d_exp, 2 * b)
            link(V_.tensor_tensor_reduce(DM[:, :], PS[:, 2, 0:NS], cn("maskd"), 1.0, LOW, ALU.add, ALU.max, DS[:, 0:1]))
            link(V_.tensor_reduce(DS[:, 1:2], PS[:, 0:2, :].rearrange("p b n -> p (b n)"), AX.X, ALU.max))
            link(V_.tensor_tensor(DS[:, 2:3], DS[:, 0:1], DS[:, 1:2], ALU.max))
            V_.tensor_scalar(DS[:, 3:4], DS[:, 2:3], -SCALE, None, ALU.mult).then_inc(d_nm, 1)
            dve.wait_ge(d_exp, 2 * b + 2)
            link(V_.tensor_tensor(DS[:, 6:7], DS[:, 4:5], DS[:, 5:6], ALU.add))
            link(V_.reciprocal(DS[:, 7:8], DS[:, 6:7]))
            if b:
                dve.wait_ge(d_o, b)
            dve.wait_ge(d_pt, 3 * b + 2)
            V_.tensor_copy(PDT[:, 4:8, :].rearrange("p a q -> p (a q)"), PS[:, 4, :]).then_inc(d_ptc_dve, 1)
            dve.wait_ge(d_pt, 3 * b + 3)
            V_.tensor_copy(PDT[0:NS, 8, :], PS[0:NS, 7, 0:P]).then_inc(d_ptc_dve, 1)
            dve.wait_ge(d_o, b + 1)
            if b:
                dve.wait_ge(d_olt, b)
            V_.tensor_scalar(OL[:, :], PS[:, 5, 0:KL], DS[:, 7:8], None, ALU.mult).then_inc(d_ol, 1)
        for t in range(NT):
            for half in range(2):
                cols = slice(half * 512, half * 512 + 512)
                dve.wait_ge(wo_mm, 2 * t + half + 1)
                ins = V_.tensor_tensor(X[:, t, cols], X[:, t, cols], PS[0:TT, 2 + 2 * t + half, :], ALU.add)
                if half == 0:
                    link(ins)
            ins.then_inc(x_mixed, 1)
            dve.wait_ge(x_mixed, t + 1)
        dve.wait_ge(gain3_in, 16)
        norm(3, G[2][:, :])
        turn_out(3, HT)
        dve.wait_ge(stored, 16 * (2 + 2 * NT))
        for t in range(NT):
            dve.wait_ge(hn_high, t + 1)
            V_.tensor_tensor(HNL[:, t, :], HN[:, t, :], HNH[:, t, :].bitcast(F32), ALU.subtract).then_inc(hn_low, 1)

        def rt(i):
            return RT[:, i, :, :]

        def rc(i):
            return RC[:, i, :]

        def wide(x):
            return x.unsqueeze(2).to_broadcast([TT, NT, NE])

        eidx = cn("eidx", TT).unsqueeze(1).to_broadcast([TT, NT, NE])
        link(V_.memset(ONE[:, :], 1.0))
        dve.wait_ge(r_mm, 1)
        link(V_.tensor_copy(rt(0), PS[0:TT, 0, 0:NT * NE].rearrange("p (t e) -> p t e", t=NT)))
        dve.wait_ge(router_in, 32)
        link(V_.tensor_tensor(rt(1), rt(0), BR[:, :].unsqueeze(1).to_broadcast([TT, NT, NE]), ALU.add))

        def one_hot_of_max(src, dst, c):
            link(V_.tensor_reduce(rc(c), src, AX.X, ALU.max))
            link(V_.tensor_tensor(rt(6), src, wide(rc(c)), ALU.is_equal))
            link(V_.tensor_scalar(rt(6), rt(6), -float(NE), float(NE), ALU.mult, ALU.add))
            link(V_.tensor_tensor(rt(6), rt(6), eidx, ALU.add))
            link(V_.tensor_reduce(rc(c + 1), rt(6), AX.X, ALU.min))
            link(V_.tensor_tensor(dst, eidx, wide(rc(c + 1)), ALU.is_equal))

        one_hot_of_max(rt(1), rt(3), 0)
        link(V_.scalar_tensor_tensor(out=rt(4), in0=rt(3), scalar=LOW, in1=rt(1), op0=ALU.mult, op1=ALU.add))
        one_hot_of_max(rt(4), rt(5), 2)
        for i, hot in ((8, 3), (9, 5)):
            link(V_.tensor_tensor(rt(6), rt(0), rt(hot), ALU.mult))
            link(V_.tensor_reduce(rc(i), rt(6), AX.X, ALU.add))
        link(V_.tensor_tensor(rc(10), rc(8), rc(9), ALU.max))
        link(V_.tensor_tensor(rc(4), rc(8), rc(10), ALU.subtract))
        V_.tensor_tensor(rc(5), rc(9), rc(10), ALU.subtract).then_inc(r_dve, 1)
        V_.tensor_tensor(rt(8), rt(3), rt(5), ALU.add).then_inc(diag_made, 1)
        dve.wait_ge(r_act, 1)
        link(V_.tensor_tensor(rc(10), rc(6), rc(7), ALU.add))
        link(V_.reciprocal(rc(11), rc(10)))
        link(V_.tensor_tensor(rc(6), rc(6), rc(11), ALU.mult))
        link(V_.tensor_tensor(rc(7), rc(7), rc(11), ALU.mult))
        dve.wait_ge(r_cnt_mm, 1)
        link(V_.tensor_copy(rt(9), PS[0:TT, 1, 0:NT * NE].rearrange("p (t e) -> p t e", t=NT)))
        link(V_.tensor_copy(TO[:, 0, :], PS[:, 2, 0:NE]))
        link(V_.tensor_scalar(TO[:, 1, :], TO[:, 0, :], 0.0, None, ALU.is_gt))
        for m in range(1, NT):
            link(V_.scalar_tensor_tensor(out=TO[:, 1, :], in0=TO[:, 0, :], scalar=float(m * CAP), in1=TO[:, 1, :],
                                         op0=ALU.is_gt, op1=ALU.add))
        link(V_.tensor_copy(TO[:, 2, :], TO[:, 1, :]))
        for e in range(1, NE):
            link(V_.tensor_tensor(TO[:, 2, e:e + 1], TO[:, 2, e:e + 1], TO[:, 2, e - 1:e], ALU.add))
        link(V_.tensor_tensor(TO[:, 3, :], TO[:, 2, :], TO[:, 1, :], ALU.subtract))
        V_.tensor_copy(NI[0:1, 0:1], TO[0:1, 2, NE - 1:NE]).then_inc(items_known, 1)
        link(V_.tensor_tensor(IE[:, :, :], CN[0:1, COL["items"][0]:COL["items"][1]].unsqueeze(2).to_broadcast([1, MAXI, NE]),
                              TO[0:1, 2:3, :].to_broadcast([1, MAXI, NE]), ALU.is_ge))
        link(V_.tensor_reduce(EF[:, :], IE[:, :, :], AX.X, ALU.add))
        V_.tensor_scalar(EI[:, :], EF[:, :], float(NE - 1), None, ALU.min).then_inc(items_known, 1)
        link(V_.tensor_scalar(TO[:, 4, :], TO[:, 3, :], float(CAP), None, ALU.mult))
        link(V_.tensor_tensor(rt(9), rt(9), TO[0:TT, 4:5, :].to_broadcast([TT, NT, NE]), ALU.add))
        for i, hot in ((8, 3), (9, 5)):
            link(V_.tensor_tensor(rt(6), rt(9), rt(hot), ALU.mult))
            link(V_.tensor_reduce(rc(i), rt(6), AX.X, ALU.add))
        for i, c in enumerate((8, 9, 6, 7)):
            for t in range(NT):
                n = NT * i + t
                if n:
                    dve.wait_ge(r_cnt_mm, 1 + n)
                V_.tensor_scalar(DG[:, :], ident[0:TT, 0:TT], RC[:, c, t:t + 1], None, ALU.mult).then_inc(diag_made, 1)
        dve.wait_ge(r_bce, 4)
        link(V_.tensor_copy(PJ[:, :], cn("part")))

        dve.wait_ge(items_known, 2)
        n_items = dve.value_load(NI[0:1, 0:1], min_val=1, max_val=MAXI)
        with dve.Fori(0, n_items) as j:
            ilink = linker(dve, item_step, j * (NT + 5))
            for t in range(NT):
                if t:
                    dve.wait_ge(i_sel, NT * j + t)
                ilink(V_.tensor_scalar(TS[:, :], cn("iota", TT), RC[:, 8, t:t + 1], None, ALU.is_equal))
                V_.scalar_tensor_tensor(out=SEL[:, t, :], in0=cn("iota", TT), scalar=RC[:, 9, t:t + 1], in1=TS[:, :],
                                        op0=ALU.is_equal, op1=ALU.add).then_inc(i_sel, 1)
            dve.wait_ge(i_sel, NT * j + NT)
            V_.tensor_scalar(RC[:, 8:10, :], RC[:, 8:10, :], -float(CAP), None, ALU.add)
            ilink(V_.scalar_tensor_tensor(out=T1[:, :], in0=G1[:, :], scalar=PJ[:, :], in1=W1[:, :],
                                          op0=ALU.is_equal, op1=ALU.mult))
            ilink(V_.scalar_tensor_tensor(out=T2[:, :], in0=G2[:, :], scalar=PJ[:, :], in1=W2[:, :],
                                          op0=ALU.is_equal, op1=ALU.mult))
            ilink(V_.tensor_scalar(PJ[:, :], PJ[:, :], float(CAP), None, ALU.add))
            ilink(V_.tensor_tensor(T1[:, :], T1[:, :], T2[:, :], ALU.add))
            ilink(V_.tensor_copy(SWH[:, :], T1[:, :]))
            V_.tensor_tensor(SWL[:, :], T1[:, :], SWH[:, :].bitcast(F32), ALU.subtract).then_inc(i_sw, 1)

            def split(c, u):
                split_low("moe", c, u, NC + j * NC + c + 1)

            split(0, 0)
            split(0, 1)
            for g in range(2):
                dve.wait_ge(i_g, 4 * j + 2 * g + 2)
                V_.tensor_copy(XL[:, 4 * g:4 * g + 4, :].rearrange("p k c -> p (k c)"), PS[:, 7, :]).then_inc(i_xl, 1)
            for c in range(NC + 1):
                if c + 1 < NC:
                    split(c + 1, 0)
                if c < NC:
                    w = CW[c]
                    dve.wait_ge(i_sg, NC * j + c + 1)
                    if c:
                        dve.wait_ge(i_t, NC * j + c)
                    V_.tensor_tensor(EA[:, 0:w], EG[:, 0:w], PS[:, c % RING, w:2 * w], ALU.mult).then_inc(i_a, 1)
                if c + 1 < NC:
                    split(c + 1, 1)
                if c >= 1:
                    w = CW[c - 1]
                    dve.wait_ge(i_ath, NC * j + c)
                    V_.tensor_tensor(ATL[(c - 1) % 2][:, 0:w // P, :].rearrange("p k c -> p (k c)"), PS[:, 3, 0:w],
                                     ATH[(c - 1) % 2][:, 0:w // P, :].rearrange("p k c -> p (k c)").bitcast(F32), ALU.subtract)\
                      .then_inc(i_atl, 1)
                    split(c - 1, 2)
            dve.wait_ge(i_yh, j + 1)
            V_.tensor_tensor(YL[:, :], PS[:, 4:6, :].rearrange("p b n -> p (b n)"), YH[:, :].bitcast(F32),
                             ALU.subtract).then_inc(i_yl, 1)
            for t in range(NT):
                for half in range(2):
                    n = 2 * t + half
                    cols = slice(half * 512, half * 512 + 512)
                    dve.wait_ge(i_o, 6 * j + n + 1)
                    V_.tensor_tensor(X[:, t, cols], X[:, t, cols], PS[0:TT, out_bank(n), :], ALU.add).then_inc(x_added, 1)
            assert ilink.n[0] == NT + 5
        dve.wait_ge(gain4_in, 16)
        norm(4, G[2][:, :])

    @block.tensor
    def _(pe):
        mm = nc.tensor.matmul

        def turn(n):
            for d in range(KD):
                for t in range(NT):
                    if d == 0:
                        pe.wait_ge(normed[n], t + 1)
                    ins = nc.tensor.transpose(PS[:, d, t * TT:(t + 1) * TT], HN[:, t, d * P:(d + 1) * P],
                                              ident[0:TT, 0:TT])
                ins.then_inc(turned[n], 1)

        def three(out, wh, wl, xh, xl, start, stop):
            mm(out, wh, xh, start=start, stop=False, skip_group_check=True)
            mm(out, wh, xl, start=False, stop=False, skip_group_check=True)
            return mm(out, wl, xh, start=False, stop=stop, skip_group_check=True)

        pe.wait_ge(consts_in, 16)
        pe.wait_ge(pool_in, 48)
        pe.wait_ge(normed[0], NT)
        pm = [cn("pm0", TT).rearrange("p (g t) -> p g t", g=4), cn("pm1", TT).rearrange("p (g t) -> p g t", g=4)]
        tail = cn("ptail", TT).rearrange("p (g t) -> p g t", g=4)
        state = cn("pstate", NB * BUF).rearrange("p (g t) -> p g t", g=4)
        for d in range(KD):
            g, cols = d // 2, slice(d * P, (d + 1) * P)
            for t in range(NT):
                mm(PS[:, d, t * TT:(t + 1) * TT], HN[:, t, cols], pm[min(t, 1)][:, g, :], start=(t == 0), stop=False,
                   skip_group_check=True)
            for t in range(NT - 1):
                mm(PS[:, d, (t + 1) * TT:(t + 1) * TT + 16], HN[:, t, cols], tail[:, g, :], start=False, stop=False,
                   skip_group_check=True)
            mm(PS[:, d, 0:SMP], ST[:, cols], state[:, g, :], start=False, stop=True,
               skip_group_check=True).then_inc(pool_mm, 1)
        pe.wait_ge(pool_act, KD // 2)
        pe.wait_ge(pool_dve, KD // 2)
        for t in range(NT):
            for half in range(2):
                for gg in range(2):
                    g = 2 * half + gg
                    for c in range(2):
                        ins = mm(PS[0:TT, 2 * t + half, gg * 256:(gg + 1) * 256], DT[:, 2 * g + c, t * TT:(t + 1) * TT],
                                 PW[:, 2 * g + c, :], start=(c == 0), stop=(c == 1))
                ins.then_inc(pool_y, 1)

        turn(1)
        pe.wait_ge(turned_act[1], KD)
        pe.wait_ge(turned_dve[1], KD)
        pe.wait_ge(x_pooled, NT)
        for i in range(6):
            ins = mm(PS[0:TT, 2 + i, :], ZB[0:1, 0:TT], ZB[0:1, 0:512], start=True, stop=False, skip_group_check=True)
        ins.then_inc(down_mm, 2)

        def ff_tile(q, j, c):
            return 2 * q + j if CW[c] == 256 else 20 + (c - 10)

        def dense_step(c, q):
            w = CW[c]
            uh = [UH[u][:, 0:KD * w].rearrange("p (k g f) -> p k g f", g=2, f=P) for u in range(2)]
            ul = [UL[u][:, 0:KD * w].rearrange("p (k g f) -> p k g f", g=2, f=P) for u in range(2)]
            if w == 256:
                for j in range(2):
                    tile = ff_tile(q, j, c)
                    pe.wait_ge(unit_low[j], q + 1)
                    if j:
                        pe.wait_ge(act_made, tile)
                    for g in range(2):
                        for k in range(KD):
                            ins = three(PS[:, g, 0:T], uh[j][:, k, g, :], ul[j][:, k, g, :], HTH[:, k, :], HTL[:, k, :],
                                        k == 0, k == KD - 1)
                        if g == 0:
                            ins.then_inc(gate_mm, 1)
                        else:
                            ins.then_inc(up_mm, 1)
            else:
                tile = ff_tile(q, 0, c)
                pe.wait_ge(act_made, tile)
                for u in range(2):
                    pe.wait_ge(unit_low[u], q + 1)
                    for g in range(2):
                        for k in range(KD // 2):
                            kk = u * KD // 2 + k
                            ins = three(PS[:, g, 0:T], uh[u][:, k, g, :], ul[u][:, k, g, :], HTH[:, kk, :], HTL[:, kk, :],
                                        kk == 0, kk == KD - 1)
                        if u == 1:
                            ins.then_inc(gate_mm if g == 0 else up_mm, 1)
                        elif g == 1:
                            ins.then_inc(unit_used[0], 1)
            pe.wait_ge(unit_low[2], q + 1)
            for j in range(w // P):
                tile = ff_tile(q, j, c)
                half = j if w == 256 else c % 2
                pe.wait_ge(act_low, tile + 1)
                for t in range(NT):
                    for n in range(2):
                        cols = slice(j * D + n * 512, j * D + n * 512 + 512)
                        ins = three(PS[0:TT, 2 + 2 * t + n, :], AH[:, half, t * TT:(t + 1) * TT],
                                    AL[:, half, t * TT:(t + 1) * TT], UH[2][:, cols], UL[2][:, cols], False, False)
                ins.then_inc(down_mm, 1)

        with pe.Fori(0, 3) as r:
            for i in range(RING):
                dense_step(i, r * RING + i)
        for c in range(9, NC):
            dense_step(c, c)

        pe.wait_ge(x_dense, NT)
        turn(2)
        pe.wait_ge(turned_act[2], KD // 2)
        pe.wait_ge(turned_dve[2], KD // 2)
        pe.wait_ge(win_in, 16)
        for t in range(NT):
            for lo, hi in ((0, 512), (512, PROJ)):
                for k in range(KD):
                    ins = mm(PS[0:TT, 2 * t + lo // 512, 0:hi - lo], HT[:, k, t * TT:(t + 1) * TT], WIN[:, k, lo:hi],
                             start=(k == 0), stop=(k == KD - 1))
                ins.then_inc(proj_mm, 1)
        pe.wait_ge(latent_ready, NT)
        pe.wait_ge(cq_ready, NT)
        for n in range(6):
            rows = QH if n == 5 else P
            for t in range(NT):
                src = PR[:, t, n * P:(n + 1) * P] if n < 3 else KVN[:, t, (n - 3) * P:(n - 2) * P] if n < 5 \
                    else KVN[:, t, KV - QH:KV]
                ins = nc.tensor.transpose(PS[0:rows, n, t * TT:(t + 1) * TT], src, ident[0:TT, 0:TT])
            ins.then_inc(lat_t, 1)
        pe.wait_ge(wuq_in, 16)
        pe.wait_ge(lat_e, 6)
        for t in range(NT):
            for i in range(3):
                n = 3 * t + i
                if n >= 8:
                    pe.wait_ge(q_ev, 1)
                for k in range(3):
                    ins = mm(PS[0:TT, q_bank(t, i), :], CQT[:, k, t * TT:(t + 1) * TT], WUQ[:, k, i * 512:(i + 1) * 512],
                             start=(k == 0), stop=(k == 2))
                ins.then_inc(q_mm, 1)
        pe.wait_ge(q_rot, NT)
        for h in range(H):
            if h >= 8:
                pe.wait_ge(qt_dve if h % 2 == 0 else qt_act, (h - 8) // 2 + 1)
            for t in range(NT):
                ins = nc.tensor.transpose(PS[0:QH, h % 8, t * TT:(t + 1) * TT], Q[:, t, h * QH:(h + 1) * QH],
                                          ident[0:TT, 0:TT])
            ins.then_inc(qt_t, 1)
        pe.wait_ge(qt_dve, H // 2)
        pe.wait_ge(qt_act, H // 2)
        pe.wait_ge(wuk_in, 16)
        for h in range(H):
            if h >= 4:
                pe.wait_ge(k_ev, h - 3)
            for c in range(2):
                ins = mm(PS[0:NOPE, h % 4, 0:TP], WUK[:, c, h * NOPE:(h + 1) * NOPE], CKT[:, c, SMP:T],
                         start=(c == 0), stop=(c == 1))
            ins.then_inc(k_mm, 1)
        pe.wait_ge(wuv_in, 16)
        for i, (p0, rows) in enumerate(QT):
            for half in range(2):
                n = 2 * i + half
                if n >= 2:
                    pe.wait_ge(v_ev, n - 1)
                for c in range(2):
                    ins = mm(PS[0:rows, 6 + half, :], CKT[:, c, SMP + p0:SMP + p0 + rows],
                             WUV[:, c, half * 512:(half + 1) * 512], start=(c == 0), stop=(c == 1))
                ins.then_inc(v_mm, 1)
        for n in range(2 * H):
            h, c = n // 2, n % 2
            if n % 4 == 0 and n >= 8:
                pe.wait_ge(uk_ev, n - 4)
            nc.tensor.transpose(PS[0:NOPE, 4 + n // 4 % 2, (n % 4) * P:(n % 4 + 1) * P],
                                WUK[:, c, h * NOPE:(h + 1) * NOPE], ident).then_inc(uk_t, 1)
        pe.wait_ge(uk_ev, 2 * H)
        pe.wait_ge(k_ev, H)
        for n in range(4):
            c, g = n // 2, n % 2
            for hh in range(8):
                h = 8 * g + hh
                ins = mm(PS[:, n, hh * SMP:(hh + 1) * SMP], UKT[:, h, c * P:(c + 1) * P], QTR[0:NOPE, h, 0:SMP],
                         start=True, stop=True)
            ins.then_inc(ql_mm, 1)
        pe.wait_ge(ql_ev, 4)
        pe.wait_ge(v_ev, 6)
        pe.wait_ge(kpe_copied, H)

        def scores(n):
            h, i = n // 3, n % 3
            p0, rows = QT[i]
            if n >= 2:
                pe.wait_ge(s_nm, n - 1)
            mm(PS[0:rows, n % 2, 0:p0 + rows], QTR[:, h, SMP + p0:SMP + p0 + rows], KT[:, h, 0:p0 + rows],
               start=True, stop=True).then_inc(s_mm, 1)

        scores(0)
        for h in range(H):
            for i, (p0, rows) in enumerate(QT):
                n = 3 * h + i
                if n + 1 < 3 * H:
                    scores(n + 1)
                pe.wait_ge(s_norm, n + 1)
                if n:
                    pe.wait_ge(s_ptc, n)
                for kb in range(i + 1):
                    k0, kr = QT[kb]
                    ins = nc.tensor.transpose(PS[0:kr, 2, kb * P:kb * P + rows], PP[n % 2][0:rows, k0:k0 + kr],
                                              ident[0:rows, 0:rows])
                ins.then_inc(s_pt, 1)
                pe.wait_ge(s_ptc, n + 1)
                lo = h % 2 * VH
                if h >= 2 and i == 0:
                    pe.wait_ge(s_oc, h - 1)
                for kb in range(i + 1):
                    kr = QT[kb][1]
                    ins = mm(PS[lo:lo + VH, 6 + h // 2 % 2, p0:p0 + rows], V[0:kr, kb, h * VH:(h + 1) * VH],
                             PPT[0:kr, kb, 0:rows], start=(kb == 0), stop=(kb == i))
                ins.then_inc(s_o, 1)
        pe.wait_ge(s_oc, H)
        pe.wait_ge(knew_in, 16 * NB)
        for b in range(NB):
            pe.wait_ge(cache_in[b % 2], 16 * 2 * NPG * (b // 2 + 1))
            for g in range(6):
                part, half = g // 2, g % 2
                if b == 0 and g < 2:
                    pass
                elif g < 2:
                    pe.wait_ge(d_ptc_act if g == 0 else d_ptc_dve, b if g == 0 else 2 * b)
                else:
                    pe.wait_ge(d_cte_dve if g % 2 == 0 else d_cte_act, 3 * b + g // 2)
                c0 = (0, P, KV - QH)[part]
                rows = QH if part == 2 else P
                for i in range(4):
                    ins = nc.tensor.transpose(PS[0:rows, 3 + (6 * b + g) % 2, i * P:(i + 1) * P],
                                              CC[b % 2][:, 4 * half + i, c0:c0 + rows], ident)
                ins.then_inc(d_ct, 1)
            pe.wait_ge(d_cte_act, 3 * b + 3)
            pe.wait_ge(d_cte_dve, 3 * b + 3)
            if b:
                pe.wait_ge(d_exp, 2 * b)
            for n in range(3):
                width = 512 if n < 2 else NS
                for c in range(2):
                    keys = CT[:, c, n * 512:(n + 1) * 512] if n < 2 else CKT[:, c, b * NS:(b + 1) * NS]
                    mm(PS[:, n, 0:width], QLT[:, c, b, :], keys, start=(c == 0), stop=False)
                keys = CT[NOPE:QH, 2, n * 512:(n + 1) * 512] if n < 2 else KPT[NOPE:QH, b * NS:(b + 1) * NS]
                ins = mm(PS[:, n, 0:width], QPT[NOPE:QH, b, :], keys, start=False, stop=True)
            ins.then_inc(d_s, 1)
            pe.wait_ge(d_exp, 2 * b + 2)
            for n in range(2):
                for i in range(4):
                    ins = nc.tensor.transpose(PS[:, 3 + n, i * P:(i + 1) * P], PD[:, (4 * n + i) * P:(4 * n + i + 1) * P],
                                              ident)
                ins.then_inc(d_pt, 1)
            nc.tensor.transpose(PS[0:NS, 7, 0:P], PD[:, PAST:PAST + NS], ident).then_inc(d_pt, 1)
            pe.wait_ge(d_ptc_act, b + 1)
            pe.wait_ge(d_ptc_dve, 2 * b + 2)
            if b:
                pe.wait_ge(d_ol, b)
            for i in range(NPG):
                mm(PS[:, 5, 0:KL], PDT[:, i, :], CC[b % 2][:, i, 0:KL], start=(i == 0), stop=False)
            mm(PS[:, 5, 0:KL], PDT[0:NS, NPG, :], KNEW[:, b, :], start=False, stop=True).then_inc(d_o, 1)
            pe.wait_ge(d_ol, b + 1)
            if b:
                pe.wait_ge(d_olc, b)
            for c in range(2):
                ins = nc.tensor.transpose(PS[:, 6, c * P:(c + 1) * P], OL[:, c * P:(c + 1) * P], ident)
            ins.then_inc(d_olt, 1)
        pe.wait_ge(d_olc, NB)
        for h in range(H):
            lo = h % 2 * VH
            for c in range(2):
                ins = mm(PS[lo:lo + VH, h // 8, (h // 2 % 4) * SMP:(h // 2 % 4 + 1) * SMP],
                         WUV[:, c, h * VH:(h + 1) * VH], OLT[:, c, h, :], start=(c == 0), stop=(c == 1),
                         skip_group_check=True)
            if h % 8 == 7:
                ins.then_inc(do_mm, 1)
        pe.wait_ge(do_ev, 2)
        pe.wait_ge(wo_in, 16)
        for t in range(NT):
            for half in range(2):
                for k in range(KD):
                    ins = mm(PS[0:TT, 2 + 2 * t + half, :], OT[:, k, t * TT:(t + 1) * TT],
                             WO[:, k, half * 512:(half + 1) * 512], start=(k == 0), stop=(k == KD - 1))
                ins.then_inc(wo_mm, 1)

        pe.wait_ge(x_mixed, NT)
        turn(3)
        pe.wait_ge(turned_act[3], KD // 2)
        pe.wait_ge(turned_dve[3], KD // 2)
        pe.wait_ge(router_in, 32)
        for t in range(NT):
            for k in range(KD):
                ins = mm(PS[0:TT, 0, t * NE:(t + 1) * NE], HT[:, k, t * TT:(t + 1) * TT], WR[:, k, :],
                         start=(k == 0), stop=(k == KD - 1))
        ins.then_inc(r_mm, 1)
        pe.wait_ge(diag_made, 1)
        for t in range(NT):
            for s in range(t + 1):
                mm(PS[0:TT, 1, t * NE:(t + 1) * NE], ONE[:, 0:TT] if s < t else cn("upper", TT), RT[:, 8, s, :],
                   start=(s == 0), stop=(s == t))
        for s in range(NT):
            ins = mm(PS[:, 2, 0:NE], ONE[:, :], RT[:, 8, s, :], start=(s == 0), stop=(s == NT - 1))
        ins.then_inc(r_cnt_mm, 1)
        for i in range(4):
            for t in range(NT):
                pe.wait_ge(diag_made, 2 + NT * i + t)
                mm(PS[:, 4 + i, t * TT:(t + 1) * TT], ONE[:, :], DG[:, :], start=True, stop=True).then_inc(r_cnt_mm, 1)

        pe.wait_ge(r_bce, 4)
        pe.wait_ge(hn_low, NT)
        pe.wait_ge(items_known, 2)
        n_items = pe.value_load(NI[0:1, 0:1], min_val=1, max_val=MAXI)
        with pe.Fori(0, n_items) as j:
            pe.wait_ge(i_sel, NT * j + NT)
            for g in range(2):
                for part, src in ((0, HNH), (1, HNL)):
                    if g == 1:
                        pe.wait_ge(i_xh if part == 0 else i_xl, 2 * j + 1)
                    for d in range(4):
                        for t in range(NT):
                            ins = mm(PS[:, 6 + part, d * CAP:(d + 1) * CAP],
                                     src[:, t, (4 * g + d) * P:(4 * g + d + 1) * P], SEL[:, t, :],
                                     start=(t == 0), stop=(t == NT - 1), skip_group_check=True)
                    ins.then_inc(i_g, 1)
            pe.wait_ge(i_xh, 2 * j + 2)
            pe.wait_ge(i_xl, 2 * j + 2)
            for n in range(2):
                mm(PS[:, 4 + n, :], ZB[0:1, 0:P], ZB[0:1, 0:512], start=True, stop=False, skip_group_check=True)
            for c in range(NC + 2):
                if c < NC:
                    w = CW[c]
                    if c >= RING:
                        pe.wait_ge(i_a, NC * j + c - RING + 1)
                    for u in range(2):
                        pe.wait_ge(unit_low[u], NC + NC * j + c + 1)
                        for k in range(KD // 2):
                            kk = u * KD // 2 + k
                            cols = slice(k * 2 * w, (k + 1) * 2 * w)
                            ins = three(PS[:, c % RING, 0:2 * w], XH[:, kk, :], XL[:, kk, :], UH[u][:, cols],
                                        UL[u][:, cols], kk == 0, kk == KD - 1)
                        if u == 0 and kk == KD // 2 - 1:
                            ins.then_inc(unit_used[0], 1)
                    ins.then_inc(i_gu, 1)
                if 1 <= c <= NC:
                    w = CW[c - 1]
                    pe.wait_ge(i_a, NC * j + c)
                    if c >= 2:
                        pe.wait_ge(i_atl, NC * j + c - 1)
                    for i in range(w // P):
                        ins = nc.tensor.transpose(PS[:, 3, i * P:(i + 1) * P], EA[:, i * P:(i + 1) * P], ident)
                    ins.then_inc(i_t, 1)
                if c >= 2:
                    w = CW[c - 2]
                    pe.wait_ge(i_atl, NC * j + c - 1)
                    pe.wait_ge(unit_low[2], NC + NC * j + c - 1)
                    for i in range(w // P):
                        for n in range(2):
                            cols = slice(i * D + n * 512, i * D + n * 512 + 512)
                            ins = three(PS[:, 4 + n, :], ATH[c % 2][:, i, :], ATL[c % 2][:, i, :], UH[2][:, cols], UL[2][:, cols],
                                        False, False)
                    ins.then_inc(unit_used[2], 1)
            pe.wait_ge(i_yl, j + 1)
            pe.wait_ge(i_sw, j + 1)
            for t in range(NT):
                for half in range(2):
                    n = 2 * t + half
                    if n >= 2:
                        pe.wait_ge(x_added, 6 * j + n - 1)
                    cols = slice(half * 512, half * 512 + 512)
                    three(PS[0:TT, out_bank(n), :], SWH[:, t * TT:(t + 1) * TT], SWL[:, t * TT:(t + 1) * TT],
                          YH[:, cols], YL[:, cols], True, True).then_inc(i_o, 1)

    ctx.close()


def q_bank(t, i):
    return (3 * t + i) % 8


def out_bank(n):
    return 6 + n % 2


_INS = ["x_prompt", "x_sample", "cache_ckv", "cache_kpe", "state_pool", "page_table", "meta_tokens",
        "g_mix", "g_ffn", "g_final", "pool_w", "pool_scale",
        "mla_w_in", "mla_g_q", "mla_g_kv", "mla_w_uq", "mla_w_uk", "mla_w_uv", "mla_w_o",
        "ffn_w_gate", "ffn_w_up", "ffn_w_down",
        "moe_w_router", "moe_b_router", "moe_w_gate", "moe_w_up", "moe_w_down"]
_OUTS = [("y_prompt", (1, SEQ, D)), ("y_sample", (NB, NS, D)),
         ("ckv_prompt", (1, 1, TP, KL)), ("kpe_prompt", (1, 1, TP, ROPE)), ("pool_prompt", (1, 1, BUF, D)),
         ("ckv_sample", (1, NB, NS, KL)), ("kpe_sample", (1, NB, NS, ROPE)), ("pool_sample", (1, NB, BUF, D))]


def kernel(**inputs):
    import concourse.bacc as bacc
    from concourse.bass_utils import run_bass_kernel_spmd as run

    nc = bacc.Bacc("TRN2", target_bir_lowering=False, num_devices=1)
    arrays, a, o = {}, {}, {}
    table, pooling = shape_constants()
    for name in _INS + ["consts", "consts_pool"]:
        x = table if name == "consts" else pooling if name == "consts_pool" else np.ascontiguousarray(inputs[name])
        arrays[f"in_{name}"] = x
        a[name] = nc.dram_tensor(f"in_{name}", x.shape, mybir.dt.from_np(x.dtype), kind="ExternalInput").ap()
    for name, shape in _OUTS:
        o[name] = nc.dram_tensor(f"out_{name}", shape, F32, kind="ExternalOutput").ap()
    program(nc, a, o)
    r = run(nc, [arrays], core_ids=[0])
    return tuple(r.results[0][f"out_{name}"] for name, _ in _OUTS)
```

```python
from contextlib import ExitStack

import numpy as np

import concourse.bass as bass
from concourse import mybir

F32 = mybir.dt.float32
F32R = mybir.dt.float32r
BF16 = mybir.dt.bfloat16
I32 = mybir.dt.int32
ALU = mybir.AluOpType
ACT = mybir.ActivationFunctionType
AX = mybir.AxisListType

P = 128
D = 1024
KD = D // P
SEQ, META, NB, NS = 256, 16, 8, 8
SMP = NB * NS
TP = SEQ + META
T = SMP + TP
NT = 3
TT = T // NT
WINDOWS = (2, 4, 8, 16)
BUF = 15
EPS = 1e-6
H = 16
QL, KL, NOPE, ROPE, VH = 384, 256, 64, 32, 64
HALF = ROPE // 2
QH = NOPE + ROPE
KV = KL + ROPE
PROJ = QL + KL + ROPE
PAST, PAGE = 1024, 128
NPG = PAST // PAGE
SCALE = float(QH) ** -0.5
FF = 2816
NE = 8
CAP = 128
MAXI = 2 * T // CAP + NE
NEG = -1e30
LOW = -3e38

CW = 256
NC = FF // CW
UNIT = KD * CW
RING_D = 3
UNITS = [u for c in range(NC + 2) for u in ([(c, 0), (c, 1)] if c < NC else []) + ([(c - 2, 2)] if c >= 2 else [])]
NU = len(UNITS)
RING = 11
HIGH = 3
assert NC * CW == FF and NU == 3 * NC and NU % RING == 0 and NU % HIGH == 0 and 3 * RING_D <= RING

QT = [(0, 16), (16, 128), (144, 128)]

_W = [("ident", 128), ("upper", TT), ("iota", 128), ("part", 1), ("mask", TP), ("maskd", NS),
      ("cos", NT * HALF), ("sin", NT * HALF), ("eidx", NE), ("items", MAXI)]
_WP = [("pm0", 4 * TT), ("pm1", 4 * TT), ("ptail", 4 * 16), ("pstate", 4 * SMP)]
COL, NCOL, NPOOL = {}, 0, 0
for _k, _w in _W:
    COL[_k] = (NCOL, NCOL + _w)
    NCOL += _w
for _k, _w in _WP:
    COL[_k] = (NPOOL, NPOOL + _w)
    NPOOL += _w


def shape_constants():
    c, pooling = np.zeros((P, NCOL), np.float32), np.zeros((P, NPOOL), np.float32)

    def put(name, a):
        (pooling if name[0] == "p" and name != "part" else c)[:a.shape[0], COL[name][0]:COL[name][1]] = a.reshape(a.shape[0], -1)

    put("ident", np.eye(P))
    put("upper", np.triu(np.ones((TT, TT)), 1))
    put("iota", np.tile(np.arange(P), (P, 1)))
    put("part", np.arange(P)[:, None])
    r = np.arange(P)[:, None]
    put("mask", np.where(np.arange(TP)[None] <= 144 + r, 0.0, NEG))
    put("maskd", np.where(np.arange(NS)[None] <= r % NS, 0.0, NEG))
    pos = np.concatenate([np.tile(PAST + np.arange(NS), NB), np.arange(TP)]).astype(np.float32)
    freqs = (np.float32(1) / np.float32(10000.0) ** (np.arange(HALF, dtype=np.float32) * np.float32(2.0 / ROPE))).astype(np.float32)
    ang = (pos[:, None] * freqs[None]).astype(np.float32).reshape(NT, TT, HALF).swapaxes(0, 1)
    put("cos", np.cos(ang))
    put("sin", np.sin(ang))
    put("eidx", np.tile(np.arange(NE), (P, 1)))
    put("items", np.tile(np.arange(MAXI), (P, 1)))
    def band(a, b, w):
        n = np.minimum(b[None] + 1, w)
        return ((a[:, None] <= b[None]) & (a[:, None] > b[None] - w)) / n - (a[:, None] == b[None])
    m0, m1 = np.zeros((2, TT, 4, TT))
    tail, state = np.zeros((TT, 4, 16)), np.zeros((NB * BUF, 4, SMP))
    first = TT - SMP
    for g, w in enumerate(WINDOWS):
        m0[SMP:, g, SMP:] = band(np.arange(first), np.arange(first), w)
        s = np.arange(NS)
        one = ((s[:, None] <= s[None]) & (s[:, None] > s[None] - w)) / w - (s[:, None] == s[None])
        old = (np.arange(BUF)[:, None] - BUF > s[None] - w) / w
        for b in range(NB):
            m0[b * NS:(b + 1) * NS, g, b * NS:(b + 1) * NS] = one
            state[b * BUF:(b + 1) * BUF, g, b * NS:(b + 1) * NS] = old
        q = first + np.arange(TT)
        m1[:, g] = band(q, q, w)
        tail[:, g] = band(q, q[-1] + 1 + np.arange(16), w)
    tail[:SMP] = 0.0
    put("pm0", m0)
    put("pm1", m1)
    put("ptail", tail)
    put("pstate", state)
    return c, pooling


def program(nc, a, o):
    ctx = ExitStack()

    top = [16640]

    def place(name, shape, dtype, off=None):
        n = 4 * int(np.prod(shape[1:]))
        if off is None:
            off = top[0]
            top[0] += (n + 31) // 32 * 32
        return nc.alloc_sbuf_tensor_at(name, shape, dtype, offset=off)

    X = place("X", [TT, NT, D], F32)
    H_OFF = top[0]
    HN = place("HN", [TT, NT, D], F32)
    HT_OFF = top[0]
    HT = place("HT", [P, KD, T], F32)
    CN = place("CN", [P, NCOL], F32)
    SCR_OFF = top[0]
    SCR = place("SCR", [P, D], F32)
    G_OFF = top[0]
    G = [place(f"G{i}", [TT, D], F32) for i in range(3)]
    GQ = place("GQ", [TT, QL], F32)
    GKV = place("GKV", [TT, KL], F32)
    SS = place("SS", [TT, 32], F32)
    RS = place("RS", [TT, 32], F32)
    ZB = place("ZB", [1, 512], BF16)
    RPS = [place(f"RPS{i}", [P, 4], F32) for i in range(2)]
    DS = place("DS", [P, 8], F32)
    DM = place("DM", [P, NS], F32)
    NHALF = place("NHALF", [TT, 2], F32)
    A = top[0]
    END = nc.sbuf_usable_end

    def area():
        cur = [A]

        def get(name, shape, dtype=F32, off=None):
            if off is not None:
                return place(name, shape, dtype, off)
            n = (4 * int(np.prod(shape[1:])) + 31) // 32 * 32
            t = place(name, shape, dtype, cur[0])
            cur[0] += n
            assert cur[0] <= END, (name, cur[0] - END)
            return t
        get.cur = cur
        return get

    get = area()
    RAW = [get(f"RAW{i}", [P, UNIT]) for i in range(RING)]
    FFN_OFF = A
    UH = [get(f"UH{i}", [P, UNIT], F32R) for i in range(HIGH)]
    FFN_END = get.cur[0]
    LOW_ = [place(f"LOW{i}", [P, UNIT], F32R, FFN_OFF + i * 4 * UNIT) for i in range(RING)]
    PAIR = [place(f"PAIR{i}", [P, KD, 2, CW], F32, FFN_OFF + 3 * i * 4 * UNIT) for i in range(RING_D)]
    LOWPAIR = [place(f"LOWPAIR{i}", [P, KD, 2, CW], F32R, FFN_OFF + 3 * i * 4 * UNIT) for i in range(RING_D)]
    HTH = place("HTH", [P, KD, T], F32R, HT_OFF)
    HTL = get("HTL", [P, KD, T], F32R)
    SG = get("SG", [P, T])
    AF = get("AF", [P, T])
    AH = get("AH", [P, 2, T], F32R)
    AL = get("AL", [P, 2, T], F32R)
    get = area()
    get.cur[0] = FFN_END
    ST = get("ST", [NB * BUF, D])
    PW = get("PW", [P, KD, 256])
    DT = place("DT", [P, KD, T], F32, HT_OFF)
    PTMP = get("PTMP", [TT, 512])
    CP = get("CP", [P, NPOOL])

    get = area()
    S1 = get.cur[0]
    WIN = get("WIN", [P, KD, PROJ])
    S2 = get.cur[0]
    Q = get("Q", [TT, NT, H * QH])
    S3 = get.cur[0]
    WUQ = get("WUQ", [P, 3, H * QH])
    S5 = get.cur[0]
    QTR = get("QTR", [QH, H, T])
    S6 = get.cur[0]
    KT = get("KT", [QH, H, TP])
    S7 = get.cur[0]
    UKT = get("UKT", [NOPE, H, KL])
    QLT = get("QLT", [P, 2, NB, H * NS])
    QPT = get("QPT", [QH, NB, H * NS])
    WUV = get("WUV", [P, 2, H * VH])
    S11 = get.cur[0]
    WUK = get("WUK", [P, 2, H * NOPE])
    KVN = get("KVN", [TT, NT, KV])
    CKT = get("CKT", [P, 2, T])
    KPT = get("KPT", [QH, T])
    PR = place("PR", [TT, NT, PROJ], F32, H_OFF)
    CQT = place("CQT", [P, 3, T], F32, H_OFF + 8064)
    OT = place("OT", [P, KD, T], F32, HT_OFF)
    CC = [place(f"CC{i}", [P, NPG, KV], F32, S1 + i * 9216) for i in range(2)]
    V = place("V", [P, 3, H * VH], F32, S2)
    PP = [place(f"PP{i}", [P, TP], F32, S2 + 12288 + i * 1088) for i in range(2)]
    PPT = place("PPT", [P, 3, P], F32, S2 + 12288 + 2176)
    CT = place("CT", [P, 3, PAST], F32, S3)
    KNEW = place("KNEW", [NS, NB, KL], F32, S7)
    WO = place("WO", [P, KD, D], F32, S5)
    PD = place("PD", [P, PAST + NS], F32, H_OFF)
    PDT = place("PDT", [P, NPG + 1, P], F32, H_OFF + 4128)
    OL = place("OL", [P, KL], F32, H_OFF + 8736)
    OLT = place("OLT", [P, 2, H, SMP], F32, S11)
    QR = place("QR", [TT, 4, H, HALF], F32, SCR_OFF)
    KR = place("KR", [TT, 4, HALF], F32, SCR_OFF + 2048)

    get = area()
    get.cur[0] = FFN_END
    HNH = get("HNH", [TT, NT, D], F32R)
    HNL = get("HNL", [TT, NT, D], F32R)
    EG = get("EG", [P, 256])
    XH = place("XH", [P, KD, CAP], F32R, H_OFF)
    XL = place("XL", [P, KD, CAP], F32R, H_OFF + 4096)
    EA = place("EA", [P, 256], F32, H_OFF + 8192)
    ATH = [place("ATH0", [P, 2, CAP], F32R, H_OFF + 9216), place("ATH1", [P, 2, CAP], F32R, HT_OFF + 9600)]
    ATL = [place("ATL0", [P, 2, CAP], F32R, H_OFF + 10240), get("ATL1", [P, 2, CAP], F32R)]
    YH = place("YH", [P, D], F32R, G_OFF)
    YL = place("YL", [P, D], F32R, G_OFF + 4096)
    SEL = place("SEL", [TT, NT, CAP], F32R, HT_OFF)
    G1 = place("G1", [P, T], F32, HT_OFF + 1536)
    G2 = place("G2", [P, T], F32, HT_OFF + 2880)
    W1 = place("W1", [P, T], F32, HT_OFF + 4224)
    W2 = place("W2", [P, T], F32, HT_OFF + 5568)
    SWH = place("SWH", [P, T], F32R, HT_OFF + 6912)
    SWL = place("SWL", [P, T], F32R, HT_OFF + 8256)
    T1 = place("T1", [P, T], F32, SCR_OFF)
    T2 = place("T2", [P, T], F32, SCR_OFF + 1344)
    TS = place("TS", [TT, CAP], F32, SCR_OFF + 2688)
    WR = get("WR", [P, KD, NE])
    BR = get("BR", [TT, NE])
    RT = place("RT", [TT, 10, NT, NE], F32, G_OFF)
    RC = get("RC", [TT, 12, NT])
    TO = place("TO", [P, 6, NE], F32, G_OFF + 1024)
    IE = place("IE", [1, MAXI, NE], F32, G_OFF + 1216)
    EF = place("EF", [1, MAXI], F32, G_OFF + 1664)
    DG = place("DG", [TT, TT], F32, G_OFF + 1728)
    ONE = place("ONE", [TT, P], F32, G_OFF + 2176)
    EI = get("EI", [1, MAXI], I32)
    NI = get("NI", [1, 2], I32)
    PJ = get("PJ", [P, 1])

    PS = ctx.enter_context(nc.psum_tensor("PS", [P, 8, 512], F32))

    def sem(name):
        return ctx.enter_context(nc.semaphore(name))

    def cn(name, rows=P):
        return (CP if name in dict(_WP) else CN)[0:rows, COL[name][0]:COL[name][1]]

    ident = cn("ident")

    x_in, consts_in, gains_in = sem("x_in"), sem("consts_in"), sem("gains_in")
    gain1_in, gain4_in, smallgains_in = sem("gain1_in"), sem("gain4_in"), sem("smallgains_in")
    gain3_in = sem("gain3_in")
    pool_in = sem("pool_in")
    gu_in = [sem(f"gu_in{i}") for i in range(RING_D)]
    dn_in = [sem(f"dn_in{i}") for i in range(RING_D)]
    raw_in = [sem(f"raw_in{i}") for i in range(RING)]
    unit_high, unit_low, unit_used = sem("unit_high"), sem("unit_low"), sem("unit_used")
    win_in, wuq_in, wuk_in, wuv_in, wo_in = (sem(n) for n in ("win_in", "wuq_in", "wuk_in", "wuv_in", "wo_in"))
    cache_in = [sem("cache_in0"), sem("cache_in1")]
    pages_in, knew_in, router_in = sem("pages_in"), sem("knew_in"), sem("router_in")
    squares = [sem(f"squares{i}") for i in range(5)]
    normed = [sem(f"normed{i}") for i in range(5)]
    turned = [sem(f"turned{i}") for i in range(4)]
    turned_act = [sem(f"turned_act{i}") for i in range(4)]
    turned_dve = [sem(f"turned_dve{i}") for i in range(4)]
    pool_mm, pool_act, pool_dve, pool_y, pool_out = (sem(n) for n in ("pool_mm", "pool_act", "pool_dve", "pool_y", "pool_out"))
    x_pooled, x_dense, x_mixed, x_added = (sem(n) for n in ("x_pooled", "x_dense", "x_mixed", "x_added"))
    gate_mm, silu_done, act_made, act_high, act_low = (
        sem(n) for n in ("gate_mm", "silu_done", "act_made", "act_high", "act_low"))
    stored = sem("stored")
    dve_step = sem("dve_step")
    act_step = sem("act_step")
    inverse_root, inverse_root_qk = [sem(f"inverse_root{i}") for i in range(5)], sem("inverse_root_qk")
    pool_step = sem("pool_step")

    block = ctx.enter_context(nc.Block())

    def linker(eng, s, base=0):
        n = [0]

        def link(ins):
            n[0] += 1
            ins.then_inc(s, 1)
            eng.wait_ge(s, base + n[0])
        link.n = n
        return link

    proj_mm, proj_out = sem("proj_mm"), sem("proj_out")
    sq_q = sem("sq_q")
    latent_ready, cq_ready = sem("latent_ready"), sem("cq_ready")
    lat_t, lat_e = sem("lat_t"), sem("lat_e")
    q_mm, q_ev, q_rot, qt_t, qt_act, qt_dve = (sem(n) for n in ("q_mm", "q_ev", "q_rot", "qt_t", "qt_act", "qt_dve"))
    k_mm, k_ev, kpe_copied, v_mm, v_ev, uk_t, uk_ev, ql_mm, ql_ev, qp_copied = (
        sem(n) for n in ("k_mm", "k_ev", "kpe_copied", "v_mm", "v_ev", "uk_t", "uk_ev", "ql_mm", "ql_ev", "qp_copied"))
    s_mm, s_nm, s_exp, s_norm, s_pt, s_ptc, s_o, s_oc = (
        sem(n) for n in ("s_mm", "s_nm", "s_exp", "s_norm", "s_pt", "s_ptc", "s_o", "s_oc"))
    d_ct, d_cte_act, d_cte_dve, d_s, d_nm, d_exp, d_rs, d_pt, d_ptc_act, d_ptc_dve, d_o, d_ol, d_olt, d_olc = (
        sem(n) for n in ("d_ct", "d_cte_act", "d_cte_dve", "d_s", "d_nm", "d_exp", "d_rs", "d_pt", "d_ptc_act",
                         "d_ptc_dve", "d_o", "d_ol", "d_olt", "d_olc"))
    do_mm, do_ev, wo_mm = sem("do_mm"), sem("do_ev"), sem("wo_mm")
    r_mm, r_cnt_mm, r_dve, r_act, r_bce, items_known = (
        sem(n) for n in ("r_mm", "r_cnt_mm", "r_dve", "r_act", "r_bce", "items_known"))
    hn_high, hn_low = sem("hn_high"), sem("hn_low")
    i_sel, i_g, i_x, i_sg, i_a, i_t, i_ath, i_atl, i_yh, i_yl, i_sw, i_o = (
        sem(n) for n in ("i_sel", "i_g", "i_x", "i_sg", "i_a", "i_t", "i_ath", "i_atl", "i_yh", "i_yl", "i_sw", "i_o"))
    item_step = sem("item_step")
    diag_made = sem("diag_made")

    def load_dense(sp, c, slot):
        cols = slice(c * CW, (c + 1) * CW)
        if c >= RING_D:
            sp.wait_ge(unit_used, 3 * (c - RING_D) + 2)
        for g, w in enumerate(("ffn_w_gate", "ffn_w_up")):
            sp.dma_start(PAIR[slot][:, :, g, :], a[w][0, :, cols].rearrange("(k p) f -> p k f", p=P)).then_inc(gu_in[slot], 16)
        if c >= RING_D:
            sp.wait_ge(unit_used, 3 * (c - RING_D) + 3)
        sp.dma_start(RAW[3 * slot + 2][:, :].rearrange("p (j d) -> p j d", d=D),
                     a["ffn_w_down"][0, cols, :].rearrange("(j p) d -> p j d", p=P)).then_inc(dn_in[slot], 16)

    def load_unit(sp, e, n):
        (c, u), slot = UNITS[n], n % RING
        cols, one = slice(c * CW, (c + 1) * CW), bass.ds(e, 1)
        if u == 2:
            to = RAW[slot][:, :].rearrange("p (h d) -> p h d", h=2)
            for h in range(2):
                sp.dma_start(to[:, h:h + 1, :], a["moe_w_down"][0, one, c * CW + h * P:c * CW + (h + 1) * P, :]
                             .rearrange("e p d -> p e d")).then_inc(raw_in[slot], 16)
        else:
            to = RAW[slot][:, :].rearrange("p (k g f) -> p k g f", g=2, f=CW)
            for g, w in enumerate(("moe_w_gate", "moe_w_up")):
                sp.dma_start(to[:, :, g, :], a[w][0, one, u * (D // 2):(u + 1) * (D // 2), cols]
                             .rearrange("e (k p) f -> p (e k) f", p=P)).then_inc(raw_in[slot], 16)

    def dense_low(c, u):
        slot = c % RING_D
        return LOW_[3 * slot + 2][:, :] if u == 2 else LOWPAIR[slot][:, :, :, u * P:(u + 1) * P]

    def dense_raw(c, u):
        slot = c % RING_D
        return RAW[3 * slot + 2][:, :] if u == 2 else PAIR[slot][:, :, :, u * P:(u + 1) * P]

    def dense_high(u):
        return UH[2][:, :] if u == 2 else UH[u][:, :].rearrange("p (k g f) -> p k g f", g=2, f=P)

    @block.sync
    def _(sp):
        sp.dma_start(X[0:SMP, 0, :], a["x_sample"].rearrange("b s d -> (b s) d")).then_inc(x_in, 16)
        sp.dma_start(X[SMP:SMP + META, 0, :], a["meta_tokens"]).then_inc(x_in, 16)
        sp.dma_start(X[SMP + META:TT, 0, :], a["x_prompt"][0, 0:TT - SMP - META, :]).then_inc(x_in, 16)
        for t in (1, 2):
            r = t * TT - SMP - META
            sp.dma_start(X[:, t, :], a["x_prompt"][0, r:r + TT, :]).then_inc(x_in, 16)
        sp.dma_start(G[0][:, :], a["g_mix"][0:1, :].partition_broadcast(TT)).then_inc(gains_in, 16)
        sp.dma_start(CN[:, :], a["consts"]).then_inc(consts_in, 16)
        sp.dma_start(CP[:, :], a["consts_pool"]).then_inc(pool_in, 16)
        sp.dma_start(ST[:, :], a["state_pool"][0].rearrange("b n d -> (b n) d")).then_inc(pool_in, 16)
        sp.dma_start(PW[:, :, :], a["pool_w"][0].rearrange("g (c p) n -> p (g c) n", p=P)).then_inc(pool_in, 16)
        sp.dma_start(G[1][:, :], a["pool_scale"][0:1, :].partition_broadcast(TT)).then_inc(gains_in, 16)
        sp.dma_start(G[2][:, :], a["g_ffn"][0:1, :].partition_broadcast(TT)).then_inc(gains_in, 16)
        sp.dma_start(GQ[:, :], a["mla_g_q"][0:1, :].partition_broadcast(TT)).then_inc(smallgains_in, 16)
        sp.dma_start(GKV[:, :], a["mla_g_kv"][0:1, :].partition_broadcast(TT)).then_inc(smallgains_in, 16)
        for c in range(RING_D):
            load_dense(sp, c, c)
        sp.wait_ge(x_pooled, NT)
        sp.dma_start(G[0][:, :], a["g_mix"][1:2, :].partition_broadcast(TT)).then_inc(gain1_in, 16)
        for c in range(RING_D, NC):
            load_dense(sp, c, c % RING_D)
        sp.wait_ge(unit_used, NU)
        sp.dma_start(WIN[:, :, :], a["mla_w_in"][0].rearrange("(k p) n -> p k n", p=P)).then_inc(win_in, 16)
        sp.dma_start(WUQ[:, :, :], a["mla_w_uq"][0].rearrange("(k p) n -> p k n", p=P)).then_inc(wuq_in, 16)
        sp.wait_ge(x_dense, NT)
        sp.dma_start(G[2][:, :], a["g_ffn"][1:2, :].partition_broadcast(TT)).then_inc(gain3_in, 16)
        sp.dma_start(WUK[:, :, :], a["mla_w_uk"][0].rearrange("(c p) h n -> p c (h n)", p=P)).then_inc(wuk_in, 16)
        sp.dma_start(WUV[:, :, :], a["mla_w_uv"][0].rearrange("(c p) h v -> p c (h v)", p=P)).then_inc(wuv_in, 16)

        nphys = a["cache_ckv"].shape[1]

        def load_cache(b):
            with sp.Fori(0, NPG) as i:
                page = sp.value_load(a["page_table"][b:b + 1, bass.ds(i, 1)], min_val=0, max_val=nphys - 1)
                one, to = bass.ds(page, 1), bass.ds(i, 1)
                sp.dma_start(CC[b % 2][:, to, 0:KL], a["cache_ckv"][0, one, :, :].rearrange("e p c -> p e c"))\
                  .then_inc(cache_in[b % 2], 16)
                sp.dma_start(CC[b % 2][:, to, KL:KV], a["cache_kpe"][0, one, :, :].rearrange("e p c -> p e c"))\
                  .then_inc(cache_in[b % 2], 16)

        sp.wait_ge(proj_mm, 2 * NT)
        for b in range(2):
            load_cache(b)
        sp.wait_ge(uk_ev, H * 2)
        sp.wait_ge(ql_ev, 2 * 2)
        for b in range(NB):
            sp.dma_start(KNEW[:, b, :], KVN[b * NS:(b + 1) * NS, 0, 0:KL]).then_inc(knew_in, 16)
        sp.wait_ge(s_oc, H)
        sp.wait_ge(qp_copied, 1)
        sp.dma_start(WO[:, :, :], a["mla_w_o"][0].rearrange("(k p) n -> p k n", p=P)).then_inc(wo_in, 16)
        for b in range(2, NB):
            sp.wait_ge(d_o, b - 1)
            load_cache(b)
        sp.wait_ge(wo_mm, 2 * NT)
        sp.dma_start(WR[:, :, :], a["moe_w_router"][0].rearrange("(k p) n -> p k n", p=P)).then_inc(router_in, 16)
        sp.dma_start(BR[:, :], a["moe_b_router"][0:1, :].partition_broadcast(TT)).then_inc(router_in, 16)
        for n in range(RING):
            load_unit(sp, 0, n)
        sp.wait_ge(normed[3], NT)
        sp.dma_start(G[2][:, :], a["g_final"].rearrange("(a d) -> a d", a=1).partition_broadcast(TT)).then_inc(gain4_in, 16)

        def load_rest(e, j):
            for n in range(RING, NU):
                sp.wait_ge(unit_used, NU * (j + 1) + n - RING + 1)
                load_unit(sp, e, n)

        sp.wait_ge(items_known, 2)
        before_last = sp.value_load(NI[0:1, 1:2], min_val=1, max_val=MAXI - 1)
        with sp.Fori(0, before_last) as j:
            e = sp.value_load(EI[0:1, bass.ds(j, 1)], min_val=0, max_val=NE - 1)
            e_next = sp.value_load(EI[0:1, 1:MAXI][:, bass.ds(j, 1)], min_val=0, max_val=NE - 1)
            load_rest(e, j)
            for n in range(RING):
                sp.wait_ge(unit_used, NU * (j + 2) + n - RING + 1)
                load_unit(sp, e_next, n)
        e = sp.value_load(EI[0:1, bass.ds(before_last, 1)], min_val=0, max_val=NE - 1)
        load_rest(e, before_last)

    @block.gpsimd
    def _(pool):
        count = [0]

        def store(dst, src):
            count[0] += 16
            pool.dma_start(dst, src).then_inc(stored, 16)

        nc.gpsimd.memset(NHALF[:, :], -0.5).then_inc(pool_step, 1)
        pool.wait_ge(pool_step, 1)
        steps = [1]

        def inverse_roots(i, step, width, done):
            cols = slice(i, i + step * (width - 1) + 1, step)
            steps[0] += 1
            nc.gpsimd.tensor_scalar(RS[:, cols], SS[:, cols], EPS, None, ALU.add).then_inc(pool_step, 1)
            pool.wait_ge(pool_step, steps[0])
            nc.gpsimd.tensor_tensor(RS[:, cols], RS[:, cols], NHALF[:, 0:width], ALU.pow).then_inc(done, 1)

        def roots_of(n):
            for t in range(NT):
                pool.wait_ge(squares[n], t + 1)
                inverse_roots(3 * n + t, 1, 1, inverse_root[n])

        roots_of(0)
        pool.wait_ge(normed[0], NT)
        pool.dma_start(o["pool_prompt"][0, 0], HN[TT - BUF:TT, 2, :]).then_inc(pool_out, 16)
        for b in range(NB):
            pool.dma_start(o["pool_sample"][0, b, BUF - NS:BUF, :], HN[b * NS:(b + 1) * NS, 0, :]).then_inc(pool_out, 16)
            pool.dma_start(o["pool_sample"][0, b, 0:BUF - NS, :], a["state_pool"][0, b, NS:BUF, :]).then_inc(pool_out, 16)
        roots_of(1)
        roots_of(2)
        for t in range(NT):
            pool.wait_ge(sq_q, 2 * t + 2)
            inverse_roots(15 + t, 3, 2, inverse_root_qk)
        pool.wait_ge(latent_ready, NT)
        store(o["ckv_sample"][0].rearrange("b s c -> (b s) c"), KVN[0:SMP, 0, 0:KL])
        store(o["kpe_sample"][0].rearrange("b s c -> (b s) c"), KVN[0:SMP, 0, KL:KV])
        for t in range(NT):
            p0 = SMP if t == 0 else 0
            r0 = t * TT + p0 - SMP
            store(o["ckv_prompt"][0, 0, r0:r0 + TT - p0, :], KVN[p0:TT, t, 0:KL])
            store(o["kpe_prompt"][0, 0, r0:r0 + TT - p0, :], KVN[p0:TT, t, KL:KV])
        pool.wait_ge(lat_e, 6)
        for h in range(H):
            nc.gpsimd.tensor_copy(KT[NOPE:QH, h, :], KPT[NOPE:QH, SMP:T]).then_inc(kpe_copied, 1)
        roots_of(3)
        roots_of(4)
        pool.wait_ge(normed[4], NT)
        store(o["y_sample"].rearrange("b s d -> (b s) d"), HN[0:SMP, 0, :])
        store(o["y_prompt"][0, 0:TT - SMP - META, :], HN[SMP + META:TT, 0, :])
        for t in (1, 2):
            r = t * TT - SMP - META
            store(o["y_prompt"][0, r:r + TT, :], HN[:, t, :])
        pool.wait_ge(stored, count[0])
        pool.wait_ge(pool_out, 16 * (1 + 2 * NB))

    @block.scalar
    def _(act):
        link = linker(act, act_step)

        def squares_of(n, ready):
            for t in range(NT):
                ready(t)
                if t:
                    act.wait_ge(squares[n], t)
                nc.scalar.activation(SCR[0:TT, :], X[:, t, :], ACT.Square, scale=1 / 32,
                                     accum_out=SS[:, 3 * n + t:3 * n + t + 1]).then_inc(squares[n], 1)

        def turn_out(n, dst):
            for d in range(1, KD, 2):
                act.wait_ge(turned[n], d + 1)
                nc.scalar.copy(dst[:, d, :], PS[:, d, 0:T]).then_inc(turned_act[n], 1)

        def split_high(dst, src, n, loaded, count):
            act.wait_ge(loaded, count)
            if not (isinstance(n, int) and n < HIGH):
                act.wait_ge(unit_used, n - HIGH + 1)
            nc.scalar.copy(dst, src).then_inc(unit_high, 1)

        squares_of(0, lambda t: act.wait_ge(x_in, 16 * 5))
        for d in range(1, KD, 2):
            act.wait_ge(pool_mm, d + 1)
            nc.scalar.copy(DT[:, d, :], PS[:, d, 0:T]).then_inc(pool_act, 1)
        squares_of(1, lambda t: act.wait_ge(x_pooled, t + 1))
        for u in range(3):
            split_high(dense_high(u), dense_raw(0, u), u, dn_in[0] if u == 2 else gu_in[0], 16 if u == 2 else 32)
        for d in range(KD):
            act.wait_ge(turned[1], d + 1)
            nc.scalar.copy(HTH[:, d, :], PS[:, d, 0:T]).then_inc(turned_act[1], 1)

        def dense_step(c, q, fills, last):
            nxt = (c + 1) % RING_D
            for j in range(2):
                tile = 2 * q + j
                act.wait_ge(gate_mm, tile + 1)
                nc.scalar.activation(SG[:, :], PS[:, 0, 0:T], ACT.Silu).then_inc(silu_done, 1)
                act.wait_ge(act_made, tile + 1)
                nc.scalar.copy(AH[:, j, :], AF[:, :]).then_inc(act_high, 1)
                if not last:
                    split_high(dense_high(j), dense_raw(nxt, j), 3 * (q + 1) + j, gu_in[nxt], fills * 32)
            if not last:
                split_high(dense_high(2), dense_raw(nxt, 2), 3 * (q + 1) + 2, dn_in[nxt], fills * 16)

        with act.Fori(0, NC // RING_D) as r:
            for i in range(RING_D):
                dense_step(i, r * RING_D + i, r + 1 + (i + 1) // RING_D, False)
        for c in range(NC // RING_D * RING_D, NC):
            dense_step(c % RING_D, c, (c + 1) // RING_D + 1, c == NC - 1)
        squares_of(2, lambda t: act.wait_ge(x_dense, t + 1))
        turn_out(2, HT)

        for t in range(NT):
            act.wait_ge(proj_mm, 2 * t + 1)
            link(nc.scalar.copy(PR[:, t, 0:512], PS[0:TT, 2 * t, :]))
            act.wait_ge(proj_mm, 2 * t + 2)
            nc.scalar.copy(PR[:, t, 512:PROJ], PS[0:TT, 2 * t + 1, 0:PROJ - 512]).then_inc(proj_out, 1)
            act.wait_ge(proj_out, t + 1)
            if t:
                act.wait_ge(sq_q, 2 * t)
            nc.scalar.activation(SCR[0:TT, 0:QL], PR[:, t, 0:QL], ACT.Square, scale=float(QL) ** -0.5,
                                 accum_out=SS[:, 15 + t:16 + t]).then_inc(sq_q, 1)
            act.wait_ge(sq_q, 2 * t + 1)
            nc.scalar.activation(SCR[0:TT, 0:KL], PR[:, t, QL:QL + KL], ACT.Square, scale=1 / 16,
                                 accum_out=SS[:, 18 + t:19 + t]).then_inc(sq_q, 1)
        for t in range(NT):
            for i in range(2):
                act.wait_ge(q_mm, 3 * t + i + 1)
                nc.scalar.copy(Q[:, t, i * 512:(i + 1) * 512], PS[0:TT, q_bank(t, i), :]).then_inc(q_ev, 1)
        for h in range(1, H, 2):
            act.wait_ge(qt_t, h + 1)
            nc.scalar.copy(QTR[:, h, :], PS[0:QH, h % 8, 0:T]).then_inc(qt_act, 1)
        for h in range(H):
            act.wait_ge(k_mm, h + 1)
            nc.scalar.copy(KT[0:NOPE, h, :], PS[0:NOPE, h % 4, 0:TP]).then_inc(k_ev, 1)
        for h in range(H):
            for c in range(2):
                n = 2 * h + c
                if n % 4 == 3:
                    act.wait_ge(uk_t, n + 1)
                    src = PS[0:NOPE, 4 + n // 4 % 2, :].rearrange("p (i x) -> p i x", i=2)
                    nc.scalar.copy(UKT[:, h - 1:h + 1, :], src).then_inc(uk_ev, 4)
        for h in range(H):
            for i, (p0, rows) in enumerate(QT):
                n = 3 * h + i
                keys = p0 + rows
                act.wait_ge(s_nm, n + 1)
                nc.scalar.activation(PP[n % 2][0:rows, 0:keys], PP[n % 2][0:rows, 0:keys], ACT.Exp, scale=SCALE,
                                     bias=RPS[n % 2][0:rows, 1:2], accum_out=RPS[n % 2][0:rows, 2:3]).then_inc(s_exp, 1)
                act.wait_ge(s_pt, n + 1)
                if n >= 1:
                    act.wait_ge(s_o, n)
                if i:
                    nc.scalar.copy(PPT[:, 1:i + 1, 0:rows],
                                   PS[:, 2, P:(i + 1) * P].rearrange("p (b r) -> p b r", r=P)[:, :, 0:rows])
                nc.scalar.copy(PPT[0:QT[0][1], 0, 0:rows], PS[0:QT[0][1], 2, 0:rows]).then_inc(s_ptc, 1)
        for b in range(NB):
            for g in (1, 3, 5):
                act.wait_ge(d_ct, 6 * b + g + 1)
                if b:
                    act.wait_ge(d_s, b)
                part = g // 2
                lo, hi = (NOPE, QH) if part == 2 else (0, P)
                nc.scalar.copy(CT[lo:hi, part, 512:1024], PS[lo:hi, 3 + (6 * b + g) % 2, :]).then_inc(d_cte_act, 1)
            act.wait_ge(d_nm, b + 1)
            if b:
                act.wait_ge(d_pt, 3 * b)
            nc.scalar.activation(PD[:, 0:PAST], PS[:, 0:2, :].rearrange("p b n -> p (b n)"), ACT.Exp, scale=SCALE,
                                 bias=DS[:, 3:4], accum_out=DS[:, 4:5]).then_inc(d_exp, 1)
            nc.scalar.activation(PD[:, PAST:PAST + NS], DM[:, :], ACT.Exp, scale=SCALE,
                                 bias=DS[:, 3:4], accum_out=DS[:, 5:6]).then_inc(d_exp, 1)
            act.wait_ge(d_pt, 3 * b + 1)
            if b:
                act.wait_ge(d_o, b)
            nc.scalar.copy(PDT[:, 0:4, :].rearrange("p a q -> p (a q)"), PS[:, 3, :]).then_inc(d_ptc_act, 1)
            act.wait_ge(d_olt, b + 1)
            nc.scalar.copy(OLT[:, :, :, b * NS:(b + 1) * NS],
                           PS[:, 6, 0:2 * P].rearrange("p (c h s) -> p c h s", c=2, h=H)).then_inc(d_olc, 1)
        for g in range(2):
            act.wait_ge(do_mm, g + 1)
            nc.scalar.copy(OT[:, 4 * g:4 * g + 4, 0:SMP], PS[:, g, 0:4 * SMP].rearrange("p (k t) -> p k t", k=4)).then_inc(do_ev, 1)
        squares_of(3, lambda t: act.wait_ge(x_mixed, t + 1))
        turn_out(3, HT)
        for t in range(NT):
            act.wait_ge(normed[3], t + 1)
            nc.scalar.copy(HNH[:, t, :], HN[:, t, :]).then_inc(hn_high, 1)
        act.wait_ge(r_dve, 1)
        nc.scalar.activation(RC[:, 6:8, :], RC[:, 4:6, :], ACT.Exp).then_inc(r_act, 1)
        for i in range(4):
            act.wait_ge(r_cnt_mm, 1 + NT * (i + 1))
            nc.scalar.copy((G1, G2, W1, W2)[i][:, :], PS[:, 4 + i, 0:T]).then_inc(r_bce, 1)

        def tokens_in(m):
            for g in range(2):
                for part, dst in ((0, XH), (1, XL)):
                    act.wait_ge(i_g, 4 * m + 2 * g + part + 1)
                    nc.scalar.copy(dst[:, 4 * g:4 * g + 4, :].rearrange("p k c -> p (k c)"),
                                   PS[:, gather_bank(g, part), :]).then_inc(i_x, 1)

        def sums_out(used):
            act.wait_ge(unit_used, used)
            nc.scalar.copy(YH[:, :], PS[:, 4:6, :].rearrange("p b n -> p (b n)")).then_inc(i_yh, 1)

        act.wait_ge(items_known, 2)
        n_items = act.value_load(NI[0:1, 0:1], min_val=1, max_val=MAXI)
        tokens_in(0)
        with act.Fori(0, n_items) as j:
            def split(n):
                split_high(UH[n % HIGH][:, :], RAW[n % RING][:, :], NU * (j + 1) + n, raw_in[n % RING],
                           32 * (NU // RING * j + n // RING + 1))

            split(0)
            split(1)
            sums_out(NU * (j + 1))
            split(2)
            split(3)
            for c in range(NC):
                act.wait_ge(unit_used, NU * (j + 1) + UNITS.index((c, 1)) + 1)
                if c:
                    act.wait_ge(i_a, NC * j + c)
                nc.scalar.activation(EG[:, :], PS[:, c % 3, 0:CW], ACT.Silu).then_inc(i_sg, 1)
                if c >= 1:
                    act.wait_ge(i_t, NC * j + c)
                    nc.scalar.copy(ATH[(c - 1) % 2][:, :, :].rearrange("p k c -> p (k c)"), PS[:, 3, 0:CW]).then_inc(i_ath, 1)
                for n in splits_after(c):
                    split(n)
            tokens_in(j + 1)
            act.wait_ge(i_t, NC * j + NC)
            nc.scalar.copy(ATH[(NC - 1) % 2][:, :, :].rearrange("p k c -> p (k c)"), PS[:, 3, 0:CW]).then_inc(i_ath, 1)
        sums_out(NU * (n_items + 1))
        act.wait_ge(x_added, (n_items + 1) * (2 * NT))
        squares_of(4, lambda t: None)

    @block.vector
    def _(dve):
        link = linker(dve, dve_step)
        V_ = nc.vector

        link(V_.memset(ZB[:, :], 0.0))

        def norm(n, gain):
            for t in range(NT):
                i = 3 * n + t
                dve.wait_ge(inverse_root[n], t + 1)
                V_.scalar_tensor_tensor(out=HN[:, t, :], in0=X[:, t, :], scalar=RS[:, i:i + 1], in1=gain,
                                        op0=ALU.mult, op1=ALU.mult).then_inc(normed[n], 1)

        def turn_out(n, dst):
            for d in range(0, KD, 2):
                dve.wait_ge(turned[n], d + 1)
                V_.tensor_copy(dst[:, d, :], PS[:, d, 0:T]).then_inc(turned_dve[n], 1)

        def split_low(dst, src, high, n):
            dve.wait_ge(unit_high, n + 1)
            V_.tensor_tensor(dst, src, high.bitcast(F32), ALU.subtract).then_inc(unit_low, 1)

        dve.wait_ge(gains_in, 16 * 3)
        norm(0, G[0][:, :])
        for d in range(0, KD, 2):
            dve.wait_ge(pool_mm, d + 1)
            V_.tensor_copy(DT[:, d, :], PS[:, d, 0:T]).then_inc(pool_dve, 1)
        for t in range(NT):
            for half in range(2):
                dve.wait_ge(pool_y, 2 * t + half + 1)
                cols = slice(half * 512, half * 512 + 512)
                link(V_.tensor_tensor(PTMP[:, :], PS[0:TT, 2 * t + half, :], G[1][:, cols], ALU.mult))
                ins = V_.tensor_tensor(X[:, t, cols], X[:, t, cols], PTMP[:, :], ALU.add)
                if half == 0:
                    link(ins)
            ins.then_inc(x_pooled, 1)
            dve.wait_ge(x_pooled, t + 1)
        dve.wait_ge(pool_out, 16 * (1 + 2 * NB))
        norm(1, G[2][:, :])
        for u in range(3):
            split_low(dense_low(0, u), dense_raw(0, u), dense_high(u), u)
        for d in range(KD):
            dve.wait_ge(turned_act[1], d + 1)
            V_.tensor_tensor(HTL[:, d, :], PS[:, d, 0:T], HTH[:, d, :].bitcast(F32), ALU.subtract)\
              .then_inc(turned_dve[1], 1)

        def dense_step(c, q, last):
            nxt = (c + 1) % RING_D
            for j in range(2):
                tile = 2 * q + j
                dve.wait_ge(silu_done, tile + 1)
                dve.wait_ge(unit_used, 3 * q + j + 1)
                if j == 0:
                    dve.wait_ge(unit_low, 3 * q + 3)
                else:
                    dve.wait_ge(act_low, tile)
                V_.tensor_tensor(AF[:, :], SG[:, :], PS[:, 1, 0:T], ALU.mult).then_inc(act_made, 1)
                dve.wait_ge(act_high, tile + 1)
                V_.tensor_tensor(AL[:, j, :], AF[:, :], AH[:, j, :].bitcast(F32), ALU.subtract).then_inc(act_low, 1)
                if not last:
                    split_low(dense_low(nxt, j), dense_raw(nxt, j), dense_high(j), 3 * (q + 1) + j)
            if not last:
                split_low(dense_low(nxt, 2), dense_raw(nxt, 2), dense_high(2), 3 * (q + 1) + 2)

        with dve.Fori(0, NC // RING_D) as r:
            for i in range(RING_D):
                dense_step(i, r * RING_D + i, False)
        for c in range(NC // RING_D * RING_D, NC):
            dense_step(c % RING_D, c, c == NC - 1)
        dve.wait_ge(unit_used, NU)
        for t in range(NT):
            for half in range(2):
                cols = slice(half * 512, half * 512 + 512)
                ins = V_.tensor_tensor(X[:, t, cols], X[:, t, cols], PS[0:TT, 2 + 2 * t + half, :], ALU.add)
                if half == 0:
                    link(ins)
            ins.then_inc(x_dense, 1)
            dve.wait_ge(x_dense, t + 1)
        dve.wait_ge(gain1_in, 16)
        norm(2, G[0][:, :])
        turn_out(2, HT)

        dve.wait_ge(smallgains_in, 32)
        cos = cn("cos", TT).rearrange("p (t f) -> p t f", t=NT)
        sin = cn("sin", TT).rearrange("p (t f) -> p t f", t=NT)
        for t in range(NT):
            dve.wait_ge(inverse_root_qk, t + 1)
            dve.wait_ge(proj_out, t + 1)
            V_.scalar_tensor_tensor(out=PR[:, t, 0:QL], in0=PR[:, t, 0:QL], scalar=RS[:, 15 + t:16 + t],
                                    in1=GQ[:, :], op0=ALU.mult, op1=ALU.mult).then_inc(cq_ready, 1)
            V_.scalar_tensor_tensor(out=KVN[:, t, 0:KL], in0=PR[:, t, QL:QL + KL], scalar=RS[:, 18 + t:19 + t],
                                    in1=GKV[:, :], op0=ALU.mult, op1=ALU.mult)
            x1, x2 = PR[:, t, QL + KL:QL + KL + HALF], PR[:, t, QL + KL + HALF:PROJ]
            V_.tensor_tensor(KR[:, 0, :], x1, cos[:, t, :], ALU.mult)
            V_.tensor_tensor(KR[:, 1, :], x2, sin[:, t, :], ALU.mult)
            V_.tensor_tensor(KR[:, 2, :], x2, cos[:, t, :], ALU.mult)
            link(V_.tensor_tensor(KR[:, 3, :], x1, sin[:, t, :], ALU.mult))
            link(V_.tensor_tensor(KVN[:, t, KL:KL + HALF], KR[:, 0, :], KR[:, 1, :], ALU.subtract))
            V_.tensor_tensor(KVN[:, t, KL + HALF:KV], KR[:, 2, :], KR[:, 3, :], ALU.add).then_inc(latent_ready, 1)
            dve.wait_ge(latent_ready, t + 1)
        for n in range(6):
            dve.wait_ge(lat_t, n + 1)
            if n < 3:
                V_.tensor_copy(CQT[:, n, :], PS[:, n, 0:T]).then_inc(lat_e, 1)
            elif n < 5:
                V_.tensor_copy(CKT[:, n - 3, :], PS[:, n, 0:T]).then_inc(lat_e, 1)
            else:
                V_.tensor_copy(KPT[NOPE:QH, :], PS[NOPE:QH, n, 0:T]).then_inc(lat_e, 1)
        for t in range(NT):
            dve.wait_ge(q_mm, 3 * t + 3)
            link(V_.tensor_copy(Q[:, t, 1024:1536], PS[0:TT, q_bank(t, 2), :]))
            dve.wait_ge(q_ev, 2 * (t + 1))
            pe_part = Q[:, t, :].rearrange("p (h x) -> p h x", h=H)
            x1, x2 = pe_part[:, :, NOPE:NOPE + HALF], pe_part[:, :, NOPE + HALF:QH]
            c3 = cos[:, t:t + 1, :].to_broadcast([TT, H, HALF])
            s3 = sin[:, t:t + 1, :].to_broadcast([TT, H, HALF])
            V_.tensor_tensor(QR[:, 0], x1, c3, ALU.mult)
            V_.tensor_tensor(QR[:, 1], x2, s3, ALU.mult)
            V_.tensor_tensor(QR[:, 2], x2, c3, ALU.mult)
            link(V_.tensor_tensor(QR[:, 3], x1, s3, ALU.mult))
            V_.tensor_tensor(x1, QR[:, 0], QR[:, 1], ALU.subtract)
            ins = V_.tensor_tensor(x2, QR[:, 2], QR[:, 3], ALU.add)
            ins.then_inc(q_rot, 1)
            dve.wait_ge(q_rot, t + 1)
        for h in range(0, H, 2):
            dve.wait_ge(qt_t, h + 1)
            V_.tensor_copy(QTR[:, h, :], PS[0:QH, h % 8, 0:T]).then_inc(qt_dve, 1)
        dve.wait_ge(qt_dve, H // 2)
        dve.wait_ge(qt_act, H // 2)
        V_.tensor_copy(QPT[NOPE:QH, :, :].rearrange("p b (h s) -> p h b s", h=H),
                       QTR[NOPE:QH, :, 0:SMP].rearrange("p h (b s) -> p h b s", b=NB)).then_inc(qp_copied, 1)
        for i, (p0, rows) in enumerate(QT):
            for half in range(2):
                n = 2 * i + half
                dve.wait_ge(v_mm, n + 1)
                V_.tensor_copy(V[0:rows, i, half * 512:(half + 1) * 512], PS[0:rows, 6 + half, :]).then_inc(v_ev, 1)
        for n in range(4):
            c, g = n // 2, n % 2
            dve.wait_ge(ql_mm, n + 1)
            V_.tensor_copy(QLT[:, c, :, :].rearrange("p b (h s) -> p h b s", h=H)[:, 8 * g:8 * g + 8],
                           PS[:, n, :].rearrange("p (h b s) -> p h b s", h=8, b=NB)).then_inc(ql_ev, 1)
        for h in range(H):
            for i, (p0, rows) in enumerate(QT):
                n = 3 * h + i
                keys = p0 + rows
                st = RPS[n % 2]
                dve.wait_ge(s_mm, n + 1)
                if n >= 2:
                    dve.wait_ge(s_pt, n - 1)
                V_.tensor_tensor_reduce(PP[n % 2][0:rows, 0:keys], PS[0:rows, n % 2, 0:keys],
                                        cn("mask")[0:rows, 144 - p0:144 - p0 + keys], 1.0, LOW, ALU.add, ALU.max,
                                        st[0:rows, 0:1]).then_inc(dve_step, 1)
                link.n[0] += 1
                dve.wait_ge(dve_step, link.n[0])
                V_.tensor_scalar(st[0:rows, 1:2], st[0:rows, 0:1], -SCALE, None, ALU.mult).then_inc(s_nm, 1)
                dve.wait_ge(s_exp, n + 1)
                link(V_.reciprocal(st[0:rows, 3:4], st[0:rows, 2:3]))
                V_.tensor_scalar(PP[n % 2][0:rows, 0:keys], PP[n % 2][0:rows, 0:keys], st[0:rows, 3:4], None,
                                 ALU.mult).then_inc(s_norm, 1)
            lo = h % 2 * VH
            dve.wait_ge(s_o, 3 * h + 3)
            V_.tensor_copy(OT[lo:lo + VH, h // 2, SMP:T], PS[lo:lo + VH, 6 + h // 2 % 2, 0:TP]).then_inc(s_oc, 1)
        for b in range(NB):
            for g in (0, 2, 4):
                dve.wait_ge(d_ct, 6 * b + g + 1)
                if b:
                    dve.wait_ge(d_s, b)
                part = g // 2
                lo, hi = (NOPE, QH) if part == 2 else (0, P)
                V_.tensor_copy(CT[lo:hi, part, 0:512], PS[lo:hi, 3 + (6 * b + g) % 2, :]).then_inc(d_cte_dve, 1)
            dve.wait_ge(d_s, b + 1)
            if b:
                dve.wait_ge(d_exp, 2 * b)
            link(V_.tensor_tensor_reduce(DM[:, :], PS[:, 2, 0:NS], cn("maskd"), 1.0, LOW, ALU.add, ALU.max, DS[:, 0:1]))
            link(V_.tensor_reduce(DS[:, 1:2], PS[:, 0:2, :].rearrange("p b n -> p (b n)"), AX.X, ALU.max))
            link(V_.tensor_tensor(DS[:, 2:3], DS[:, 0:1], DS[:, 1:2], ALU.max))
            V_.tensor_scalar(DS[:, 3:4], DS[:, 2:3], -SCALE, None, ALU.mult).then_inc(d_nm, 1)
            dve.wait_ge(d_exp, 2 * b + 2)
            link(V_.tensor_tensor(DS[:, 6:7], DS[:, 4:5], DS[:, 5:6], ALU.add))
            link(V_.reciprocal(DS[:, 7:8], DS[:, 6:7]))
            if b:
                dve.wait_ge(d_o, b)
            dve.wait_ge(d_pt, 3 * b + 2)
            V_.tensor_copy(PDT[:, 4:8, :].rearrange("p a q -> p (a q)"), PS[:, 4, :]).then_inc(d_ptc_dve, 1)
            dve.wait_ge(d_pt, 3 * b + 3)
            V_.tensor_copy(PDT[0:NS, 8, :], PS[0:NS, 7, 0:P]).then_inc(d_ptc_dve, 1)
            dve.wait_ge(d_o, b + 1)
            if b:
                dve.wait_ge(d_olt, b)
            V_.tensor_scalar(OL[:, :], PS[:, 5, 0:KL], DS[:, 7:8], None, ALU.mult).then_inc(d_ol, 1)
        for t in range(NT):
            for half in range(2):
                cols = slice(half * 512, half * 512 + 512)
                dve.wait_ge(wo_mm, 2 * t + half + 1)
                ins = V_.tensor_tensor(X[:, t, cols], X[:, t, cols], PS[0:TT, 2 + 2 * t + half, :], ALU.add)
                if half == 0:
                    link(ins)
            ins.then_inc(x_mixed, 1)
            dve.wait_ge(x_mixed, t + 1)
        dve.wait_ge(gain3_in, 16)
        norm(3, G[2][:, :])
        turn_out(3, HT)
        dve.wait_ge(stored, 16 * (2 + 2 * NT))
        for t in range(NT):
            dve.wait_ge(hn_high, t + 1)
            V_.tensor_tensor(HNL[:, t, :], HN[:, t, :], HNH[:, t, :].bitcast(F32), ALU.subtract).then_inc(hn_low, 1)

        def rt(i):
            return RT[:, i, :, :]

        def rc(i):
            return RC[:, i, :]

        def wide(x):
            return x.unsqueeze(2).to_broadcast([TT, NT, NE])

        eidx = cn("eidx", TT).unsqueeze(1).to_broadcast([TT, NT, NE])
        link(V_.memset(ONE[:, :], 1.0))
        dve.wait_ge(r_mm, 1)
        link(V_.tensor_copy(rt(0), PS[0:TT, 0, 0:NT * NE].rearrange("p (t e) -> p t e", t=NT)))
        dve.wait_ge(router_in, 32)
        link(V_.tensor_tensor(rt(1), rt(0), BR[:, :].unsqueeze(1).to_broadcast([TT, NT, NE]), ALU.add))

        def one_hot_of_max(src, dst, c):
            link(V_.tensor_reduce(rc(c), src, AX.X, ALU.max))
            link(V_.tensor_tensor(rt(6), src, wide(rc(c)), ALU.is_equal))
            link(V_.tensor_scalar(rt(6), rt(6), -float(NE), float(NE), ALU.mult, ALU.add))
            link(V_.tensor_tensor(rt(6), rt(6), eidx, ALU.add))
            link(V_.tensor_reduce(rc(c + 1), rt(6), AX.X, ALU.min))
            link(V_.tensor_tensor(dst, eidx, wide(rc(c + 1)), ALU.is_equal))

        one_hot_of_max(rt(1), rt(3), 0)
        link(V_.scalar_tensor_tensor(out=rt(4), in0=rt(3), scalar=LOW, in1=rt(1), op0=ALU.mult, op1=ALU.add))
        one_hot_of_max(rt(4), rt(5), 2)
        for i, hot in ((8, 3), (9, 5)):
            link(V_.tensor_tensor(rt(6), rt(0), rt(hot), ALU.mult))
            link(V_.tensor_reduce(rc(i), rt(6), AX.X, ALU.add))
        link(V_.tensor_tensor(rc(10), rc(8), rc(9), ALU.max))
        link(V_.tensor_tensor(rc(4), rc(8), rc(10), ALU.subtract))
        V_.tensor_tensor(rc(5), rc(9), rc(10), ALU.subtract).then_inc(r_dve, 1)
        V_.tensor_tensor(rt(8), rt(3), rt(5), ALU.add).then_inc(diag_made, 1)
        dve.wait_ge(r_act, 1)
        link(V_.tensor_tensor(rc(10), rc(6), rc(7), ALU.add))
        link(V_.reciprocal(rc(11), rc(10)))
        link(V_.tensor_tensor(rc(6), rc(6), rc(11), ALU.mult))
        link(V_.tensor_tensor(rc(7), rc(7), rc(11), ALU.mult))
        dve.wait_ge(r_cnt_mm, 1)
        link(V_.tensor_copy(rt(9), PS[0:TT, 1, 0:NT * NE].rearrange("p (t e) -> p t e", t=NT)))
        link(V_.tensor_copy(TO[:, 0, :], PS[:, 2, 0:NE]))
        link(V_.tensor_scalar(TO[:, 1, :], TO[:, 0, :], 0.0, None, ALU.is_gt))
        for m in range(1, NT):
            link(V_.scalar_tensor_tensor(out=TO[:, 1, :], in0=TO[:, 0, :], scalar=float(m * CAP), in1=TO[:, 1, :],
                                         op0=ALU.is_gt, op1=ALU.add))
        link(V_.tensor_scalar(TO[:, 1, 0:1], TO[:, 1, 0:1], 1.0, None, ALU.max))
        link(V_.tensor_copy(TO[:, 2, :], TO[:, 1, :]))
        for e in range(1, NE):
            link(V_.tensor_tensor(TO[:, 2, e:e + 1], TO[:, 2, e:e + 1], TO[:, 2, e - 1:e], ALU.add))
        link(V_.tensor_tensor(TO[:, 3, :], TO[:, 2, :], TO[:, 1, :], ALU.subtract))
        V_.tensor_scalar(NI[0:1, 1:2], TO[0:1, 2, NE - 1:NE], -1.0, None, ALU.add)
        V_.tensor_copy(NI[0:1, 0:1], TO[0:1, 2, NE - 1:NE]).then_inc(items_known, 1)
        link(V_.tensor_tensor(IE[:, :, :], CN[0:1, COL["items"][0]:COL["items"][1]].unsqueeze(2).to_broadcast([1, MAXI, NE]),
                              TO[0:1, 2:3, :].to_broadcast([1, MAXI, NE]), ALU.is_ge))
        link(V_.tensor_reduce(EF[:, :], IE[:, :, :], AX.X, ALU.add))
        V_.tensor_scalar(EI[:, :], EF[:, :], float(NE - 1), None, ALU.min).then_inc(items_known, 1)
        link(V_.tensor_scalar(TO[:, 4, :], TO[:, 3, :], float(CAP), None, ALU.mult))
        link(V_.tensor_tensor(rt(9), rt(9), TO[0:TT, 4:5, :].to_broadcast([TT, NT, NE]), ALU.add))
        for i, hot in ((8, 3), (9, 5)):
            link(V_.tensor_tensor(rt(6), rt(9), rt(hot), ALU.mult))
            link(V_.tensor_reduce(rc(i), rt(6), AX.X, ALU.add))
        for i, c in enumerate((8, 9, 6, 7)):
            for t in range(NT):
                n = NT * i + t
                if n:
                    dve.wait_ge(r_cnt_mm, 1 + n)
                V_.tensor_scalar(DG[:, :], ident[0:TT, 0:TT], RC[:, c, t:t + 1], None, ALU.mult).then_inc(diag_made, 1)
        dve.wait_ge(r_bce, 4)
        link(V_.tensor_copy(PJ[:, :], cn("part")))

        def select(lk, m):
            for t in range(NT):
                if not (isinstance(m, int) and t == 0):
                    dve.wait_ge(i_sel, NT * m + t)
                lk(V_.tensor_scalar(TS[:, :], cn("iota", TT), RC[:, 8, t:t + 1], None, ALU.is_equal))
                V_.scalar_tensor_tensor(out=SEL[:, t, :], in0=cn("iota", TT), scalar=RC[:, 9, t:t + 1], in1=TS[:, :],
                                        op0=ALU.is_equal, op1=ALU.add).then_inc(i_sel, 1)
            dve.wait_ge(i_sel, NT * m + NT)
            lk(V_.tensor_scalar(RC[:, 8:10, :], RC[:, 8:10, :], -float(CAP), None, ALU.add))

        def way_back(lk):
            lk(V_.scalar_tensor_tensor(out=T1[:, :], in0=G1[:, :], scalar=PJ[:, :], in1=W1[:, :],
                                       op0=ALU.is_equal, op1=ALU.mult))
            lk(V_.scalar_tensor_tensor(out=T2[:, :], in0=G2[:, :], scalar=PJ[:, :], in1=W2[:, :],
                                       op0=ALU.is_equal, op1=ALU.mult))
            lk(V_.tensor_scalar(PJ[:, :], PJ[:, :], float(CAP), None, ALU.add))
            lk(V_.tensor_tensor(T1[:, :], T1[:, :], T2[:, :], ALU.add))
            lk(V_.tensor_copy(SWH[:, :], T1[:, :]))
            V_.tensor_tensor(SWL[:, :], T1[:, :], SWH[:, :].bitcast(F32), ALU.subtract).then_inc(i_sw, 1)

        def sums_low(m):
            dve.wait_ge(i_yh, m + 1)
            V_.tensor_tensor(YL[:, :], PS[:, 4:6, :].rearrange("p b n -> p (b n)"), YH[:, :].bitcast(F32),
                             ALU.subtract).then_inc(i_yl, 1)

        def add_outputs(m):
            for t in range(NT):
                for half in range(2):
                    n = 2 * t + half
                    cols = slice(half * 512, half * 512 + 512)
                    dve.wait_ge(i_o, 6 * m + n + 1)
                    V_.tensor_tensor(X[:, t, cols], X[:, t, cols], PS[0:TT, out_bank(n), :], ALU.add).then_inc(x_added, 1)

        def act_low_part(c, j):
            dve.wait_ge(i_ath, NC * j + c + 1)
            V_.tensor_tensor(ATL[c % 2][:, :, :].rearrange("p k c -> p (k c)"), PS[:, 3, 0:CW],
                             ATH[c % 2][:, :, :].rearrange("p k c -> p (k c)").bitcast(F32), ALU.subtract).then_inc(i_atl, 1)

        select(link, 0)
        V_.tensor_scalar(SWH[:, :], W1[:, :], 0.0, None, ALU.mult)
        V_.tensor_scalar(SWL[:, :], W1[:, :], 0.0, None, ALU.mult).then_inc(i_sw, 1)
        dve.wait_ge(items_known, 2)
        n_items = dve.value_load(NI[0:1, 0:1], min_val=1, max_val=MAXI)
        with dve.Fori(0, n_items) as j:
            ilink = linker(dve, item_step, j * (NT + 6))

            def split(n):
                split_low(LOW_[n % RING][:, :], RAW[n % RING][:, :], UH[n % HIGH][:, :], NU * (j + 1) + n)

            split(0)
            split(1)
            sums_low(j)
            split(2)
            split(3)
            for c in range(NC):
                dve.wait_ge(i_sg, NC * j + c + 1)
                if c:
                    dve.wait_ge(i_t, NC * j + c)
                V_.tensor_tensor(EA[:, :], EG[:, :], PS[:, c % 3, CW:2 * CW], ALU.mult).then_inc(i_a, 1)
                if c >= 1:
                    act_low_part(c - 1, j)
                if c == 1:
                    add_outputs(j)
                for n in splits_after(c):
                    split(n)
                if c == 4:
                    dve.wait_ge(x_added, 6 * j + 6)
                    way_back(ilink)
                if c == 6:
                    dve.wait_ge(i_g, 4 * j + 4)
                    select(ilink, j + 1)
            act_low_part(NC - 1, j)
            assert ilink.n[0] == NT + 6
        sums_low(n_items)
        add_outputs(n_items)
        dve.wait_ge(gain4_in, 16)
        norm(4, G[2][:, :])

    @block.tensor
    def _(pe):
        mm = nc.tensor.matmul

        def turn(n):
            for d in range(KD):
                for t in range(NT):
                    if d == 0:
                        pe.wait_ge(normed[n], t + 1)
                    ins = nc.tensor.transpose(PS[:, d, t * TT:(t + 1) * TT], HN[:, t, d * P:(d + 1) * P],
                                              ident[0:TT, 0:TT])
                ins.then_inc(turned[n], 1)

        def three(out, wh, wl, xh, xl, start, stop):
            mm(out, wh, xh, start=start, stop=False, skip_group_check=True)
            mm(out, wh, xl, start=False, stop=False, skip_group_check=True)
            return mm(out, wl, xh, start=False, stop=stop, skip_group_check=True)

        pe.wait_ge(consts_in, 16)
        pe.wait_ge(pool_in, 48)
        pe.wait_ge(normed[0], NT)
        pm = [cn("pm0", TT).rearrange("p (g t) -> p g t", g=4), cn("pm1", TT).rearrange("p (g t) -> p g t", g=4)]
        tail = cn("ptail", TT).rearrange("p (g t) -> p g t", g=4)
        state = cn("pstate", NB * BUF).rearrange("p (g t) -> p g t", g=4)
        for d in range(KD):
            g, cols = d // 2, slice(d * P, (d + 1) * P)
            for t in range(NT):
                mm(PS[:, d, t * TT:(t + 1) * TT], HN[:, t, cols], pm[min(t, 1)][:, g, :], start=(t == 0), stop=False,
                   skip_group_check=True)
            for t in range(NT - 1):
                mm(PS[:, d, (t + 1) * TT:(t + 1) * TT + 16], HN[:, t, cols], tail[:, g, :], start=False, stop=False,
                   skip_group_check=True)
            mm(PS[:, d, 0:SMP], ST[:, cols], state[:, g, :], start=False, stop=True,
               skip_group_check=True).then_inc(pool_mm, 1)
        pe.wait_ge(pool_act, KD // 2)
        pe.wait_ge(pool_dve, KD // 2)
        for t in range(NT):
            for half in range(2):
                for gg in range(2):
                    g = 2 * half + gg
                    for c in range(2):
                        ins = mm(PS[0:TT, 2 * t + half, gg * 256:(gg + 1) * 256], DT[:, 2 * g + c, t * TT:(t + 1) * TT],
                                 PW[:, 2 * g + c, :], start=(c == 0), stop=(c == 1))
                ins.then_inc(pool_y, 1)

        turn(1)
        pe.wait_ge(turned_act[1], KD)
        pe.wait_ge(turned_dve[1], KD)
        pe.wait_ge(x_pooled, NT)
        for i in range(6):
            mm(PS[0:TT, 2 + i, :], ZB[0:1, 0:TT], ZB[0:1, 0:512], start=True, stop=False, skip_group_check=True)

        def dense_step(c, q):
            for j in range(2):
                wh, wl = dense_high(j), dense_low(c, j)
                pe.wait_ge(unit_low, 3 * q + j + 1)
                for g in range(2):
                    for k in range(KD):
                        ins = three(PS[:, g, 0:T], wh[:, k, g, :], wl[:, k, g, :], HTH[:, k, :], HTL[:, k, :],
                                    k == 0, k == KD - 1)
                    ins.then_inc(gate_mm if g == 0 else unit_used, 1)
                pe.wait_ge(act_made, 2 * q + j + 1)
            wh, wl = dense_high(2), dense_low(c, 2)
            pe.wait_ge(unit_low, 3 * q + 3)
            for j in range(2):
                pe.wait_ge(act_low, 2 * q + j + 1)
                for t in range(NT):
                    for n in range(2):
                        cols = slice(j * D + n * 512, j * D + n * 512 + 512)
                        ins = three(PS[0:TT, 2 + 2 * t + n, :], AH[:, j, t * TT:(t + 1) * TT],
                                    AL[:, j, t * TT:(t + 1) * TT], wh[:, cols], wl[:, cols], False, False)
            ins.then_inc(unit_used, 1)

        with pe.Fori(0, NC // RING_D) as r:
            for i in range(RING_D):
                dense_step(i, r * RING_D + i)
        for c in range(NC // RING_D * RING_D, NC):
            dense_step(c % RING_D, c)

        pe.wait_ge(x_dense, NT)
        turn(2)
        pe.wait_ge(turned_act[2], KD // 2)
        pe.wait_ge(turned_dve[2], KD // 2)
        pe.wait_ge(win_in, 16)
        for t in range(NT):
            for lo, hi in ((0, 512), (512, PROJ)):
                for k in range(KD):
                    ins = mm(PS[0:TT, 2 * t + lo // 512, 0:hi - lo], HT[:, k, t * TT:(t + 1) * TT], WIN[:, k, lo:hi],
                             start=(k == 0), stop=(k == KD - 1))
                ins.then_inc(proj_mm, 1)
        pe.wait_ge(latent_ready, NT)
        pe.wait_ge(cq_ready, NT)
        for n in range(6):
            rows = QH if n == 5 else P
            for t in range(NT):
                src = PR[:, t, n * P:(n + 1) * P] if n < 3 else KVN[:, t, (n - 3) * P:(n - 2) * P] if n < 5 \
                    else KVN[:, t, KV - QH:KV]
                ins = nc.tensor.transpose(PS[0:rows, n, t * TT:(t + 1) * TT], src, ident[0:TT, 0:TT])
            ins.then_inc(lat_t, 1)
        pe.wait_ge(wuq_in, 16)
        pe.wait_ge(lat_e, 6)
        for t in range(NT):
            for i in range(3):
                n = 3 * t + i
                if n >= 8:
                    pe.wait_ge(q_ev, 1)
                for k in range(3):
                    ins = mm(PS[0:TT, q_bank(t, i), :], CQT[:, k, t * TT:(t + 1) * TT], WUQ[:, k, i * 512:(i + 1) * 512],
                             start=(k == 0), stop=(k == 2))
                ins.then_inc(q_mm, 1)
        pe.wait_ge(q_rot, NT)
        for h in range(H):
            if h >= 8:
                pe.wait_ge(qt_dve if h % 2 == 0 else qt_act, (h - 8) // 2 + 1)
            for t in range(NT):
                ins = nc.tensor.transpose(PS[0:QH, h % 8, t * TT:(t + 1) * TT], Q[:, t, h * QH:(h + 1) * QH],
                                          ident[0:TT, 0:TT])
            ins.then_inc(qt_t, 1)
        pe.wait_ge(qt_dve, H // 2)
        pe.wait_ge(qt_act, H // 2)
        pe.wait_ge(wuk_in, 16)
        for h in range(H):
            if h >= 4:
                pe.wait_ge(k_ev, h - 3)
            for c in range(2):
                ins = mm(PS[0:NOPE, h % 4, 0:TP], WUK[:, c, h * NOPE:(h + 1) * NOPE], CKT[:, c, SMP:T],
                         start=(c == 0), stop=(c == 1))
            ins.then_inc(k_mm, 1)
        pe.wait_ge(wuv_in, 16)
        for i, (p0, rows) in enumerate(QT):
            for half in range(2):
                n = 2 * i + half
                if n >= 2:
                    pe.wait_ge(v_ev, n - 1)
                for c in range(2):
                    ins = mm(PS[0:rows, 6 + half, :], CKT[:, c, SMP + p0:SMP + p0 + rows],
                             WUV[:, c, half * 512:(half + 1) * 512], start=(c == 0), stop=(c == 1))
                ins.then_inc(v_mm, 1)
        for n in range(2 * H):
            h, c = n // 2, n % 2
            if n % 4 == 0 and n >= 8:
                pe.wait_ge(uk_ev, n - 4)
            nc.tensor.transpose(PS[0:NOPE, 4 + n // 4 % 2, (n % 4) * P:(n % 4 + 1) * P],
                                WUK[:, c, h * NOPE:(h + 1) * NOPE], ident).then_inc(uk_t, 1)
        pe.wait_ge(uk_ev, 2 * H)
        pe.wait_ge(k_ev, H)
        for n in range(4):
            c, g = n // 2, n % 2
            for hh in range(8):
                h = 8 * g + hh
                ins = mm(PS[:, n, hh * SMP:(hh + 1) * SMP], UKT[:, h, c * P:(c + 1) * P], QTR[0:NOPE, h, 0:SMP],
                         start=True, stop=True)
            ins.then_inc(ql_mm, 1)
        pe.wait_ge(ql_ev, 4)
        pe.wait_ge(v_ev, 6)
        pe.wait_ge(kpe_copied, H)

        def scores(n):
            h, i = n // 3, n % 3
            p0, rows = QT[i]
            if n >= 2:
                pe.wait_ge(s_nm, n - 1)
            mm(PS[0:rows, n % 2, 0:p0 + rows], QTR[:, h, SMP + p0:SMP + p0 + rows], KT[:, h, 0:p0 + rows],
               start=True, stop=True).then_inc(s_mm, 1)

        scores(0)
        for h in range(H):
            for i, (p0, rows) in enumerate(QT):
                n = 3 * h + i
                if n + 1 < 3 * H:
                    scores(n + 1)
                pe.wait_ge(s_norm, n + 1)
                if n:
                    pe.wait_ge(s_ptc, n)
                for kb in range(i + 1):
                    k0, kr = QT[kb]
                    ins = nc.tensor.transpose(PS[0:kr, 2, kb * P:kb * P + rows], PP[n % 2][0:rows, k0:k0 + kr],
                                              ident[0:rows, 0:rows])
                ins.then_inc(s_pt, 1)
                pe.wait_ge(s_ptc, n + 1)
                lo = h % 2 * VH
                if h >= 2 and i == 0:
                    pe.wait_ge(s_oc, h - 1)
                for kb in range(i + 1):
                    kr = QT[kb][1]
                    ins = mm(PS[lo:lo + VH, 6 + h // 2 % 2, p0:p0 + rows], V[0:kr, kb, h * VH:(h + 1) * VH],
                             PPT[0:kr, kb, 0:rows], start=(kb == 0), stop=(kb == i))
                ins.then_inc(s_o, 1)
        pe.wait_ge(s_oc, H)
        pe.wait_ge(knew_in, 16 * NB)
        for b in range(NB):
            pe.wait_ge(cache_in[b % 2], 16 * 2 * NPG * (b // 2 + 1))
            for g in range(6):
                part, half = g // 2, g % 2
                if b == 0 and g < 2:
                    pass
                elif g < 2:
                    pe.wait_ge(d_ptc_act if g == 0 else d_ptc_dve, b if g == 0 else 2 * b)
                else:
                    pe.wait_ge(d_cte_dve if g % 2 == 0 else d_cte_act, 3 * b + g // 2)
                c0 = (0, P, KV - QH)[part]
                rows = QH if part == 2 else P
                for i in range(4):
                    ins = nc.tensor.transpose(PS[0:rows, 3 + (6 * b + g) % 2, i * P:(i + 1) * P],
                                              CC[b % 2][:, 4 * half + i, c0:c0 + rows], ident)
                ins.then_inc(d_ct, 1)
            pe.wait_ge(d_cte_act, 3 * b + 3)
            pe.wait_ge(d_cte_dve, 3 * b + 3)
            if b:
                pe.wait_ge(d_exp, 2 * b)
            for n in range(3):
                width = 512 if n < 2 else NS
                for c in range(2):
                    keys = CT[:, c, n * 512:(n + 1) * 512] if n < 2 else CKT[:, c, b * NS:(b + 1) * NS]
                    mm(PS[:, n, 0:width], QLT[:, c, b, :], keys, start=(c == 0), stop=False)
                keys = CT[NOPE:QH, 2, n * 512:(n + 1) * 512] if n < 2 else KPT[NOPE:QH, b * NS:(b + 1) * NS]
                ins = mm(PS[:, n, 0:width], QPT[NOPE:QH, b, :], keys, start=False, stop=True)
            ins.then_inc(d_s, 1)
            pe.wait_ge(d_exp, 2 * b + 2)
            for n in range(2):
                for i in range(4):
                    ins = nc.tensor.transpose(PS[:, 3 + n, i * P:(i + 1) * P], PD[:, (4 * n + i) * P:(4 * n + i + 1) * P],
                                              ident)
                ins.then_inc(d_pt, 1)
            nc.tensor.transpose(PS[0:NS, 7, 0:P], PD[:, PAST:PAST + NS], ident).then_inc(d_pt, 1)
            pe.wait_ge(d_ptc_act, b + 1)
            pe.wait_ge(d_ptc_dve, 2 * b + 2)
            if b:
                pe.wait_ge(d_ol, b)
            for i in range(NPG):
                mm(PS[:, 5, 0:KL], PDT[:, i, :], CC[b % 2][:, i, 0:KL], start=(i == 0), stop=False)
            mm(PS[:, 5, 0:KL], PDT[0:NS, NPG, :], KNEW[:, b, :], start=False, stop=True).then_inc(d_o, 1)
            pe.wait_ge(d_ol, b + 1)
            if b:
                pe.wait_ge(d_olc, b)
            for c in range(2):
                ins = nc.tensor.transpose(PS[:, 6, c * P:(c + 1) * P], OL[:, c * P:(c + 1) * P], ident)
            ins.then_inc(d_olt, 1)
        pe.wait_ge(d_olc, NB)
        for h in range(H):
            lo = h % 2 * VH
            for c in range(2):
                ins = mm(PS[lo:lo + VH, h // 8, (h // 2 % 4) * SMP:(h // 2 % 4 + 1) * SMP],
                         WUV[:, c, h * VH:(h + 1) * VH], OLT[:, c, h, :], start=(c == 0), stop=(c == 1),
                         skip_group_check=True)
            if h % 8 == 7:
                ins.then_inc(do_mm, 1)
        pe.wait_ge(do_ev, 2)
        pe.wait_ge(wo_in, 16)
        for t in range(NT):
            for half in range(2):
                for k in range(KD):
                    ins = mm(PS[0:TT, 2 + 2 * t + half, :], OT[:, k, t * TT:(t + 1) * TT],
                             WO[:, k, half * 512:(half + 1) * 512], start=(k == 0), stop=(k == KD - 1))
                ins.then_inc(wo_mm, 1)

        pe.wait_ge(x_mixed, NT)
        turn(3)
        pe.wait_ge(turned_act[3], KD // 2)
        pe.wait_ge(turned_dve[3], KD // 2)
        pe.wait_ge(router_in, 32)
        for t in range(NT):
            for k in range(KD):
                ins = mm(PS[0:TT, 0, t * NE:(t + 1) * NE], HT[:, k, t * TT:(t + 1) * TT], WR[:, k, :],
                         start=(k == 0), stop=(k == KD - 1))
        ins.then_inc(r_mm, 1)
        pe.wait_ge(diag_made, 1)
        for t in range(NT):
            for s in range(t + 1):
                mm(PS[0:TT, 1, t * NE:(t + 1) * NE], ONE[:, 0:TT] if s < t else cn("upper", TT), RT[:, 8, s, :],
                   start=(s == 0), stop=(s == t))
        for s in range(NT):
            ins = mm(PS[:, 2, 0:NE], ONE[:, :], RT[:, 8, s, :], start=(s == 0), stop=(s == NT - 1))
        ins.then_inc(r_cnt_mm, 1)
        for i in range(4):
            for t in range(NT):
                pe.wait_ge(diag_made, 2 + NT * i + t)
                mm(PS[:, 4 + i, t * TT:(t + 1) * TT], ONE[:, :], DG[:, :], start=True, stop=True).then_inc(r_cnt_mm, 1)

        def gather(m):
            pe.wait_ge(i_sel, NT * m + NT)
            for g in range(2):
                for part, src in ((0, HNH), (1, HNL)):
                    for d in range(4):
                        for t in range(NT):
                            ins = mm(PS[:, gather_bank(g, part), d * CAP:(d + 1) * CAP],
                                     src[:, t, (4 * g + d) * P:(4 * g + d + 1) * P], SEL[:, t, :],
                                     start=(t == 0), stop=(t == NT - 1), skip_group_check=True)
                    ins.then_inc(i_g, 1)

        def send_back(m):
            pe.wait_ge(i_yl, m + 1)
            pe.wait_ge(i_sw, m + 1)
            for t in range(NT):
                for half in range(2):
                    n = 2 * t + half
                    if n >= 2:
                        pe.wait_ge(x_added, 6 * m + n - 1)
                    cols = slice(half * 512, half * 512 + 512)
                    three(PS[0:TT, out_bank(n), :], SWH[:, t * TT:(t + 1) * TT], SWL[:, t * TT:(t + 1) * TT],
                          YH[:, cols], YL[:, cols], True, True).then_inc(i_o, 1)

        pe.wait_ge(r_bce, 4)
        pe.wait_ge(hn_low, NT)
        pe.wait_ge(items_known, 2)
        n_items = pe.value_load(NI[0:1, 0:1], min_val=1, max_val=MAXI)
        for n in range(2):
            mm(PS[:, 4 + n, :], ZB[0:1, 0:P], ZB[0:1, 0:512], start=True, stop=True, skip_group_check=True)
        gather(0)
        with pe.Fori(0, n_items) as j:
            def gate_up(c):
                for u in range(2):
                    n = UNITS.index((c, u))
                    pe.wait_ge(unit_low, NU * (j + 1) + n + 1)
                    for k in range(KD // 2):
                        kk = u * KD // 2 + k
                        cols = slice(k * 2 * CW, (k + 1) * 2 * CW)
                        ins = three(PS[:, c % 3, :], XH[:, kk, :], XL[:, kk, :], UH[n % HIGH][:, cols],
                                    LOW_[n % RING][:, cols], kk == 0, kk == KD - 1)
                    ins.then_inc(unit_used, 1)

            def turn_act(c):
                pe.wait_ge(i_a, NC * j + c + 1)
                if c:
                    pe.wait_ge(i_atl, NC * j + c)
                for i in range(CW // P):
                    ins = nc.tensor.transpose(PS[:, 3, i * P:(i + 1) * P], EA[:, i * P:(i + 1) * P], ident)
                ins.then_inc(i_t, 1)

            def down(c):
                n = UNITS.index((c, 2))
                pe.wait_ge(i_atl, NC * j + c + 1)
                pe.wait_ge(unit_low, NU * (j + 1) + n + 1)
                for i in range(CW // P):
                    for h in range(2):
                        cols = slice(i * D + h * 512, i * D + h * 512 + 512)
                        ins = three(PS[:, 4 + h, :], ATH[c % 2][:, i, :], ATL[c % 2][:, i, :], UH[n % HIGH][:, cols],
                                    LOW_[n % RING][:, cols], c == 0 and i == 0, c == NC - 1 and i == CW // P - 1)
                ins.then_inc(unit_used, 1)

            pe.wait_ge(i_x, 4 * j + 4)
            for c in range(NC):
                gate_up(c)
                if c >= 1:
                    turn_act(c - 1)
                if c == 1:
                    send_back(j)
                if c >= 2:
                    down(c - 2)
            pe.wait_ge(x_added, 6 * j + 6)
            gather(j + 1)
            turn_act(NC - 1)
            down(NC - 2)
            down(NC - 1)
        send_back(n_items)

    ctx.close()


def q_bank(t, i):
    return (3 * t + i) % 8


def splits_after(c):
    def last(c):
        return min(UNITS.index((c, 1)) + 2, NU - 1)
    return range(last(c) + 1, (last(c + 1) if c < NC - 1 else NU - 1) + 1)


def gather_bank(g, part):
    return ((6, 7), (2, 0))[g][part]


def out_bank(n):
    return 6 + n % 2


_INS = ["x_prompt", "x_sample", "cache_ckv", "cache_kpe", "state_pool", "page_table", "meta_tokens",
        "g_mix", "g_ffn", "g_final", "pool_w", "pool_scale",
        "mla_w_in", "mla_g_q", "mla_g_kv", "mla_w_uq", "mla_w_uk", "mla_w_uv", "mla_w_o",
        "ffn_w_gate", "ffn_w_up", "ffn_w_down",
        "moe_w_router", "moe_b_router", "moe_w_gate", "moe_w_up", "moe_w_down"]
_OUTS = [("y_prompt", (1, SEQ, D)), ("y_sample", (NB, NS, D)),
         ("ckv_prompt", (1, 1, TP, KL)), ("kpe_prompt", (1, 1, TP, ROPE)), ("pool_prompt", (1, 1, BUF, D)),
         ("ckv_sample", (1, NB, NS, KL)), ("kpe_sample", (1, NB, NS, ROPE)), ("pool_sample", (1, NB, BUF, D))]


def kernel(**inputs):
    import concourse.bacc as bacc
    from concourse.bass_utils import run_bass_kernel_spmd as run

    nc = bacc.Bacc("TRN2", target_bir_lowering=False, num_devices=1)
    arrays, a, o = {}, {}, {}
    table, pooling = shape_constants()
    for name in _INS + ["consts", "consts_pool"]:
        x = table if name == "consts" else pooling if name == "consts_pool" else np.ascontiguousarray(inputs[name])
        arrays[f"in_{name}"] = x
        a[name] = nc.dram_tensor(f"in_{name}", x.shape, mybir.dt.from_np(x.dtype), kind="ExternalInput").ap()
    for name, shape in _OUTS:
        o[name] = nc.dram_tensor(f"out_{name}", shape, F32, kind="ExternalOutput").ap()
    program(nc, a, o)
    r = run(nc, [arrays], core_ids=[0])
    return tuple(r.results[0][f"out_{name}"] for name, _ in _OUTS)
```

```python
from contextlib import ExitStack

import numpy as np

import concourse.bass as bass
from concourse import mybir

F32 = mybir.dt.float32
F32R = mybir.dt.float32r
BF16 = mybir.dt.bfloat16
I32 = mybir.dt.int32
ALU = mybir.AluOpType
ACT = mybir.ActivationFunctionType
AX = mybir.AxisListType

P = 128
D = 1024
KD = D // P
SEQ, META, NB, NS = 256, 16, 8, 8
SMP = NB * NS
TP = SEQ + META
T = SMP + TP
NT = 3
TT = T // NT
WINDOWS = (2, 4, 8, 16)
BUF = 15
EPS = 1e-6
H = 16
QL, KL, NOPE, ROPE, VH = 384, 256, 64, 32, 64
HALF = ROPE // 2
QH = NOPE + ROPE
KV = KL + ROPE
PROJ = QL + KL + ROPE
PAST, PAGE = 1024, 128
NPG = PAST // PAGE
SCALE = float(QH) ** -0.5
FF = 2816
NE = 8
CAP = 128
MAXI = 2 * T // CAP + NE
NEG = -1e30
LOW = -3e38

CW = 256
NC = FF // CW
UNIT = KD * CW
RING_D = 3
UNITS = [u for c in range(NC + 2) for u in ([(c, 0), (c, 1)] if c < NC else []) + ([(c - 2, 2)] if c >= 2 else [])]
NU = len(UNITS)
RING = 11
HIGH = 3
assert NC * CW == FF and NU == 3 * NC and NU % RING == 0 and NU % HIGH == 0 and 3 * RING_D <= RING

KB = [(0, 128), (128, 128), (256, 16)]
TAIL, T0 = 32, TP - 32
GROUP = P // TAIL
AU = [u for g in range(H // GROUP) for u in [("tail", g)] + [("head", h) for h in range(GROUP * g, GROUP * g + GROUP)]]
NAU = len(AU)
PAIR_DONE = {AU.index(("head", 2 * p + 1)): p for p in range(H // 2)}

_W = [("ident", 128), ("upper", TT), ("iota", 128), ("part", 1), ("mask", 2 * P), ("maskt", TP), ("maskd", NS),
      ("cos", NT * HALF), ("sin", NT * HALF), ("ridx", NE), ("tri", NE * NE), ("steps", NE * NT), ("items", MAXI)]
_WP = [("pm0", 4 * P), ("pm1", 4 * P), ("pstate", 4 * SMP)]
COL, NCOL, NPOOL = {}, 0, 0
for _k, _w in _W:
    COL[_k] = (NCOL, NCOL + _w)
    NCOL += _w
for _k, _w in _WP:
    COL[_k] = (NPOOL, NPOOL + _w)
    NPOOL += _w


def shape_constants():
    c, pooling = np.zeros((P, NCOL), np.float32), np.zeros((P, NPOOL), np.float32)

    def put(name, a):
        (pooling if name[0] == "p" and name != "part" else c)[:a.shape[0], COL[name][0]:COL[name][1]] = a.reshape(a.shape[0], -1)

    put("ident", np.eye(P))
    put("upper", np.triu(np.ones((TT, TT)), 1))
    put("iota", np.tile(np.arange(P), (P, 1)))
    put("part", np.arange(P)[:, None])
    r = np.arange(P)[:, None]
    put("mask", np.where(np.arange(2 * P)[None] <= P + r, 0.0, NEG))
    put("maskt", np.where(np.arange(TP)[None] <= T0 + r % TAIL, 0.0, NEG))
    put("maskd", np.where(np.arange(NS)[None] <= r % NS, 0.0, NEG))
    pos = np.concatenate([np.tile(PAST + np.arange(NS), NB), np.arange(TP)]).astype(np.float32)
    freqs = (np.float32(1) / np.float32(10000.0) ** (np.arange(HALF, dtype=np.float32) * np.float32(2.0 / ROPE))).astype(np.float32)
    ang = (pos[:, None] * freqs[None]).astype(np.float32).reshape(NT, TT, HALF).swapaxes(0, 1)
    put("cos", np.cos(ang))
    put("sin", np.sin(ang))
    put("ridx", np.tile(NE - np.arange(NE), (P, 1)))
    put("tri", np.tile(np.tril(np.ones((NE, NE))).reshape(1, -1), (P, 1)))
    steps = np.tile(CAP * np.arange(NT), (NE, 1))
    steps[0, 0] = -1
    put("steps", np.tile(steps.reshape(1, -1), (P, 1)))
    put("items", np.tile(np.arange(MAXI), (P, 1)))
    def band(a, b, w):
        n = np.minimum(b[None] + 1, w)
        return ((a[:, None] <= b[None]) & (a[:, None] > b[None] - w)) / n - (a[:, None] == b[None])
    m0, m1 = np.zeros((2, TT, 4, P))
    state = np.zeros((NB * BUF, 4, SMP))
    first = TT - SMP
    for g, w in enumerate(WINDOWS):
        m0[SMP:, g, SMP:] = band(np.arange(first), np.arange(first + 16), w)
        s = np.arange(NS)
        one = ((s[:, None] <= s[None]) & (s[:, None] > s[None] - w)) / w - (s[:, None] == s[None])
        old = (np.arange(BUF)[:, None] - BUF > s[None] - w) / w
        for b in range(NB):
            m0[b * NS:(b + 1) * NS, g, b * NS:(b + 1) * NS] = one
            state[b * BUF:(b + 1) * BUF, g, b * NS:(b + 1) * NS] = old
        q = first + np.arange(TT)
        m1[:, g] = band(q, q[0] + np.arange(P), w)
    put("pm0", m0)
    put("pm1", m1)
    put("pstate", state)
    return c, pooling


def program(nc, a, o):
    ctx = ExitStack()

    top = [16640]

    def place(name, shape, dtype, off=None):
        n = 4 * int(np.prod(shape[1:]))
        if off is None:
            off = top[0]
            top[0] += (n + 31) // 32 * 32
        return nc.alloc_sbuf_tensor_at(name, shape, dtype, offset=off)

    X = place("X", [TT, NT, D], F32)
    H_OFF = top[0]
    HN = place("HN", [TT, NT, D], F32)
    HT_OFF = top[0]
    HTH = place("HTH", [P, KD, T], F32R)
    CN = place("CN", [P, NCOL], F32)
    SCR_OFF = top[0]
    SCR = place("SCR", [P, D], F32)
    G_OFF = top[0]
    G = [place(f"G{i}", [TT, D], F32) for i in range(3)]
    GQ = place("GQ", [TT, QL], F32)
    GKV = place("GKV", [TT, KL], F32)
    SS = place("SS", [TT, 32], F32)
    RS = place("RS", [TT, 32], F32)
    ZB = place("ZB", [1, 512], BF16)
    RPS = [place(f"RPS{i}", [P, 8], F32) for i in range(4)]
    DS = place("DS", [P, 8], F32)
    DM = place("DM", [P, NS], F32)
    PAGES = place("PAGES", [1, NB * NPG], I32)
    WR = place("WR", [P, KD, NE], F32)
    BR = place("BR", [TT, NE], F32)
    NHALF = place("NHALF", [TT, 2], F32)
    A = top[0]
    END = nc.sbuf_usable_end

    def area():
        cur = [A]

        def get(name, shape, dtype=F32, off=None):
            if off is not None:
                return place(name, shape, dtype, off)
            n = (4 * int(np.prod(shape[1:])) + 31) // 32 * 32
            t = place(name, shape, dtype, cur[0])
            cur[0] += n
            assert cur[0] <= END, (name, cur[0] - END)
            return t
        get.cur = cur
        return get

    get = area()
    RAW = [get(f"RAW{i}", [P, UNIT]) for i in range(RING)]
    FFN_OFF = A
    UH = [get(f"UH{i}", [P, UNIT], F32R) for i in range(HIGH)]
    FFN_END = get.cur[0]
    LOWS = [place(f"LOW{i}", [P, UNIT], F32R, FFN_OFF + i * 4 * UNIT) for i in range(RING)]
    PAIR = [place(f"PAIR{i}", [P, KD, 2, CW], F32, FFN_OFF + 3 * i * 4 * UNIT) for i in range(RING_D)]
    LOWPAIR = [place(f"LOWPAIR{i}", [P, KD, 2, CW], F32R, FFN_OFF + 3 * i * 4 * UNIT) for i in range(RING_D)]
    HTL = get("HTL", [P, KD, T], F32R)
    SG = get("SG", [P, T])
    AF = get("AF", [P, T])
    AH = get("AH", [P, 2, T], F32R)
    AL = get("AL", [P, 2, T], F32R)
    get = area()
    get.cur[0] = FFN_END
    ST = get("ST", [NB * BUF, D])
    PW = get("PW", [P, KD, 256])
    DT = place("DT", [P, KD, T], F32, HT_OFF)
    PSC = place("PSC", [P, D], F32, G_OFF + 4 * D)
    CP = get("CP", [P, NPOOL])

    get = area()
    S1 = get.cur[0]
    get.cur[0] += 4 * KD * PROJ
    WIN_OFF = A + 4 * (RING * UNIT - KD * PROJ)
    WIN = place("WIN", [P, KD, PROJ], F32, WIN_OFF)
    WINL = place("WINL", [P, KD, PROJ], F32R, WIN_OFF)
    WINH = [place(f"WINH{k}", [P, PROJ], F32R, A + 4 * (6 * UNIT + k * PROJ) if k < KD - 1 else G_OFF + 4 * D)
            for k in range(KD)]
    WUQ = place("WUQ", [P, 3, H * QH], F32, A)
    WUQL = place("WUQL", [P, 3, H * QH], F32R, A)
    WUQH = place("WUQH", [P, 3, H * QH], F32R, A + 4 * RING * UNIT)
    S2 = get.cur[0]
    Q = get("Q", [TT, NT, H * QH])
    S3 = get.cur[0]
    get.cur[0] += 4 * 3 * H * QH
    S5 = get.cur[0]
    QTR = get("QTR", [QH, H, T])
    KT = get("KT", [QH, H, TP])
    S7 = get.cur[0]
    UKT = get("UKT", [NOPE, H, KL])
    QLT = get("QLT", [P, 2, NB, H * NS])
    QPT = get("QPT", [QH, NB, H * NS])
    WUV = get("WUV", [P, 2, H * VH])
    S11 = get.cur[0]
    WUK = get("WUK", [P, 2, H * NOPE])
    KVN = get("KVN", [TT, NT, KV])
    CKT = get("CKT", [P, 2, T])
    KPT = get("KPT", [QH, T])
    PR = place("PR", [TT, NT, PROJ], F32, H_OFF)
    CQTH = place("CQTH", [P, 3, T], F32R, H_OFF + 8064)
    CQTL = place("CQTL", [P, 3, T], F32R, S3)
    OT = place("OT", [P, KD, T], F32, HT_OFF)
    CC = [place(f"CC{i}", [P, NPG, KV], F32, off) for i, off in enumerate((S1, S1 + 9216, S7))]
    V = place("V", [P, 3, H * VH], F32, S2)
    PP = [place(f"PP{i}", [P, 384], F32, S2 + 12288 + i * 1536) for i in range(4)]
    PPT = [place(f"PPT{i}", [P, 384], F32, H_OFF + 4128 + i * 1536) for i in range(2)]
    CT = [place(f"CT{i}", [P, 3, PAST], F32, S2 + 12288 * (2 - i)) for i in range(2)]
    KNEW = place("KNEW", [NS, NB, KL], F32, G_OFF)
    WO = place("WO", [P, KD, D], F32, S5)
    PD = place("PD", [P, PAST + NS], F32, H_OFF)
    PDT = place("PDT", [P, NPG + 1, P], F32, H_OFF + 4128)
    OL = place("OL", [P, KL], F32, H_OFF + 8736)
    OLT = place("OLT", [P, 2, H, SMP], F32, S11)
    QR = place("QR", [TT, 4, H, HALF], F32, SCR_OFF)
    KR = place("KR", [TT, 4, HALF], F32, SCR_OFF + 2048)

    get = area()
    get.cur[0] = FFN_END
    HNH = get("HNH", [TT, NT, D], F32R)
    HNL = get("HNL", [TT, NT, D], F32R)
    EG = get("EG", [P, 256])
    XN = get("XN", [P, D])
    XH = place("XH", [P, KD, CAP], F32R, H_OFF)
    XL = place("XL", [P, KD, CAP], F32R, H_OFF + 4096)
    EA = place("EA", [P, 256], F32, H_OFF + 8192)
    ATH = [place("ATH0", [P, 2, CAP], F32R, H_OFF + 9216), place("ATH1", [P, 2, CAP], F32R, HT_OFF + 9600)]
    ATL = [place("ATL0", [P, 2, CAP], F32R, H_OFF + 10240), get("ATL1", [P, 2, CAP], F32R)]
    YH = place("YH", [P, D], F32R, G_OFF)
    YL = place("YL", [P, D], F32R, G_OFF + 4096)
    SEL = place("SEL", [TT, NT, CAP], F32R, HT_OFF)
    G1 = place("G1", [P, T], F32, HT_OFF + 1536)
    G2 = place("G2", [P, T], F32, HT_OFF + 2880)
    W1 = place("W1", [P, T], F32, HT_OFF + 4224)
    W2 = place("W2", [P, T], F32, HT_OFF + 5568)
    SWH = place("SWH", [P, T], F32R, HT_OFF + 6912)
    SWL = place("SWL", [P, T], F32R, HT_OFF + 8256)
    T1 = place("T1", [P, T], F32, SCR_OFF)
    T2 = place("T2", [P, T], F32, SCR_OFF + 1344)
    TS = place("TS", [TT, CAP], F32, SCR_OFF + 2688)
    RT = place("RT", [TT, 10, NT, NE], F32, G_OFF)
    RC = get("RC", [TT, 12, NT])
    TO = place("TO", [P, 3, NE], F32, G_OFF + 1024)
    IE = place("IE", [1, MAXI, NE], F32, G_OFF + 1216)
    EF = place("EF", [1, MAXI], F32, G_OFF + 1664)
    FL = place("FL", [P, NE, NT], F32, G_OFF + 1728)
    TR = place("TR", [P, NE, NE], F32, G_OFF + 1824)
    BOTH = get("BOTH", [TT, NT, NE], BF16)
    ONEH = get("ONEH", [TT, P], BF16)
    UPH = get("UPH", [TT, TT], BF16)
    ONE = place("ONE", [TT, P], F32, G_OFF + 2176)
    DG = [place(f"DG{i}", [TT, NT, TT], F32, off)
          for i, off in enumerate((SCR_OFF, SCR_OFF + 1344, SCR_OFF + 2688, G_OFF + 2688))]
    HT3 = place("HT3", [P, 2, KD, TT], F32, FFN_OFF + 4 * (RING + 2) * UNIT)
    EI = get("EI", [1, MAXI], I32)
    NI = get("NI", [1, 1], I32)
    PJ = get("PJ", [P, 1])

    PS = ctx.enter_context(nc.psum_tensor("PS", [P, 8, 512], F32))

    def sem(name):
        return ctx.enter_context(nc.semaphore(name))

    def cn(name, rows=P):
        return (CP if name in dict(_WP) else CN)[0:rows, COL[name][0]:COL[name][1]]

    ident = cn("ident")

    x_in, consts_in, gains_in = sem("x_in"), sem("consts_in"), sem("gains_in")
    gain1_in, gain4_in, small_in = sem("gain1_in"), sem("gain4_in"), sem("small_in")
    gain3_in, dense_done = sem("gain3_in"), sem("dense_done")
    gain0_in, pool_in, pool_w_in = sem("gain0_in"), sem("pool_in"), sem("pool_w_in")
    gu_in = [sem(f"gu_in{i}") for i in range(RING_D)]
    dn_in = [sem(f"dn_in{i}") for i in range(RING_D)]
    raw_in = [sem(f"raw_in{i}") for i in range(RING)]
    unit_high, unit_low, unit_used = sem("unit_high"), sem("unit_low"), sem("unit_used")
    win_in, wuq_in, wuk_in, wuv_in, wo_in = (sem(n) for n in ("win_in", "wuq_in", "wuk_in", "wuv_in", "wo_in"))
    cache_in = [sem(f"cache_in{i}") for i in range(3)]
    knew_in = sem("knew_in")
    squares = [sem(f"squares{i}") for i in range(5)]
    normed = [sem(f"normed{i}") for i in range(5)]
    turned = {i: sem(f"turned{i}") for i in (1, 2, 3)}
    turned_act = {i: sem(f"turned_act{i}") for i in (1, 2, 3)}
    turned_dve = {i: sem(f"turned_dve{i}") for i in (1, 2, 3)}
    pool_mm, pool_act, pool_dve, pool_y, pool_out = (sem(n) for n in ("pool_mm", "pool_act", "pool_dve", "pool_y", "pool_out"))
    x_pooled, x_dense, x_mixed, x_added = (sem(n) for n in ("x_pooled", "x_dense", "x_mixed", "x_added"))
    gate_mm, silu_done, act_made, act_high, act_low = (
        sem(n) for n in ("gate_mm", "silu_done", "act_made", "act_high", "act_low"))
    stored, y_out = sem("stored"), sem("y_out")
    dve_step = sem("dve_step")
    act_step = sem("act_step")
    inverse_root, inverse_root_qk = [sem(f"inverse_root{i}") for i in range(5)], sem("inverse_root_qk")
    pool_step = sem("pool_step")

    block = ctx.enter_context(nc.Block())

    def linker(eng, s, base=0):
        n = [0]

        def link(ins):
            n[0] += 1
            ins.then_inc(s, 1)
            eng.wait_ge(s, base + n[0])
        link.n = n
        return link

    proj_mm, proj_out = sem("proj_mm"), sem("proj_out")
    sq_q = sem("sq_q")
    latent_ready = sem("latent_ready")
    lat_t, lat_h, lat_e = sem("lat_t"), sem("lat_h"), sem("lat_e")
    wide_high, wide_low = sem("wide_high"), sem("wide_low")
    q_mm, q_ev, q_rot, qt_t, qt_act, qt_dve = (sem(n) for n in ("q_mm", "q_ev", "q_rot", "qt_t", "qt_act", "qt_dve"))
    k_mm, k_ev, kpe_copied, v_mm, v_ev, uk_t, uk_ev, ql_mm, ql_ev, qp_copied = (
        sem(n) for n in ("k_mm", "k_ev", "kpe_copied", "v_mm", "v_ev", "uk_t", "uk_ev", "ql_mm", "ql_ev", "qp_copied"))
    s_mm, s_nm, s_exp, s_norm, s_pt, s_ptc, s_o, s_oc = (
        sem(n) for n in ("s_mm", "s_nm", "s_exp", "s_norm", "s_pt", "s_ptc", "s_o", "s_oc"))
    d_ct, d_cte_act, d_cte_dve, d_s, d_nm, d_exp, d_pt, d_ptc_act, d_ptc_dve, d_o, d_ol, d_olt, d_olc = (
        sem(n) for n in ("d_ct", "d_cte_act", "d_cte_dve", "d_s", "d_nm", "d_exp", "d_pt", "d_ptc_act",
                         "d_ptc_dve", "d_o", "d_ol", "d_olt", "d_olc"))
    do_mm, do_ev, wo_mm = sem("do_mm"), sem("do_ev"), sem("wo_mm")
    r_mm, r_cnt_mm, r_dve, r_act, items_known = (
        sem(n) for n in ("r_mm", "r_cnt_mm", "r_dve", "r_act", "items_known"))
    hn_high, hn_low = sem("hn_high"), sem("hn_low")
    i_sel, i_g, i_n, i_xt, i_xh, i_xl, i_sg, i_a, i_t, i_ath, i_atl, i_yh, i_yl, i_sw, i_o = (
        sem(n) for n in ("i_sel", "i_g", "i_n", "i_xt", "i_xh", "i_xl", "i_sg", "i_a", "i_t", "i_ath", "i_atl", "i_yh", "i_yl", "i_sw", "i_o"))
    item_step = sem("item_step")
    diag_made = sem("diag_made")

    def load_dense(sp, c, slot):
        cols = slice(c * CW, (c + 1) * CW)
        if c >= RING_D:
            sp.wait_ge(unit_used, 3 * (c - RING_D) + 2)
        for g, w in enumerate(("ffn_w_gate", "ffn_w_up")):
            sp.dma_start(PAIR[slot][:, :, g, :], a[w][0, :, cols].rearrange("(k p) f -> p k f", p=P)).then_inc(gu_in[slot], 16)
        if c >= RING_D:
            sp.wait_ge(unit_used, 3 * (c - RING_D) + 3)
        sp.dma_start(RAW[3 * slot + 2][:, :].rearrange("p (j d) -> p j d", d=D),
                     a["ffn_w_down"][0, cols, :].rearrange("(j p) d -> p j d", p=P)).then_inc(dn_in[slot], 16)

    def load_unit(sp, e, n):
        (c, u), slot = UNITS[n], n % RING
        cols, one = slice(c * CW, (c + 1) * CW), bass.ds(e, 1)
        if u == 2:
            to = RAW[slot][:, :].rearrange("p (h d) -> p h d", h=2)
            for h in range(2):
                sp.dma_start(to[:, h:h + 1, :], a["moe_w_down"][0, one, c * CW + h * P:c * CW + (h + 1) * P, :]
                             .rearrange("e p d -> p e d")).then_inc(raw_in[slot], 16)
        else:
            to = RAW[slot][:, :].rearrange("p (k g f) -> p k g f", g=2, f=CW)
            for g, w in enumerate(("moe_w_gate", "moe_w_up")):
                sp.dma_start(to[:, :, g, :], a[w][0, one, u * (D // 2):(u + 1) * (D // 2), cols]
                             .rearrange("e (k p) f -> p (e k) f", p=P)).then_inc(raw_in[slot], 16)

    def dense_low(c, u):
        slot = c % RING_D
        return LOWS[3 * slot + 2][:, :] if u == 2 else LOWPAIR[slot][:, :, :, u * P:(u + 1) * P]

    def dense_raw(c, u):
        slot = c % RING_D
        return RAW[3 * slot + 2][:, :] if u == 2 else PAIR[slot][:, :, :, u * P:(u + 1) * P]

    def dense_high(u):
        return UH[2][:, :] if u == 2 else UH[u][:, :].rearrange("p (k g f) -> p k g f", g=2, f=P)

    @block.sync
    def _(sp):
        sp.dma_start(X[0:SMP, 0, :], a["x_sample"].rearrange("b s d -> (b s) d")).then_inc(x_in, 16)
        sp.dma_start(X[SMP:SMP + META, 0, :], a["meta_tokens"]).then_inc(x_in, 16)
        sp.dma_start(X[SMP + META:TT, 0, :], a["x_prompt"][0, 0:TT - SMP - META, :]).then_inc(x_in, 16)
        for t in (1, 2):
            r = t * TT - SMP - META
            sp.dma_start(X[:, t, :], a["x_prompt"][0, r:r + TT, :]).then_inc(x_in, 16)
        sp.dma_start(G[0][:, :], a["g_mix"][0:1, :].partition_broadcast(TT)).then_inc(gain0_in, 16)
        sp.dma_start(CP[:, :], a["consts_pool"]).then_inc(pool_in, 16)
        sp.dma_start(ST[:, :], a["state_pool"][0].rearrange("b n d -> (b n) d")).then_inc(pool_in, 16)
        sp.dma_start(PSC[:, :], a["pool_scale"][0:1, :].partition_broadcast(P)).then_inc(pool_w_in, 16)
        sp.dma_start(PW[:, :, :], a["pool_w"][0].rearrange("g (c p) n -> p (g c) n", p=P)).then_inc(pool_w_in, 16)
        sp.dma_start(G[2][:, :], a["g_ffn"][0:1, :].partition_broadcast(TT)).then_inc(gains_in, 16)
        sp.dma_start(CN[:, :], a["consts"]).then_inc(consts_in, 16)
        sp.wait_ge(pool_out, 16 * 2)
        for c in range(RING_D):
            load_dense(sp, c, c)
        sp.dma_start(PAGES[:, :], a["page_table"].rearrange("(o b) p -> o (b p)", o=1)).then_inc(small_in, 16)
        sp.dma_start(GQ[:, :], a["mla_g_q"][0:1, :].partition_broadcast(TT)).then_inc(small_in, 16)
        sp.dma_start(GKV[:, :], a["mla_g_kv"][0:1, :].partition_broadcast(TT)).then_inc(small_in, 16)
        sp.dma_start(WR[:, :, :], a["moe_w_router"][0].rearrange("(k p) n -> p k n", p=P)).then_inc(small_in, 16)
        sp.dma_start(BR[:, :], a["moe_b_router"][0:1, :].partition_broadcast(TT)).then_inc(small_in, 16)
        sp.wait_ge(x_pooled, NT)
        sp.dma_start(G[0][:, :], a["g_mix"][1:2, :].partition_broadcast(TT)).then_inc(gain1_in, 16)
        for c in range(RING_D, NC):
            load_dense(sp, c, c % RING_D)
        sp.wait_ge(unit_used, NU - 6)
        sp.dma_start(WIN[:, :, :], a["mla_w_in"][0].rearrange("(k p) n -> p k n", p=P)).then_inc(win_in, 16)
        sp.wait_ge(unit_used, NU - 3)
        sp.dma_start(WUQ[:, :, :], a["mla_w_uq"][0].rearrange("(k p) n -> p k n", p=P)).then_inc(wuq_in, 16)
        sp.wait_ge(x_dense, NT)
        sp.dma_start(G[2][:, :], a["g_ffn"][1:2, :].partition_broadcast(TT)).then_inc(gain3_in, 16)
        sp.dma_start(WUK[:, :, :], a["mla_w_uk"][0].rearrange("(c p) h n -> p c (h n)", p=P)).then_inc(wuk_in, 16)
        sp.dma_start(WUV[:, :, :], a["mla_w_uv"][0].rearrange("(c p) h v -> p c (h v)", p=P)).then_inc(wuv_in, 16)

        nphys = a["cache_ckv"].shape[1]

        def load_cache(b):
            with sp.Fori(0, NPG) as i:
                page = sp.value_load(PAGES[0:1, b * NPG:(b + 1) * NPG][:, bass.ds(i, 1)], min_val=0, max_val=nphys - 1)
                one, to = bass.ds(page, 1), bass.ds(i, 1)
                sp.dma_start(CC[b % 3][:, to, 0:KL], a["cache_ckv"][0, one, :, :].rearrange("e p c -> p e c"))\
                  .then_inc(cache_in[b % 3], 16)
                sp.dma_start(CC[b % 3][:, to, KL:KV], a["cache_kpe"][0, one, :, :].rearrange("e p c -> p e c"))\
                  .then_inc(cache_in[b % 3], 16)

        sp.wait_ge(small_in, 16 * 5)
        sp.wait_ge(q_mm, 3 * NT)
        for b in range(2):
            load_cache(b)
        sp.wait_ge(ql_mm, 2 * 2)
        load_cache(2)
        for b in range(NB):
            sp.dma_start(KNEW[:, b, :], KVN[b * NS:(b + 1) * NS, 0, 0:KL]).then_inc(knew_in, 16)
        sp.wait_ge(s_oc, H // 2)
        sp.wait_ge(qp_copied, 1)
        sp.dma_start(WO[:, :, :], a["mla_w_o"][0].rearrange("(k p) n -> p k n", p=P)).then_inc(wo_in, 16)
        for b in range(3, NB):
            sp.wait_ge(d_o, b - 2)
            load_cache(b)
        sp.wait_ge(d_o, NB)
        for n in range(RING):
            if n == (S5 - A) // (4 * UNIT):
                sp.wait_ge(wo_mm, 2 * NT)
            load_unit(sp, 0, n)
        sp.wait_ge(normed[3], NT)
        sp.dma_start(G[2][:, :], a["g_final"].rearrange("(a d) -> a d", a=1).partition_broadcast(TT)).then_inc(gain4_in, 16)

        def load_rest(e, j):
            for n in range(RING, NU):
                sp.wait_ge(unit_used, NU * (j + 1) + n - RING + 1)
                load_unit(sp, e, n)

        sp.wait_ge(items_known, 2)
        before_last = sp.value_load(NI[0:1, 0:1], min_val=1, max_val=MAXI - 1)
        with sp.Fori(0, before_last) as j:
            e = sp.value_load(EI[0:1, bass.ds(j, 1)], min_val=0, max_val=NE - 1)
            e_next = sp.value_load(EI[0:1, 1:MAXI][:, bass.ds(j, 1)], min_val=0, max_val=NE - 1)
            load_rest(e, j)
            for n in range(RING):
                sp.wait_ge(unit_used, NU * (j + 2) + n - RING + 1)
                load_unit(sp, e_next, n)
        e = sp.value_load(EI[0:1, bass.ds(before_last, 1)], min_val=0, max_val=NE - 1)
        load_rest(e, before_last)

        sp.wait_ge(normed[4], 1)
        sp.dma_start(o["y_sample"].rearrange("b s d -> (b s) d"), HN[0:SMP, 0, :]).then_inc(y_out, 16)
        sp.dma_start(o["y_prompt"][0, 0:TT - SMP - META, :], HN[SMP + META:TT, 0, :]).then_inc(y_out, 16)
        for t in (1, 2):
            r = t * TT - SMP - META
            sp.wait_ge(normed[4], t + 1)
            sp.dma_start(o["y_prompt"][0, r:r + TT, :], HN[:, t, :]).then_inc(y_out, 16)
        sp.wait_ge(y_out, 16 * 4)

    @block.gpsimd
    def _(pool):
        count = [0]

        def store(dst, src):
            count[0] += 16
            pool.dma_start(dst, src).then_inc(stored, 16)

        nc.gpsimd.memset(NHALF[:, :], -0.5).then_inc(pool_step, 1)
        pool.wait_ge(pool_step, 1)
        steps = [1]

        def inverse_roots(i, step, width, done):
            cols = slice(i, i + step * (width - 1) + 1, step)
            steps[0] += 1
            nc.gpsimd.tensor_scalar(RS[:, cols], SS[:, cols], EPS, None, ALU.add).then_inc(pool_step, 1)
            pool.wait_ge(pool_step, steps[0])
            nc.gpsimd.tensor_tensor(RS[:, cols], RS[:, cols], NHALF[:, 0:width], ALU.pow).then_inc(done, 1)

        def roots_of(n):
            for t in range(NT):
                pool.wait_ge(squares[n], t + 1)
                inverse_roots(3 * n + t, 1, 1, inverse_root[n])

        pool.dma_start(o["pool_sample"][0, :, 0:BUF - NS, :], a["state_pool"][0, :, NS:BUF, :]).then_inc(stored, 16)
        count[0] += 16
        roots_of(0)
        pool.wait_ge(normed[0], NT)
        pool.dma_start(o["pool_prompt"][0, 0], HN[TT - BUF:TT, 2, :]).then_inc(pool_out, 16)
        pool.dma_start(o["pool_sample"][0, :, BUF - NS:BUF, :], HN[0:SMP, 0, :]).then_inc(pool_out, 16)
        roots_of(1)
        roots_of(2)
        for t in range(NT):
            pool.wait_ge(sq_q, 2 * t + 2)
            inverse_roots(15 + t, 3, 2, inverse_root_qk)
        pool.wait_ge(latent_ready, NT)
        store(o["ckv_sample"][0].rearrange("b s c -> (b s) c"), KVN[0:SMP, 0, 0:KL])
        store(o["kpe_sample"][0].rearrange("b s c -> (b s) c"), KVN[0:SMP, 0, KL:KV])
        for t in range(NT):
            p0 = SMP if t == 0 else 0
            r0 = t * TT + p0 - SMP
            store(o["ckv_prompt"][0, 0, r0:r0 + TT - p0, :], KVN[p0:TT, t, 0:KL])
            store(o["kpe_prompt"][0, 0, r0:r0 + TT - p0, :], KVN[p0:TT, t, KL:KV])
        pool.wait_ge(lat_e, 9)
        pool.wait_ge(q_mm, 3 * NT)
        for h in range(H):
            nc.gpsimd.tensor_copy(KT[NOPE:QH, h, :], KPT[NOPE:QH, SMP:T]).then_inc(kpe_copied, 1)
        for i, t in enumerate(MIXED):
            pool.wait_ge(squares[3], i + 1)
            inverse_roots(9 + t, 1, 1, inverse_root[3])
        roots_of(4)
        pool.wait_ge(stored, count[0])
        pool.wait_ge(pool_out, 16 * 2)

    @block.scalar
    def _(act):
        link = linker(act, act_step)

        def split_high(dst, src, n, loaded, count):
            act.wait_ge(loaded, count)
            if not (isinstance(n, int) and n < HIGH):
                act.wait_ge(unit_used, n - HIGH + 1)
            nc.scalar.copy(dst, src).then_inc(unit_high, 1)

        def square(n, t, ready, count, before=None):
            act.wait_ge(ready, count)
            before = t if before is None else before
            if before:
                act.wait_ge(squares[n], before)
            nc.scalar.activation(SCR[0:TT, :], X[:, t, :], ACT.Square, scale=1 / 32,
                                 accum_out=SS[:, 3 * n + t:3 * n + t + 1]).then_inc(squares[n], 1)

        def tile_high(n, t):
            for g in range(2):
                act.wait_ge(turned[n], 2 * t + g + 1)
                nc.scalar.copy(HTH[:, 4 * g:4 * g + 4, t * TT:(t + 1) * TT],
                               PS[:, g, 0:4 * TT].rearrange("p (d t) -> p d t", d=4)).then_inc(turned_act[n], 1)

        for t in range(NT):
            square(0, t, x_in, 16 * 5)
        for d in range(1, KD, 2):
            act.wait_ge(pool_mm, d + 1)
            nc.scalar.copy(DT[:, d, :], PS[:, d, 0:T]).then_inc(pool_act, 1)
        for u in range(3):
            split_high(dense_high(u), dense_raw(0, u), u, dn_in[0] if u == 2 else gu_in[0], 16 if u == 2 else 32)
        square(1, 0, x_pooled, 1)
        square(1, 1, x_pooled, 2)
        tile_high(1, 0)
        square(1, 2, x_pooled, 3)
        tile_high(1, 1)
        tile_high(1, 2)

        def dense_step(c, q, fills, last):
            nxt = (c + 1) % RING_D
            for j in range(2):
                tile = 2 * q + j
                act.wait_ge(gate_mm, tile + 1)
                nc.scalar.activation(SG[:, :], PS[:, 0, 0:T], ACT.Silu).then_inc(silu_done, 1)
                act.wait_ge(act_made, tile + 1)
                nc.scalar.copy(AH[:, j, :], AF[:, :]).then_inc(act_high, 1)
                if last and j == 0:
                    act.wait_ge(win_in, 16)
                    for k in range(KD):
                        nc.scalar.copy(WINH[k][:, :], WIN[:, k, :]).then_inc(wide_high, 1)
                if not last:
                    split_high(dense_high(j), dense_raw(nxt, j), 3 * (q + 1) + j, gu_in[nxt], fills * 32)
            if not last:
                split_high(dense_high(2), dense_raw(nxt, 2), 3 * (q + 1) + 2, dn_in[nxt], fills * 16)

        with act.Fori(0, NC // RING_D) as r:
            for i in range(RING_D):
                dense_step(i, r * RING_D + i, r + 1 + (i + 1) // RING_D, False)
        for c in range(NC // RING_D * RING_D, NC):
            dense_step(c % RING_D, c, (c + 1) // RING_D + 1, c == NC - 1)
        def tile_out(i):
            act.wait_ge(turned[3], 2 * i + 1)
            nc.scalar.copy(HT3[:, i % 2, 0:4, :], PS[:, 0, 0:4 * TT].rearrange("p (d t) -> p d t", d=4))\
              .then_inc(turned_act[3], 1)

        def projected(t):
            act.wait_ge(proj_mm, 2 * t + 1)
            link(nc.scalar.copy(PR[:, t, 0:512], PS[0:TT, 2 + 2 * t, :]))
            act.wait_ge(proj_mm, 2 * t + 2)
            nc.scalar.copy(PR[:, t, 512:PROJ], PS[0:TT, 3 + 2 * t, 0:PROJ - 512]).then_inc(proj_out, 1)
            act.wait_ge(proj_out, t + 1)
            act.wait_ge(sq_q, 2 * t) if t else act.wait_ge(squares[2], NT)
            nc.scalar.activation(SCR[0:TT, 0:QL], PR[:, t, 0:QL], ACT.Square, scale=float(QL) ** -0.5,
                                 accum_out=SS[:, 15 + t:16 + t]).then_inc(sq_q, 1)
            act.wait_ge(sq_q, 2 * t + 1)
            nc.scalar.activation(SCR[0:TT, 0:KL], PR[:, t, QL:QL + KL], ACT.Square, scale=1 / 16,
                                 accum_out=SS[:, 18 + t:19 + t]).then_inc(sq_q, 1)

        def latent_high(t):
            act.wait_ge(lat_t, 2 * t + 1)
            nc.scalar.copy(CQTH[:, :, t * TT:(t + 1) * TT], PS[:, 0, 0:3 * TT].rearrange("p (n t) -> p n t", n=3))\
              .then_inc(lat_h, 1)

        square(2, 0, x_dense, 1)
        square(2, 1, x_dense, 2)
        tile_high(2, 0)
        square(2, 2, x_dense, 3)
        tile_high(2, 1)
        projected(0)
        act.wait_ge(wuq_in, 16)

        def query_weights_high(k):
            nc.scalar.copy(WUQH[:, k, :], WUQ[:, k, :]).then_inc(wide_high, 1)

        query_weights_high(0)
        tile_high(2, 2)
        query_weights_high(1)
        projected(1)
        query_weights_high(2)
        latent_high(0)
        projected(2)
        latent_high(1)
        for t in range(NT):
            for i in range(2):
                act.wait_ge(q_mm, 3 * t + i + 1)
                nc.scalar.copy(Q[:, t, i * 512:(i + 1) * 512], PS[0:TT, q_bank(t, i), :]).then_inc(q_ev, 1)
            if t == 0:
                latent_high(2)
        for h in range(H):
            act.wait_ge(k_mm, h // 2 + 1)
            nc.scalar.copy(KT[0:NOPE, h, :], PS[h % 2 * NOPE:h % 2 * NOPE + NOPE, key_bank(h // 2), 0:TP]).then_inc(k_ev, 1)
        for h in range(H):
            for c in range(2):
                n = 2 * h + c
                if n % 4 == 3:
                    act.wait_ge(uk_t, n + 1)
                    src = PS[0:NOPE, 2 + n // 4 % 4, :].rearrange("p (i x) -> p i x", i=2)
                    nc.scalar.copy(UKT[:, h - 1:h + 1, :], src).then_inc(uk_ev, 4)
        for h in range(1, H, 2):
            act.wait_ge(qt_t, h + 1)
            nc.scalar.copy(QTR[:, h, :], PS[0:QH, h % 8, 0:T]).then_inc(qt_act, 1)

        def latent_out(b):
            act.wait_ge(d_olt, b + 1)
            nc.scalar.copy(OLT[:, :, :, b * NS:(b + 1) * NS],
                           PS[:, 2, 2 * P:4 * P].rearrange("p (c h s) -> p c h s", c=2, h=H)).then_inc(d_olc, 1)

        def cache_out(b, g):
            act.wait_ge(d_ct, 6 * b + g + 1)
            part, half = g // 2, g % 2
            lo, hi = (NOPE, QH) if part == 2 else (0, P)
            nc.scalar.copy(CT[b % 2][lo:hi, part, half * 512:half * 512 + 512],
                           PS[lo:hi, turn_bank("cache", b, g), :]).then_inc(d_cte_act, 1)

        for g in CTE_ACT:
            cache_out(0, g)
        for u in range(NAU + 2):
            if u < NAU:
                act.wait_ge(s_nm, u + 1)
                probs, st = PP[u % 4], RPS[u % 4]
                parts = ((0, P), (P, 3 * P)) if AU[u][0] == "head" else ((0, TP),)
                for i, (lo, hi) in enumerate(parts):
                    nc.scalar.activation(probs[:, lo:hi], probs[:, lo:hi], ACT.Exp, scale=SCALE, bias=st[:, 2 + i:3 + i],
                                         accum_out=st[:, 4 + i:5 + i]).then_inc(s_exp, 2 // len(parts))
            if u >= 2:
                w = u - 2
                act.wait_ge(s_pt, w + 1)
                if AU[w][0] == "head":
                    nc.scalar.copy(PPT[w % 2][:, :], PS[:, 3 + w % 2, 0:384]).then_inc(s_ptc, 2)
                else:
                    nc.scalar.copy(PPT[w % 2][:, 0:256], PS[:, 3 + w % 2, 0:256]).then_inc(s_ptc, 1)
                    nc.scalar.copy(PPT[w % 2][0:16, 256:384], PS[0:16, 3 + w % 2, 256:384]).then_inc(s_ptc, 1)
        for b in range(NB):
            if b + 1 < NB:
                cache_out(b + 1, 0)
                cache_out(b + 1, 1)
            act.wait_ge(d_nm, b + 1)
            nc.scalar.activation(PD[:, 0:PAST], PS[:, 0:2, :].rearrange("p b n -> p (b n)"), ACT.Exp, scale=SCALE,
                                 bias=DS[:, 3:4], accum_out=DS[:, 4:5]).then_inc(d_exp, 1)
            nc.scalar.activation(PD[:, PAST:PAST + NS], DM[:, :], ACT.Exp, scale=SCALE,
                                 bias=DS[:, 3:4], accum_out=DS[:, 5:6]).then_inc(d_exp, 1)
            act.wait_ge(d_pt, 3 * b + 1)
            nc.scalar.copy(PDT[:, 0:4, :].rearrange("p a q -> p (a q)"), PS[:, turn_bank("probs", b, 0), :]).then_inc(d_ptc_act, 1)
            if b + 1 < NB:
                cache_out(b + 1, 5)
            if b:
                latent_out(b - 1)
            if b >= NB - 2:
                square(3, MIXED[b - NB + 2], x_mixed, 2 * (b - NB + 2) + 2, b - NB + 2)
        latent_out(NB - 1)
        for g in range(2):
            act.wait_ge(do_mm, g + 1)
            nc.scalar.copy(OT[:, 4 * g:4 * g + 4, 0:SMP], PS[:, g, 0:4 * SMP].rearrange("p (k t) -> p k t", k=4)).then_inc(do_ev, 1)
        def high_tokens(i):
            act.wait_ge(normed[3], i + 1)
            nc.scalar.copy(HNH[:, MIXED[i], :], HN[:, MIXED[i], :]).then_inc(hn_high, 1)

        high_tokens(0)
        high_tokens(1)
        tile_out(0)
        square(3, MIXED[2], x_mixed, 6, 2)
        tile_out(1)
        tile_out(2)
        high_tokens(2)

        def split(m, n):
            split_high(UH[n % HIGH][:, :], RAW[n % RING][:, :], NU * (m + 1) + n, raw_in[n % RING],
                       32 * (NU // RING * m + n // RING + 1))

        split(0, 0)
        split(0, 1)
        act.wait_ge(r_dve, 1)
        nc.scalar.activation(RC[:, 6:8, :], RC[:, 4:6, :], ACT.Exp).then_inc(r_act, 1)

        def tokens_in(m):
            for half in range(2):
                act.wait_ge(i_g, 2 * m + half + 1)
                nc.scalar.copy(XN[:, half * 512:(half + 1) * 512], PS[:, 6 + half, :]).then_inc(i_n, 1)

        def tokens_high(m):
            for g in range(2):
                act.wait_ge(i_xt, 2 * m + g + 1)
                nc.scalar.copy(XH[:, 4 * g:4 * g + 4, :].rearrange("p k c -> p (k c)"), PS[:, turned_bank(g), :]).then_inc(i_xh, 1)

        def sums_out(used):
            act.wait_ge(unit_used, used)
            nc.scalar.copy(YH[:, :], PS[:, 4:6, :].rearrange("p b n -> p (b n)")).then_inc(i_yh, 1)

        tokens_in(0)
        tokens_high(0)
        split(0, 2)
        act.wait_ge(r_cnt_mm, 5)
        sums_out(NU)

        def item(j, last):
            split(j, 3)
            for c in range(NC):
                act.wait_ge(unit_used, NU * (j + 1) + UNITS.index((c, 1)) + 1)
                if c:
                    act.wait_ge(i_a, NC * j + c)
                nc.scalar.activation(EG[:, :], PS[:, c % 3, 0:CW], ACT.Silu).then_inc(i_sg, 1)
                if c >= 1:
                    act.wait_ge(i_t, NC * j + c)
                    nc.scalar.copy(ATH[(c - 1) % 2][:, :, :].rearrange("p k c -> p (k c)"), PS[:, 3, 0:CW]).then_inc(i_ath, 1)
                for n in splits_after(c):
                    split(j, n)
            if not last:
                tokens_in(j + 1)
            act.wait_ge(i_t, NC * j + NC)
            nc.scalar.copy(ATH[(NC - 1) % 2][:, :, :].rearrange("p k c -> p (k c)"), PS[:, 3, 0:CW]).then_inc(i_ath, 1)
            if not last:
                split(j + 1, 0)
                tokens_high(j + 1)
                split(j + 1, 1)
            sums_out(NU * (j + 2))
            if not last:
                split(j + 1, 2)

        act.wait_ge(items_known, 2)
        before_last = act.value_load(NI[0:1, 0:1], min_val=1, max_val=MAXI - 1)
        with act.Fori(0, before_last) as j:
            item(j, False)
        item(before_last, True)
        for t in range(NT):
            square(4, t, x_added, (before_last + 2) * (2 * NT) - 2 * NT + 2 * t + 2)

    @block.vector
    def _(dve):
        link = linker(dve, dve_step)
        V_ = nc.vector

        link(V_.memset(ZB[:, :], 0.0))

        def norm(n, gain, tiles=range(NT)):
            for t in tiles:
                i = 3 * n + t
                dve.wait_ge(inverse_root[n], t + 1)
                V_.scalar_tensor_tensor(out=HN[:, t, :], in0=X[:, t, :], scalar=RS[:, i:i + 1], in1=gain,
                                        op0=ALU.mult, op1=ALU.mult).then_inc(normed[n], 1)

        def tile_out(i):
            dve.wait_ge(turned[3], 2 * i + 2)
            V_.tensor_copy(HT3[:, i % 2, 4:8, :], PS[:, 1, 0:4 * TT].rearrange("p (d t) -> p d t", d=4))\
              .then_inc(turned_dve[3], 1)

        def split_low(dst, src, high, n):
            dve.wait_ge(unit_high, n + 1)
            V_.tensor_tensor(dst, src, high.bitcast(F32), ALU.subtract).then_inc(unit_low, 1)

        def tile_low(n, t):
            for g in range(2):
                dve.wait_ge(turned_act[n], 2 * t + g + 1)
                where = (slice(None), slice(4 * g, 4 * g + 4), slice(t * TT, (t + 1) * TT))
                V_.tensor_tensor(HTL[where], PS[:, g, 0:4 * TT].rearrange("p (d t) -> p d t", d=4),
                                 HTH[where].bitcast(F32), ALU.subtract).then_inc(turned_dve[n], 1)

        dve.wait_ge(gain0_in, 16)
        norm(0, G[0][:, :])
        for d in range(0, KD, 2):
            dve.wait_ge(pool_mm, d + 1)
            V_.tensor_copy(DT[:, d, :], PS[:, d, 0:T]).then_inc(pool_dve, 1)
            if d in (2, 4):
                dve.wait_ge(pool_w_in, 16 * 2)
                half = PW[:, :, :].rearrange("p (g c) n -> p c g n", c=2)[:, d // 2 - 1, :, :]
                V_.tensor_tensor(half, half, PSC[:, :].rearrange("p (g n) -> p g n", g=4), ALU.mult).then_inc(pool_dve, 1)

        def first_low(u):
            split_low(dense_low(0, u), dense_raw(0, u), dense_high(u), u)

        first_low(0)
        dve.wait_ge(gains_in, 16)
        for t in range(NT):
            for half in range(2):
                dve.wait_ge(pool_y, 2 * t + half + 1)
                cols = slice(half * 512, half * 512 + 512)
                ins = V_.tensor_tensor(X[:, t, cols], X[:, t, cols], PS[0:TT, 2 * t + half, :], ALU.add)
                if half == 0:
                    link(ins)
                if t == 0 and half == 0:
                    first_low(1)
            ins.then_inc(x_pooled, 1)
            dve.wait_ge(x_pooled, t + 1)
            if t == 0:
                dve.wait_ge(pool_out, 16 * 2)
            elif t == 1:
                norm(1, G[2][:, :], (0,))
        tile_low(1, 0)
        norm(1, G[2][:, :], (1, 2))
        tile_low(1, 1)
        tile_low(1, 2)
        first_low(2)

        def dense_step(c, q, last):
            nxt = (c + 1) % RING_D
            for j in range(2):
                tile = 2 * q + j
                dve.wait_ge(silu_done, tile + 1)
                dve.wait_ge(unit_used, 3 * q + j + 1)
                if j == 0:
                    dve.wait_ge(unit_low, 3 * q + 3)
                else:
                    dve.wait_ge(act_low, tile)
                V_.tensor_tensor(AF[:, :], SG[:, :], PS[:, 1, 0:T], ALU.mult).then_inc(act_made, 1)
                dve.wait_ge(act_high, tile + 1)
                V_.tensor_tensor(AL[:, j, :], AF[:, :], AH[:, j, :].bitcast(F32), ALU.subtract).then_inc(act_low, 1)
                if last and j == 0:
                    for k in range(KD):
                        dve.wait_ge(wide_high, k + 1)
                        V_.tensor_tensor(WINL[:, k, :], WIN[:, k, :], WINH[k][:, :].bitcast(F32), ALU.subtract)\
                          .then_inc(wide_low, 1)
                if not last:
                    split_low(dense_low(nxt, j), dense_raw(nxt, j), dense_high(j), 3 * (q + 1) + j)
            if not last:
                split_low(dense_low(nxt, 2), dense_raw(nxt, 2), dense_high(2), 3 * (q + 1) + 2)

        with dve.Fori(0, NC // RING_D) as r:
            for i in range(RING_D):
                dense_step(i, r * RING_D + i, False)
        for c in range(NC // RING_D * RING_D, NC):
            dense_step(c % RING_D, c, c == NC - 1)
        def dense_in(t):
            dve.wait_ge(dense_done, t + 1) if t < NT - 1 else dve.wait_ge(unit_used, NU)
            for half in range(2):
                cols = slice(half * 512, half * 512 + 512)
                ins = V_.tensor_tensor(X[:, t, cols], X[:, t, cols], PS[0:TT, 2 + 2 * t + half, :], ALU.add)
                if half == 0:
                    link(ins)
            ins.then_inc(x_dense, 1)

        dve.wait_ge(small_in, 16 * 5)
        cos = cn("cos", TT).rearrange("p (t f) -> p t f", t=NT)
        sin = cn("sin", TT).rearrange("p (t f) -> p t f", t=NT)

        def latent(t):
            dve.wait_ge(inverse_root_qk, t + 1)
            dve.wait_ge(proj_out, t + 1)
            V_.scalar_tensor_tensor(out=PR[:, t, 0:QL], in0=PR[:, t, 0:QL], scalar=RS[:, 15 + t:16 + t],
                                    in1=GQ[:, :], op0=ALU.mult, op1=ALU.mult)
            V_.scalar_tensor_tensor(out=KVN[:, t, 0:KL], in0=PR[:, t, QL:QL + KL], scalar=RS[:, 18 + t:19 + t],
                                    in1=GKV[:, :], op0=ALU.mult, op1=ALU.mult)
            x1, x2 = PR[:, t, QL + KL:QL + KL + HALF], PR[:, t, QL + KL + HALF:PROJ]
            V_.tensor_tensor(KR[:, 0, :], x1, cos[:, t, :], ALU.mult)
            V_.tensor_tensor(KR[:, 1, :], x2, sin[:, t, :], ALU.mult)
            V_.tensor_tensor(KR[:, 2, :], x2, cos[:, t, :], ALU.mult)
            link(V_.tensor_tensor(KR[:, 3, :], x1, sin[:, t, :], ALU.mult))
            link(V_.tensor_tensor(KVN[:, t, KL:KL + HALF], KR[:, 0, :], KR[:, 1, :], ALU.subtract))
            V_.tensor_tensor(KVN[:, t, KL + HALF:KV], KR[:, 2, :], KR[:, 3, :], ALU.add).then_inc(latent_ready, 1)
            dve.wait_ge(latent_ready, t + 1)

        def latent_out(t):
            cols = slice(t * TT, (t + 1) * TT)
            dve.wait_ge(lat_h, t + 1)
            V_.tensor_tensor(CQTL[:, :, cols], PS[:, 0, 0:3 * TT].rearrange("p (n t) -> p n t", n=3),
                             CQTH[:, :, cols].bitcast(F32), ALU.subtract).then_inc(lat_e, 1)
            dve.wait_ge(lat_t, 2 * t + 2)
            V_.tensor_copy(CKT[:, :, cols], PS[:, 1, 0:2 * TT].rearrange("p (n t) -> p n t", n=2)).then_inc(lat_e, 1)
            V_.tensor_copy(KPT[NOPE:QH, cols], PS[NOPE:QH, 1, 2 * TT:3 * TT]).then_inc(lat_e, 1)

        dve.wait_ge(gain1_in, 16)
        dense_in(0)
        dense_in(1)
        norm(2, G[0][:, :], (0,))
        dense_in(2)
        tile_low(2, 0)
        norm(2, G[0][:, :], (1,))
        norm(2, G[0][:, :], (2,))
        tile_low(2, 1)

        def query_weights_low(k):
            dve.wait_ge(wide_high, KD + k + 1)
            V_.tensor_tensor(WUQL[:, k, :], WUQ[:, k, :], WUQH[:, k, :].bitcast(F32), ALU.subtract).then_inc(wide_low, 1)

        latent(0)
        tile_low(2, 2)
        for k in range(3):
            query_weights_low(k)
        latent_out(0)
        latent(1)
        latent_out(1)
        latent(2)
        latent_out(2)
        for t in range(NT):
            dve.wait_ge(q_mm, 3 * t + 3)
            link(V_.tensor_copy(Q[:, t, 1024:1536], PS[0:TT, q_bank(t, 2), :]))
            dve.wait_ge(q_ev, 2 * (t + 1))
            pe_part = Q[:, t, :].rearrange("p (h x) -> p h x", h=H)
            x1, x2 = pe_part[:, :, NOPE:NOPE + HALF], pe_part[:, :, NOPE + HALF:QH]
            c3 = cos[:, t:t + 1, :].to_broadcast([TT, H, HALF])
            s3 = sin[:, t:t + 1, :].to_broadcast([TT, H, HALF])
            V_.tensor_tensor(QR[:, 0], x1, c3, ALU.mult)
            V_.tensor_tensor(QR[:, 1], x2, s3, ALU.mult)
            V_.tensor_tensor(QR[:, 2], x2, c3, ALU.mult)
            link(V_.tensor_tensor(QR[:, 3], x1, s3, ALU.mult))
            V_.tensor_tensor(x1, QR[:, 0], QR[:, 1], ALU.subtract)
            ins = V_.tensor_tensor(x2, QR[:, 2], QR[:, 3], ALU.add)
            ins.then_inc(q_rot, 1)
            dve.wait_ge(q_rot, t + 1)
        for h in range(0, H, 2):
            dve.wait_ge(qt_t, h + 1)
            V_.tensor_copy(QTR[:, h, :], PS[0:QH, h % 8, 0:T]).then_inc(qt_dve, 1)
        for i, (p0, rows) in enumerate(KB):
            for half in range(2):
                n = 2 * i + half
                dve.wait_ge(v_mm, n + 1)
                V_.tensor_copy(V[0:rows, i, half * 512:(half + 1) * 512], PS[0:rows, half, :]).then_inc(v_ev, 1)
        dve.wait_ge(qt_dve, H // 2)
        dve.wait_ge(qt_act, H // 2)
        V_.tensor_copy(QPT[NOPE:QH, :, :].rearrange("p b (h s) -> p h b s", h=H),
                       QTR[NOPE:QH, :, 0:SMP].rearrange("p h (b s) -> p h b s", b=NB)).then_inc(qp_copied, 1)
        for n in range(4):
            c, g = n // 2, n % 2
            dve.wait_ge(ql_mm, n + 1)
            V_.tensor_copy(QLT[:, c, :, :].rearrange("p b (h s) -> p h b s", h=H)[:, 8 * g:8 * g + 8],
                           PS[:, 2 + n, :].rearrange("p (h b s) -> p h b s", h=8, b=NB)).then_inc(ql_ev, 1)

        def cache_out(b, g):
            dve.wait_ge(d_ct, 6 * b + g + 1)
            part, half = g // 2, g % 2
            lo, hi = (NOPE, QH) if part == 2 else (0, P)
            V_.tensor_copy(CT[b % 2][lo:hi, part, half * 512:half * 512 + 512],
                           PS[lo:hi, turn_bank("cache", b, g), :]).then_inc(d_cte_dve, 1)

        for g in CTE_DVE:
            cache_out(0, g)
        for u in range(NAU + 4):
            if u < NAU:
                dve.wait_ge(s_mm, u + 1)
                probs, st = PP[u % 4], RPS[u % 4]
                parts = [(0, P, cn("mask")[:, P:2 * P]), (P, 3 * P, cn("mask"))] if AU[u][0] == "head" else \
                    [(0, TP, cn("maskt"))]
                for i, (lo, hi, mask) in enumerate(parts):
                    ins = V_.tensor_tensor_reduce(probs[:, lo:hi], PS[:, u % 3, lo:hi], mask, 1.0, LOW, ALU.add, ALU.max,
                                                  st[:, i:i + 1])
                    link(ins)
                V_.tensor_scalar(st[:, 2:2 + len(parts)], st[:, 0:len(parts)], -SCALE, None, ALU.mult).then_inc(s_nm, 1)
            if 1 <= u <= NAU:
                w = u - 1
                probs, st = PP[w % 4], RPS[w % 4]
                parts = ((0, P), (P, 3 * P)) if AU[w][0] == "head" else ((0, TP),)
                dve.wait_ge(s_exp, 2 * w + 2)
                link(V_.reciprocal(st[:, 6:6 + len(parts)], st[:, 4:4 + len(parts)]))
                for i, (lo, hi) in enumerate(parts):
                    V_.tensor_scalar(probs[:, lo:hi], probs[:, lo:hi], st[:, 6 + i:7 + i], None, ALU.mult)\
                      .then_inc(s_norm, 2 // len(parts))
            if u - 4 in PAIR_DONE:
                p = PAIR_DONE[u - 4]
                dve.wait_ge(s_o, u - 3)
                V_.tensor_copy(OT[:, p, SMP:T], PS[:, 5 + p % 3, 0:TP]).then_inc(s_oc, 1)
        def mix_in(i):
            t, half = MIXED[i // 2], i % 2
            cols = slice(half * 512, half * 512 + 512)
            dve.wait_ge(wo_mm, i + 1)
            V_.tensor_tensor(X[:, t, cols], X[:, t, cols], PS[0:TT, mix_bank(i), :], ALU.add).then_inc(x_mixed, 1)

        def latent_output(b):
            dve.wait_ge(d_o, b + 1)
            V_.tensor_scalar(OL[:, :], PS[:, 7, 0:KL], DS[:, 7:8], None, ALU.mult).then_inc(d_ol, 1)

        for b in range(NB):
            if b:
                latent_output(b - 1)
            dve.wait_ge(d_s, b + 1)
            link(V_.tensor_tensor_reduce(DM[:, :], PS[:, 2, 0:NS], cn("maskd"), 1.0, LOW, ALU.add, ALU.max, DS[:, 0:1]))
            link(V_.tensor_reduce(DS[:, 1:2], PS[:, 0:2, :].rearrange("p b n -> p (b n)"), AX.X, ALU.max))
            link(V_.tensor_tensor(DS[:, 2:3], DS[:, 0:1], DS[:, 1:2], ALU.max))
            V_.tensor_scalar(DS[:, 3:4], DS[:, 2:3], -SCALE, None, ALU.mult).then_inc(d_nm, 1)
            if b + 1 < NB:
                cache_out(b + 1, 2)
                cache_out(b + 1, 3)
            dve.wait_ge(d_exp, 2 * b + 2)
            link(V_.tensor_tensor(DS[:, 6:7], DS[:, 4:5], DS[:, 5:6], ALU.add))
            link(V_.reciprocal(DS[:, 7:8], DS[:, 6:7]))
            dve.wait_ge(d_pt, 3 * b + 2)
            V_.tensor_copy(PDT[:, 4:8, :].rearrange("p a q -> p (a q)"), PS[:, turn_bank("probs", b, 1), :]).then_inc(d_ptc_dve, 1)
            dve.wait_ge(d_pt, 3 * b + 3)
            V_.tensor_copy(PDT[0:NS, 8, :], PS[0:NS, 2, P:2 * P]).then_inc(d_ptc_dve, 1)
            if b + 1 < NB:
                cache_out(b + 1, 4)
            for i in range(4):
                if MIX_UNITS[8 * i + 7] == b:
                    mix_in(i)
        latent_output(NB - 1)
        def norm_mixed(i):
            t = MIXED[i]
            dve.wait_ge(inverse_root[3], i + 1)
            V_.scalar_tensor_tensor(out=HN[:, t, :], in0=X[:, t, :], scalar=RS[:, 9 + t:10 + t], in1=G[2][:, :],
                                    op0=ALU.mult, op1=ALU.mult).then_inc(normed[3], 1)

        def low_tokens(i):
            t = MIXED[i]
            dve.wait_ge(hn_high, i + 1)
            V_.tensor_tensor(HNL[:, t, :], HN[:, t, :], HNH[:, t, :].bitcast(F32), ALU.subtract).then_inc(hn_low, 1)

        dve.wait_ge(gain3_in, 16)
        dve.wait_ge(stored, 16 * (3 + 2 * NT))
        dve.wait_ge(d_olt, NB)
        norm_mixed(0)
        norm_mixed(1)
        dve.wait_ge(do_mm, 2)
        tile_out(0)
        low_tokens(0)
        mix_in(4)
        mix_in(5)
        tile_out(1)
        low_tokens(1)
        norm_mixed(2)
        tile_out(2)
        low_tokens(2)

        def split(m, n):
            split_low(LOWS[n % RING][:, :], RAW[n % RING][:, :], UH[n % HIGH][:, :], NU * (m + 1) + n)

        def rt(i):
            return RT[:, i, :, :]

        def rc(i):
            return RC[:, i, :]

        def wide(x):
            return x.unsqueeze(2).to_broadcast([TT, NT, NE])

        logits = PS[0:TT, 2, 0:NT * NE].rearrange("p (t e) -> p t e", t=NT)
        hots = RT[:, 2:4, :, :]
        ridx = cn("ridx", TT).unsqueeze(1).to_broadcast([TT, NT, NE])
        link(V_.memset(ONE[:, :], 1.0))
        link(V_.memset(ONEH[:, :], 1.0))
        link(V_.tensor_copy(UPH[:, :], cn("upper", TT)))
        dve.wait_ge(small_in, 16 * 5)
        dve.wait_ge(r_mm, 1)
        link(V_.tensor_tensor(rt(1), logits, BR[:, :].unsqueeze(1).to_broadcast([TT, NT, NE]), ALU.add))

        def one_hot_of_max(src, dst):
            link(V_.tensor_reduce(rc(0), src, AX.X, ALU.max))
            link(V_.tensor_tensor(rt(6), src, wide(rc(0)), ALU.is_equal))
            link(V_.tensor_tensor(rt(6), rt(6), ridx, ALU.mult))
            link(V_.tensor_reduce(rc(1), rt(6), AX.X, ALU.max))
            link(V_.tensor_tensor(dst, rt(6), wide(rc(1)), ALU.is_equal))

        one_hot_of_max(rt(1), rt(2))
        link(V_.scalar_tensor_tensor(out=rt(4), in0=rt(2), scalar=LOW, in1=rt(1), op0=ALU.mult, op1=ALU.add))
        one_hot_of_max(rt(4), rt(3))
        V_.tensor_tensor(BOTH[:, :, :], rt(2), rt(3), ALU.add).then_inc(diag_made, 1)

        def pick(src, dst):
            for i in range(2):
                ins = V_.tensor_tensor(RT[:, 6 + i, :, :], src, hots[:, i, :, :], ALU.mult)
            link(ins)
            link(V_.tensor_reduce(dst, RT[:, 6:8, :, :], AX.X, ALU.add))

        dve.wait_ge(r_cnt_mm, 1)
        link(V_.tensor_tensor(FL[:, :, :], PS[:, 3, 64:64 + NE].unsqueeze(2).to_broadcast([P, NE, NT]),
                              cn("steps").rearrange("p (e m) -> p e m", e=NE), ALU.is_gt))
        link(V_.tensor_reduce(TO[:, 0, :], FL[:, :, :], AX.X, ALU.add))
        link(V_.tensor_tensor(TR[:, :, :], TO[:, 0:1, :].to_broadcast([P, NE, NE]),
                              cn("tri").rearrange("p (e f) -> p e f", e=NE), ALU.mult))
        link(V_.tensor_reduce(TO[:, 1, :], TR[:, :, :], AX.X, ALU.add))
        link(V_.tensor_tensor(TO[:, 2, :], TO[:, 1, :], TO[:, 0, :], ALU.subtract))
        link(V_.scalar_tensor_tensor(out=rt(9), in0=TO[0:TT, 2:3, :].to_broadcast([TT, NT, NE]), scalar=float(CAP),
                                     in1=PS[0:TT, 3, 0:NT * NE].rearrange("p (t e) -> p t e", t=NT), op0=ALU.mult, op1=ALU.add))
        pick(rt(9), RC[:, 8:10, :])
        link(V_.tensor_copy(RC[:, 2:4, :], RC[:, 8:10, :]))

        def select(lk, m, t):
            if not (isinstance(m, int) and t == 0):
                dve.wait_ge(i_sel, NT * m + t)
            lk(V_.tensor_scalar(TS[:, :], cn("iota", TT), RC[:, 8, t:t + 1], None, ALU.is_equal))
            V_.scalar_tensor_tensor(out=SEL[:, t, :], in0=cn("iota", TT), scalar=RC[:, 9, t:t + 1], in1=TS[:, :],
                                    op0=ALU.is_equal, op1=ALU.add).then_inc(i_sel, 1)
            if t == NT - 1:
                dve.wait_ge(i_sel, NT * m + NT)
                lk(V_.tensor_scalar(RC[:, 8:10, :], RC[:, 8:10, :], -float(CAP), None, ALU.add))

        def way_back(lk, step):
            if step == 0:
                lk(V_.scalar_tensor_tensor(out=T1[:, :], in0=G1[:, :], scalar=PJ[:, :], in1=W1[:, :],
                                           op0=ALU.is_equal, op1=ALU.mult))
                lk(V_.scalar_tensor_tensor(out=T2[:, :], in0=G2[:, :], scalar=PJ[:, :], in1=W2[:, :],
                                           op0=ALU.is_equal, op1=ALU.mult))
            elif step == 1:
                lk(V_.tensor_scalar(PJ[:, :], PJ[:, :], float(CAP), None, ALU.add))
                lk(V_.tensor_tensor(T1[:, :], T1[:, :], T2[:, :], ALU.add))
            else:
                lk(V_.tensor_copy(SWH[:, :], T1[:, :]))
                V_.tensor_tensor(SWL[:, :], T1[:, :], SWH[:, :].bitcast(F32), ALU.subtract).then_inc(i_sw, 1)

        def tokens_low(m):
            for g in range(2):
                dve.wait_ge(i_xh, 2 * m + g + 1)
                V_.tensor_tensor(XL[:, 4 * g:4 * g + 4, :].rearrange("p k c -> p (k c)"), PS[:, turned_bank(g), :],
                                 XH[:, 4 * g:4 * g + 4, :].rearrange("p k c -> p (k c)").bitcast(F32),
                                 ALU.subtract).then_inc(i_xl, 1)

        def sums_low(m):
            dve.wait_ge(i_yh, m + 1)
            V_.tensor_tensor(YL[:, :], PS[:, 4:6, :].rearrange("p b n -> p (b n)"), YH[:, :].bitcast(F32),
                             ALU.subtract).then_inc(i_yl, 1)

        def add_outputs(m, t):
            for half in range(2):
                n = 2 * t + half
                cols = slice(half * 512, half * 512 + 512)
                dve.wait_ge(i_o, 6 * m + n + 1)
                V_.tensor_tensor(X[:, t, cols], X[:, t, cols], PS[0:TT, out_bank(n), :], ALU.add).then_inc(x_added, 1)

        def act_low_part(c, j):
            dve.wait_ge(i_ath, NC * j + c + 1)
            V_.tensor_tensor(ATL[c % 2][:, :, :].rearrange("p k c -> p (k c)"), PS[:, 3, 0:CW],
                             ATH[c % 2][:, :, :].rearrange("p k c -> p (k c)").bitcast(F32), ALU.subtract).then_inc(i_atl, 1)

        for t in range(NT):
            select(link, 0, t)
        V_.tensor_scalar(NI[:, :], TO[0:1, 1, NE - 1:NE], -1.0, None, ALU.add).then_inc(items_known, 1)
        link(V_.tensor_tensor(IE[:, :, :], CN[0:1, COL["items"][0]:COL["items"][1]].unsqueeze(2).to_broadcast([1, MAXI, NE]),
                              TO[0:1, 1:2, :].to_broadcast([1, MAXI, NE]), ALU.is_ge))
        link(V_.tensor_reduce(EF[:, :], IE[:, :, :], AX.X, ALU.add))
        V_.tensor_scalar(EI[:, :], EF[:, :], float(NE - 1), None, ALU.min).then_inc(items_known, 1)
        pick(logits, RC[:, 10:12, :])
        link(V_.tensor_tensor(rc(0), rc(10), rc(11), ALU.max))
        V_.tensor_tensor(RC[:, 4:6, :], RC[:, 10:12, :], RC[:, 0:1, :].to_broadcast([TT, 2, NT]), ALU.subtract).then_inc(r_dve, 1)
        split(0, 0)
        dve.wait_ge(r_act, 1)
        link(V_.tensor_tensor(rc(10), rc(6), rc(7), ALU.add))
        link(V_.reciprocal(rc(11), rc(10)))
        link(V_.tensor_tensor(RC[:, 6:8, :], RC[:, 6:8, :], RC[:, 11:12, :].to_broadcast([TT, 2, NT]), ALU.mult))
        for i, c in enumerate((2, 3, 6, 7)):
            V_.tensor_tensor(DG[i][:, :, :], ident[0:TT, 0:TT].unsqueeze(1).to_broadcast([TT, NT, TT]),
                             RC[:, c, :].unsqueeze(2).to_broadcast([TT, NT, TT]), ALU.mult).then_inc(diag_made, 1)

        def spread_out(i):
            dve.wait_ge(r_cnt_mm, 2 + i)
            link(V_.tensor_copy((G1, G2, W1, W2)[i][:, :], PS[:, spread_bank(i), 0:T]))

        tokens_low(0)
        split(0, 1)
        spread_out(0)
        spread_out(1)
        split(0, 2)
        spread_out(2)
        spread_out(3)
        split(0, 3)
        link(V_.tensor_copy(PJ[:, :], cn("part")))
        V_.tensor_scalar(SWH[:, :], W1[:, :], 0.0, None, ALU.mult)
        V_.tensor_scalar(SWL[:, :], W1[:, :], 0.0, None, ALU.mult).then_inc(i_sw, 1)
        sums_low(0)

        def item(j, last):
            ilink = linker(dve, item_step, j * (NT + 6))
            for c in range(NC):
                dve.wait_ge(i_sg, NC * j + c + 1)
                if c:
                    dve.wait_ge(i_t, NC * j + c)
                V_.tensor_tensor(EA[:, :], EG[:, :], PS[:, c % 3, CW:2 * CW], ALU.mult).then_inc(i_a, 1)
                if c >= 1:
                    act_low_part(c - 1, j)
                units = list(splits_after(c))
                split(j, units[0])
                if 1 <= c <= 3:
                    add_outputs(j, c - 1)
                if 4 <= c <= 6:
                    if c == 4:
                        dve.wait_ge(x_added, 6 * j + 6)
                    way_back(ilink, c - 4)
                if 7 <= c <= 9 and not last:
                    if c == 7:
                        dve.wait_ge(i_g, 2 * j + 2)
                    select(ilink, j + 1, c - 7)
                for n in units[1:]:
                    split(j, n)
            act_low_part(NC - 1, j)
            if not last:
                split(j + 1, 0)
                tokens_low(j + 1)
                split(j + 1, 1)
            sums_low(j + 1)
            if not last:
                split(j + 1, 2)
                split(j + 1, 3)
                assert ilink.n[0] == NT + 6

        dve.wait_ge(items_known, 2)
        before_last = dve.value_load(NI[0:1, 0:1], min_val=1, max_val=MAXI - 1)
        with dve.Fori(0, before_last) as j:
            item(j, False)
        item(before_last, True)
        dve.wait_ge(gain4_in, 16)
        add_outputs(before_last + 1, 0)
        add_outputs(before_last + 1, 1)
        norm(4, G[2][:, :], (0,))
        add_outputs(before_last + 1, 2)
        norm(4, G[2][:, :], (1, 2))

    @block.tensor
    def _(pe):
        mm = nc.tensor.matmul

        def turn_tile(n, t, before=None):
            before = t if before is None else before
            pe.wait_ge(normed[n], before + 1)
            if before:
                pe.wait_ge(turned_act[n], before * (2 if n < 3 else 1))
                pe.wait_ge(turned_dve[n], before * (2 if n < 3 else 1))
            for d in range(KD):
                ins = nc.tensor.transpose(PS[:, d // 4, d % 4 * TT:(d % 4 + 1) * TT], HN[:, t, d * P:(d + 1) * P],
                                          ident[0:TT, 0:TT])
                if d % 4 == 3:
                    ins.then_inc(turned[n], 1)

        def three(out, wh, wl, xh, xl, start, stop):
            mm(out, wh, xh, start=start, stop=False, skip_group_check=True)
            mm(out, wh, xl, start=False, stop=False, skip_group_check=True)
            return mm(out, wl, xh, start=False, stop=stop, skip_group_check=True)

        pe.wait_ge(pool_in, 32)
        pe.wait_ge(normed[0], NT)
        pm = [cn("pm0", TT).rearrange("p (g t) -> p g t", g=4), cn("pm1", TT).rearrange("p (g t) -> p g t", g=4)]
        state = cn("pstate", NB * BUF).rearrange("p (g t) -> p g t", g=4)
        for d in range(KD):
            g, cols = d // 2, slice(d * P, (d + 1) * P)
            mm(PS[:, d, 0:T], ZB[0:1, 0:P], ZB[0:1, 0:T], start=True, stop=False, skip_group_check=True)
            for t in range(NT):
                wide = P if t < NT - 1 else TT
                mm(PS[:, d, t * TT:t * TT + wide], HN[:, t, cols], pm[min(t, 1)][:, g, 0:wide], start=False, stop=False,
                   skip_group_check=True)
            mm(PS[:, d, 0:SMP], ST[:, cols], state[:, g, :], start=False, stop=True,
               skip_group_check=True).then_inc(pool_mm, 1)
        pe.wait_ge(pool_act, KD // 2)
        pe.wait_ge(pool_dve, KD // 2 + 2)
        for t in range(NT):
            for half in range(2):
                for gg in range(2):
                    g = 2 * half + gg
                    for c in range(2):
                        ins = mm(PS[0:TT, 2 * t + half, gg * 256:(gg + 1) * 256], DT[:, 2 * g + c, t * TT:(t + 1) * TT],
                                 PW[:, 2 * g + c, :], start=(c == 0), stop=(c == 1))
                ins.then_inc(pool_y, 1)

        pe.wait_ge(consts_in, 16)
        turn_tile(1, 0)
        pe.wait_ge(x_pooled, NT)
        for t in (1, 2):
            for i in range(3):
                mm(PS[0:TT, 3 * t - 1 + i, :], ZB[0:1, 0:TT], ZB[0:1, 0:512], start=True, stop=False, skip_group_check=True)
            turn_tile(1, t)
        pe.wait_ge(turned_dve[1], 2 * NT)

        def dense_step(c, q, last=False):
            for j in range(2):
                wh, wl = dense_high(j), dense_low(c, j)
                pe.wait_ge(unit_low, 3 * q + j + 1)
                for g in range(2):
                    if j:
                        pe.wait_ge(silu_done if g == 0 else act_made, 2 * q + 1)
                    for k in range(KD):
                        ins = three(PS[:, g, 0:T], wh[:, k, g, :], wl[:, k, g, :], HTH[:, k, :], HTL[:, k, :],
                                    k == 0, k == KD - 1)
                    ins.then_inc(gate_mm if g == 0 else unit_used, 1)
            wh, wl = dense_high(2), dense_low(c, 2)
            pe.wait_ge(unit_low, 3 * q + 3)
            if last:
                pe.wait_ge(act_low, 2 * q + 2)
            for t, j in [(t, j) for t in range(NT) for j in range(2)] if last else [(t, j) for j in range(2) for t in range(NT)]:
                if not last and t == 0:
                    pe.wait_ge(act_low, 2 * q + j + 1)
                for n in range(2):
                    cols = slice(j * D + n * 512, j * D + n * 512 + 512)
                    ins = three(PS[0:TT, 2 + 2 * t + n, :], AH[:, j, t * TT:(t + 1) * TT],
                                AL[:, j, t * TT:(t + 1) * TT], wh[:, cols], wl[:, cols], False, False)
                if last and j == 1 and t < NT - 1:
                    ins.then_inc(dense_done, 1)
            ins.then_inc(unit_used, 1)

        with pe.Fori(0, NC // RING_D) as r:
            for i in range(RING_D):
                dense_step(i, r * RING_D + i)
        for c in range(NC // RING_D * RING_D, NC):
            dense_step(c % RING_D, c, c == NC - 1)

        def project_in(t, block):
            if block == 0:
                pe.wait_ge(turned_dve[2], 2 * t + 2)
            cols = slice(t * TT, (t + 1) * TT)
            lo, hi = ((0, 512), (512, PROJ))[block]
            for k in range(KD):
                ins = three(PS[0:TT, 2 + 2 * t + block, 0:hi - lo], HTH[:, k, cols], HTL[:, k, cols],
                            WINH[k][:, lo:hi], WINL[:, k, lo:hi], k == 0, k == KD - 1)
            ins.then_inc(proj_mm, 1)

        def turn_latent(t):
            pe.wait_ge(latent_ready, t + 1)
            if t:
                pe.wait_ge(lat_e, 3 * t)
            for n in range(6):
                rows = QH if n == 5 else P
                src = PR[:, t, n * P:(n + 1) * P] if n < 3 else KVN[:, t, (n - 3) * P:(n - 2) * P] if n < 5 \
                    else KVN[:, t, KV - QH:KV]
                ins = nc.tensor.transpose(PS[0:rows, n // 3, n % 3 * TT:(n % 3 + 1) * TT], src, ident[0:TT, 0:TT])
                if n % 3 == 2:
                    ins.then_inc(lat_t, 1)

        def queries(t, i):
            if i == 0:
                pe.wait_ge(lat_e, 3 * t + 3)
            if t == 2 and i == 0:
                pe.wait_ge(q_rot, 1)
            cols, out = slice(t * TT, (t + 1) * TT), slice(i * 512, (i + 1) * 512)
            for k in range(3):
                ins = three(PS[0:TT, q_bank(t, i), :], CQTH[:, k, cols], CQTL[:, k, cols], WUQH[:, k, out],
                            WUQL[:, k, out], k == 0, k == 2)
            ins.then_inc(q_mm, 1)

        turn_tile(2, 0)
        pe.wait_ge(wide_low, KD)
        project_in(0, 0)
        turn_tile(2, 1)
        project_in(0, 1)
        project_in(1, 0)
        turn_tile(2, 2)
        project_in(1, 1)
        project_in(2, 0)
        turn_latent(0)
        project_in(2, 1)
        pe.wait_ge(wide_low, KD + 3)
        queries(0, 0)
        turn_latent(1)
        queries(0, 1)
        queries(0, 2)
        queries(1, 0)
        turn_latent(2)
        queries(1, 1)
        queries(1, 2)
        for i in range(3):
            queries(2, i)
        pe.wait_ge(wuk_in, 16)
        for p in range(H // 2):
            if p >= 4:
                pe.wait_ge(k_ev, 2 * (p - 3))
            elif p == 2:
                pe.wait_ge(q_rot, 2)
            for c in range(2):
                ins = mm(PS[:, key_bank(p), 0:TP], WUK[:, c, 2 * p * NOPE:(2 * p + 2) * NOPE], CKT[:, c, SMP:T],
                         start=(c == 0), stop=(c == 1))
            ins.then_inc(k_mm, 1)
        pe.wait_ge(q_rot, NT)
        pe.wait_ge(k_ev, H)
        for n in range(2 * H):
            h, c = n // 2, n % 2
            if n % 4 == 0 and n >= 16:
                pe.wait_ge(uk_ev, n - 12)
            nc.tensor.transpose(PS[0:NOPE, 2 + n // 4 % 4, (n % 4) * P:(n % 4 + 1) * P],
                                WUK[:, c, h * NOPE:(h + 1) * NOPE], ident).then_inc(uk_t, 1)
        pe.wait_ge(uk_ev, 2 * H)
        for h in range(H):
            if h >= 8:
                pe.wait_ge(qt_dve if h % 2 == 0 else qt_act, (h - 8) // 2 + 1)
            for t in range(NT):
                ins = nc.tensor.transpose(PS[0:QH, h % 8, t * TT:(t + 1) * TT], Q[:, t, h * QH:(h + 1) * QH],
                                          ident[0:TT, 0:TT])
            ins.then_inc(qt_t, 1)
        pe.wait_ge(wuv_in, 16)
        for i, (p0, rows) in enumerate(KB):
            for half in range(2):
                n = 2 * i + half
                if n >= 2:
                    pe.wait_ge(v_ev, n - 1)
                else:
                    pe.wait_ge(qt_act if n else qt_dve, 5)
                for c in range(2):
                    ins = mm(PS[0:rows, half, :], CKT[:, c, SMP + p0:SMP + p0 + rows],
                             WUV[:, c, half * 512:(half + 1) * 512], start=(c == 0), stop=(c == 1))
                ins.then_inc(v_mm, 1)
        pe.wait_ge(qt_dve, H // 2)
        pe.wait_ge(qt_act, H // 2)
        for n in range(4):
            c, g = n // 2, n % 2
            for hh in range(8):
                h = 8 * g + hh
                ins = mm(PS[:, 2 + n, hh * SMP:(hh + 1) * SMP], UKT[:, h, c * P:(c + 1) * P], QTR[0:NOPE, h, 0:SMP],
                         start=True, stop=True)
            ins.then_inc(ql_mm, 1)

        def wait_for_bank(*turn):
            before = TURNS.index(turn) - 3
            if before < 0:
                return
            kind, b, g = TURNS[before]
            if kind == "probs":
                pe.wait_ge(d_ptc_act if g == 0 else d_ptc_dve, b + 1 if g == 0 else 2 * b + 1)
            elif g in CTE_ACT:
                pe.wait_ge(d_cte_act, 3 * b + CTE_ACT.index(g) + 1)
            else:
                pe.wait_ge(d_cte_dve, 3 * b + CTE_DVE.index(g) + 1)

        def turn_cache(b, g):
            part, half = g // 2, g % 2
            if g == 0:
                pe.wait_ge(cache_in[b % 3], 16 * 2 * NPG * (b // 3 + 1))
            wait_for_bank("cache", b, g)
            c0 = (0, P, KV - QH)[part]
            rows = QH if part == 2 else P
            for i in range(4):
                ins = nc.tensor.transpose(PS[0:rows, turn_bank("cache", b, g), i * P:(i + 1) * P],
                                          CC[b % 3][:, 4 * half + i, c0:c0 + rows], ident)
            ins.then_inc(d_ct, 1)

        pe.wait_ge(ql_ev, 4)
        pe.wait_ge(v_ev, 6)
        pe.wait_ge(kpe_copied, H)
        for g in range(6):
            turn_cache(0, g)
        pe.wait_ge(d_cte_dve, 3)
        pe.wait_ge(d_cte_act, 3)

        def prompt_scores(u):
            kind, n = AU[u]
            if kind == "head":
                mm(PS[:, u % 3, 0:P], QTR[:, n, SMP:SMP + P], KT[:, n, 0:P], start=True, stop=True)
                ins = mm(PS[:, u % 3, P:3 * P], QTR[:, n, SMP + P:SMP + 2 * P], KT[:, n, 0:2 * P], start=True, stop=True)
            else:
                for i in range(GROUP):
                    h = GROUP * n + i
                    ins = mm(PS[i * TAIL:(i + 1) * TAIL, u % 3, 0:TP], QTR[:, h, SMP + T0:T], KT[:, h, :],
                             start=True, stop=True, tile_position=(0, i * TAIL))
            ins.then_inc(s_mm, 1)

        def prompt_turn(u):
            pe.wait_ge(s_norm, 2 * u + 2)
            for kb in range(3):
                kr = P if AU[u][0] == "head" else KB[kb][1]
                ins = nc.tensor.transpose(PS[0:kr, 3 + u % 2, kb * P:(kb + 1) * P], PP[u % 4][:, kb * P:kb * P + kr], ident)
            ins.then_inc(s_pt, 1)

        def prompt_values(u):
            kind, n = AU[u]
            pe.wait_ge(s_ptc, 2 * u + 2)
            if kind == "head":
                out = PS[n % 2 * VH:n % 2 * VH + VH, 5 + n // 2 % 3, :]
                vh = slice(n * VH, (n + 1) * VH)
                mm(out[:, 0:P], V[:, 0, vh], PPT[u % 2][:, 0:P], start=True, stop=True, skip_group_check=True)
                for kb in range(2):
                    ins = mm(out[:, P:2 * P], V[:, kb, vh], PPT[u % 2][:, (kb + 1) * P:(kb + 2) * P],
                             start=(kb == 0), stop=(kb == 1), skip_group_check=True)
            else:
                for i in range(GROUP):
                    h = GROUP * n + i
                    pair = h // 2
                    if pair >= 3 and h % 2 == 0:
                        pe.wait_ge(s_oc, pair - 2)
                    for kb, (_, kr) in enumerate(KB):
                        new = slice(kb * P + i * TAIL + 16, kb * P + (i + 1) * TAIL)
                        ins = mm(PS[h % 2 * VH:h % 2 * VH + VH, 5 + pair % 3, 2 * P:TP], V[0:kr, kb, h * VH:(h + 1) * VH],
                                 PPT[u % 2][0:kr, new], start=(kb == 0), stop=(kb == 2), skip_group_check=True)
            ins.then_inc(s_o, 1)

        for u in range(NAU + 3):
            if u < NAU:
                prompt_scores(u)
            if 2 <= u < NAU + 2:
                prompt_turn(u - 2)
            if u >= 3:
                prompt_values(u - 3)

        def project_out(i, k):
            t, half = MIXED[i // 2], i % 2
            if k == 0 and 1 <= i < 4:
                pe.wait_ge(x_mixed, i)
            ins = mm(PS[0:TT, mix_bank(i), :], OT[:, k, t * TT:(t + 1) * TT], WO[:, k, half * 512:(half + 1) * 512],
                     start=(k == 0), stop=(k == KD - 1))
            if k == KD - 1:
                ins.then_inc(wo_mm, 1)

        mixed = [0]

        def fill(b, count):
            for _ in range(count):
                assert MIX_UNITS[mixed[0]] == b
                project_out(mixed[0] // KD, mixed[0] % KD)
                mixed[0] += 1

        pe.wait_ge(knew_in, 16 * NB)

        def latent_turn(b):
            pe.wait_ge(d_ol, b + 1)
            for c in range(2):
                ins = nc.tensor.transpose(PS[:, 2, (2 + c) * P:(3 + c) * P], OL[:, c * P:(c + 1) * P], ident)
            ins.then_inc(d_olt, 1)

        for b in range(NB):
            pe.wait_ge(d_cte_act, 3 * b + 3)
            pe.wait_ge(d_cte_dve, 3 * b + 3)
            for n in range(3):
                width = 512 if n < 2 else NS
                if n == 2 and b >= 2:
                    pe.wait_ge(d_olc, b - 1)
                for c in range(2):
                    keys = CT[b % 2][:, c, n * 512:(n + 1) * 512] if n < 2 else CKT[:, c, b * NS:(b + 1) * NS]
                    mm(PS[:, n, 0:width], QLT[:, c, b, :], keys, start=(c == 0), stop=False)
                keys = CT[b % 2][NOPE:QH, 2, n * 512:(n + 1) * 512] if n < 2 else KPT[NOPE:QH, b * NS:(b + 1) * NS]
                ins = mm(PS[:, n, 0:width], QPT[NOPE:QH, b, :], keys, start=False, stop=True)
            ins.then_inc(d_s, 1)
            if b == 0:
                pe.wait_ge(s_oc, H // 2)
            if b == 1:
                pe.wait_ge(wo_in, 16)
            if b + 1 < NB:
                turn_cache(b + 1, 0)
                turn_cache(b + 1, 1)
                if b:
                    fill(b, 2)
                turn_cache(b + 1, 2)
                turn_cache(b + 1, 3)
                if b:
                    fill(b, 2)
            else:
                fill(b, 5)
            pe.wait_ge(d_exp, 2 * b + 2)
            for n in range(2):
                wait_for_bank("probs", b, n)
                for i in range(4):
                    ins = nc.tensor.transpose(PS[:, turn_bank("probs", b, n), i * P:(i + 1) * P], PD[:, (4 * n + i) * P:(4 * n + i + 1) * P],
                                              ident)
                ins.then_inc(d_pt, 1)
            nc.tensor.transpose(PS[0:NS, 2, P:2 * P], PD[:, PAST:PAST + NS], ident).then_inc(d_pt, 1)
            if b + 1 < NB:
                for g in range(4, 6):
                    turn_cache(b + 1, g)
            else:
                fill(b, 3)
            pe.wait_ge(d_ptc_act, b + 1)
            pe.wait_ge(d_ptc_dve, 2 * b + 2)
            if b:
                latent_turn(b - 1)
            for i in range(NPG):
                mm(PS[:, 7, 0:KL], PDT[:, i, :], CC[b % 3][:, i, 0:KL], start=(i == 0), stop=False)
            mm(PS[:, 7, 0:KL], PDT[0:NS, NPG, :], KNEW[:, b, :], start=False, stop=True).then_inc(d_o, 1)
        pe.wait_ge(d_olc, NB - 1)
        latent_turn(NB - 1)
        pe.wait_ge(d_olc, NB)
        for h in range(H):
            lo = h % 2 * VH
            for c in range(2):
                ins = mm(PS[lo:lo + VH, h // 8, (h // 2 % 4) * SMP:(h // 2 % 4 + 1) * SMP],
                         WUV[:, c, h * VH:(h + 1) * VH], OLT[:, c, h, :], start=(c == 0), stop=(c == 1),
                         skip_group_check=True)
            if h % 8 == 7:
                ins.then_inc(do_mm, 1)
        pe.wait_ge(do_ev, 2)
        pe.wait_ge(wo_in, 16)

        def route_tile(i):
            t = MIXED[i]
            turn_tile(3, t, i)
            pe.wait_ge(turned_act[3], i + 1)
            pe.wait_ge(turned_dve[3], i + 1)
            for k in range(KD):
                ins = mm(PS[0:TT, 2, t * NE:(t + 1) * NE], HT3[:, i % 2, k, :], WR[:, k, :],
                         start=(k == 0), stop=(k == KD - 1), skip_group_check=True)
            if i == NT - 1:
                ins.then_inc(r_mm, 1)

        pe.wait_ge(small_in, 16 * 5)
        for k in range(KD):
            project_out(4, k)
        route_tile(0)
        for k in range(KD):
            project_out(5, k)
        route_tile(1)
        route_tile(2)
        pe.wait_ge(diag_made, 1)
        for t in range(NT):
            for s in range(t + 1):
                mm(PS[0:TT, 3, t * NE:(t + 1) * NE], ONEH[:, 0:TT] if s < t else UPH[:, :], BOTH[:, s, :],
                   start=(s == 0), stop=(s == t))
        for s in range(NT):
            ins = mm(PS[:, 3, 64:64 + NE], ONEH[:, :], BOTH[:, s, :], start=(s == 0), stop=(s == NT - 1))
        ins.then_inc(r_cnt_mm, 1)

        def gather(m):
            pe.wait_ge(i_sel, NT * m + NT)
            for half in range(2):
                for t in range(NT):
                    for src in (HNH, HNL):
                        ins = mm(PS[:, 6 + half, :], SEL[:, t, :], src[:, t, half * 512:(half + 1) * 512],
                                 start=(t == 0 and src is HNH), stop=(t == NT - 1 and src is HNL))
                ins.then_inc(i_g, 1)

        def turn_tokens(m):
            for g in range(2):
                pe.wait_ge(i_n, 2 * m + g + 1)
                for d in range(4):
                    ins = nc.tensor.transpose(PS[:, turned_bank(g), d * CAP:(d + 1) * CAP],
                                              XN[:, (4 * g + d) * P:(4 * g + d + 1) * P], ident)
                ins.then_inc(i_xt, 1)

        def send_back(m, t):
            if t == 0:
                pe.wait_ge(i_yl, m + 1)
                pe.wait_ge(i_sw, m + 1)
            for half in range(2):
                n = 2 * t + half
                if n >= 2:
                    pe.wait_ge(x_added, 6 * m + n - 1)
                cols = slice(half * 512, half * 512 + 512)
                three(PS[0:TT, out_bank(n), :], SWH[:, t * TT:(t + 1) * TT], SWL[:, t * TT:(t + 1) * TT],
                      YH[:, cols], YL[:, cols], True, True).then_inc(i_o, 1)

        def spread(i):
            pe.wait_ge(diag_made, 2 + i)
            for t in range(NT):
                ins = mm(PS[:, spread_bank(i), t * TT:(t + 1) * TT], ONE[:, :], DG[i][:, t, :], start=True, stop=True)
            ins.then_inc(r_cnt_mm, 1)

        for n in range(2):
            mm(PS[:, 4 + n, :], ZB[0:1, 0:P], ZB[0:1, 0:512], start=True, stop=True, skip_group_check=True)
        pe.wait_ge(hn_low, NT)
        gather(0)
        turn_tokens(0)
        for i in range(4):
            spread(i)
        pe.wait_ge(items_known, 2)
        before_last = pe.value_load(NI[0:1, 0:1], min_val=1, max_val=MAXI - 1)

        def item(j, last):
            def gate_up(c):
                for u in range(2):
                    n = UNITS.index((c, u))
                    pe.wait_ge(unit_low, NU * (j + 1) + n + 1)
                    for k in range(KD // 2):
                        kk = u * KD // 2 + k
                        cols = slice(k * 2 * CW, (k + 1) * 2 * CW)
                        ins = three(PS[:, c % 3, :], XH[:, kk, :], XL[:, kk, :], UH[n % HIGH][:, cols],
                                    LOWS[n % RING][:, cols], kk == 0, kk == KD - 1)
                    ins.then_inc(unit_used, 1)

            def turn_act(c):
                pe.wait_ge(i_a, NC * j + c + 1)
                if c:
                    pe.wait_ge(i_atl, NC * j + c)
                for i in range(CW // P):
                    ins = nc.tensor.transpose(PS[:, 3, i * P:(i + 1) * P], EA[:, i * P:(i + 1) * P], ident)
                ins.then_inc(i_t, 1)

            def down(c):
                n = UNITS.index((c, 2))
                pe.wait_ge(i_atl, NC * j + c + 1)
                pe.wait_ge(unit_low, NU * (j + 1) + n + 1)
                for i in range(CW // P):
                    for h in range(2):
                        cols = slice(i * D + h * 512, i * D + h * 512 + 512)
                        ins = three(PS[:, 4 + h, :], ATH[c % 2][:, i, :], ATL[c % 2][:, i, :], UH[n % HIGH][:, cols],
                                    LOWS[n % RING][:, cols], c == 0 and i == 0, c == NC - 1 and i == CW // P - 1)
                ins.then_inc(unit_used, 1)

            pe.wait_ge(i_xl, 2 * j + 2)
            for c in range(NC):
                gate_up(c)
                if c >= 1:
                    turn_act(c - 1)
                if 1 <= c <= NT:
                    send_back(j, c - 1)
                if c >= 2:
                    down(c - 2)
            if last:
                down(NC - 2)
                turn_act(NC - 1)
            else:
                pe.wait_ge(x_added, 6 * j + 6)
                gather(j + 1)
                turn_act(NC - 1)
                down(NC - 2)
                turn_tokens(j + 1)
            down(NC - 1)

        with pe.Fori(0, before_last) as j:
            item(j, False)
        item(before_last, True)
        for t in range(NT):
            send_back(before_last + 1, t)

    ctx.close()


def key_bank(p):
    return (0, 1, 5, 6)[p % 4]


def q_bank(t, i):
    return (2, 5, 2)[t] + i


CTE_ACT, CTE_DVE = (0, 1, 5), (2, 3, 4)
TURNS = [("cache", 0, g) for g in range(6)]
for _b in range(NB):
    TURNS += [("cache", _b + 1, g) for g in range(4) if _b + 1 < NB] + [("probs", _b, 0), ("probs", _b, 1)]
    TURNS += [("cache", _b + 1, g) for g in (4, 5) if _b + 1 < NB]


def turn_bank(*turn):
    return 3 + TURNS.index(turn) % 3


MIX_UNITS = [b for b in range(1, NB - 1) for _ in range(4)] + [NB - 1] * 8


def mix_bank(i):
    return 6 if i < 4 else i - 1


MIXED = (1, 2, 0)


def splits_after(c):
    def last(c):
        return min(UNITS.index((c, 1)) + 2, NU - 1)
    return range(last(c) + 1, (last(c + 1) if c < NC - 1 else NU - 1) + 1)


def spread_bank(i):
    return (1, 3, 6, 7)[i]


def turned_bank(g):
    return (2, 0)[g]


def out_bank(n):
    return 6 + n % 2


_INS = ["x_prompt", "x_sample", "cache_ckv", "cache_kpe", "state_pool", "page_table", "meta_tokens",
        "g_mix", "g_ffn", "g_final", "pool_w", "pool_scale",
        "mla_w_in", "mla_g_q", "mla_g_kv", "mla_w_uq", "mla_w_uk", "mla_w_uv", "mla_w_o",
        "ffn_w_gate", "ffn_w_up", "ffn_w_down",
        "moe_w_router", "moe_b_router", "moe_w_gate", "moe_w_up", "moe_w_down"]
_OUTS = [("y_prompt", (1, SEQ, D)), ("y_sample", (NB, NS, D)),
         ("ckv_prompt", (1, 1, TP, KL)), ("kpe_prompt", (1, 1, TP, ROPE)), ("pool_prompt", (1, 1, BUF, D)),
         ("ckv_sample", (1, NB, NS, KL)), ("kpe_sample", (1, NB, NS, ROPE)), ("pool_sample", (1, NB, BUF, D))]


def kernel(**inputs):
    import concourse.bacc as bacc
    from concourse.bass_utils import run_bass_kernel_spmd as run

    nc = bacc.Bacc("TRN2", target_bir_lowering=False, num_devices=1)
    arrays, a, o = {}, {}, {}
    table, pooling = shape_constants()
    for name in _INS + ["consts", "consts_pool"]:
        x = table if name == "consts" else pooling if name == "consts_pool" else np.ascontiguousarray(inputs[name])
        arrays[f"in_{name}"] = x
        a[name] = nc.dram_tensor(f"in_{name}", x.shape, mybir.dt.from_np(x.dtype), kind="ExternalInput").ap()
    for name, shape in _OUTS:
        o[name] = nc.dram_tensor(f"out_{name}", shape, F32, kind="ExternalOutput").ap()
    program(nc, a, o)
    r = run(nc, [arrays], core_ids=[0])
    return tuple(r.results[0][f"out_{name}"] for name, _ in _OUTS)
```
